# Optimizing a Trainium2 kernel written in Bass

```python
import jax, jax.numpy as jnp
from jax import lax
import numpy as np

D_MODEL = 1024
BATCH = 1
SEQ = 512
DEPTH = 1

HEAD_DIM = 64
FOX_HEADS = 8
FOX_W = FOX_HEADS * HEAD_DIM
CONV_WIDTH = 512
CONV_K = 3
NSA_HEADS = 8
NSA_KV_GROUPS = 2
NSA_W = NSA_HEADS * HEAD_DIM
NSA_KV_W = NSA_KV_GROUPS * HEAD_DIM
CMP_LEN = 32
CMP_STRIDE = 16
SEL_LEN = 64
SEL_TOP = 16
WIN = 512
Q_BLOCK = 128
D_FF = 2816
FFN_CONV_K = 3
N_BRANCH = 3
EPS = 1e-6
NEG_INF = -1e30
FORCE_BONUS = 1e4

IN_SIZES = (D_MODEL, D_MODEL, D_MODEL,
            FOX_W, FOX_W, FOX_W, FOX_HEADS,
            CONV_WIDTH, CONV_WIDTH, CONV_WIDTH,
            NSA_W,
            NSA_KV_W, NSA_KV_W,
            NSA_KV_W, NSA_KV_W,
            NSA_KV_W, NSA_KV_W,
            NSA_HEADS * 3)
IN_DIM = sum(IN_SIZES)
FOX_F_OFFSET = 3 * D_MODEL + 3 * FOX_W

kernel_name = 'hybrid_fox_shortconv_nsa_block'

def rmsnorm(x, g):
    x32 = x.astype(jnp.float32)
    y = x32 * lax.rsqrt(jnp.mean(x32 * x32, axis=-1, keepdims=True) + EPS)
    return y.astype(x.dtype) * g

def causal_dwconv(u, w):
    k, c = w.shape
    return lax.conv_general_dilated(u, w[:, None, :].astype(u.dtype), window_strides=(1,),
                                    padding=[(k - 1, 0)], dimension_numbers=('NWC', 'WIO', 'NWC'),
                                    feature_group_count=c)

def masked_softmax(logits, valid):
    p = jax.nn.softmax(jnp.where(valid, logits, NEG_INF), axis=-1)
    return jnp.where(valid, p, 0.0)

def alibi_slopes(n):
    return np.array([2.0 ** (-8.0 * (i + 1) / n) for i in range(n)], dtype=np.float32)

def selection_map(n_sel, n_cmp):
    sel_start = np.arange(n_sel)[:, None] * SEL_LEN
    cmp_start = np.arange(n_cmp)[None, :] * CMP_STRIDE
    ov = np.minimum(sel_start + SEL_LEN, cmp_start + CMP_LEN) - np.maximum(sel_start, cmp_start)
    return (np.clip(ov, 0, None) / CMP_STRIDE).astype(np.float32)

def fox_attention(q, k, v, f_logit):
    b, s, _ = q.shape
    def heads(t):
        return t.reshape(b, s, FOX_HEADS, HEAD_DIM).transpose(0, 2, 1, 3)
    q, k, v = heads(q), heads(k), heads(v)
    cum = jnp.cumsum(jax.nn.log_sigmoid(f_logit.astype(jnp.float32)), axis=1).transpose(0, 2, 1)
    kpos = jnp.arange(s)
    scale = HEAD_DIM ** -0.5

    def block(i):
        q0 = i * Q_BLOCK
        qb = lax.dynamic_slice_in_dim(q, q0, Q_BLOCK, axis=2)
        cq = lax.dynamic_slice_in_dim(cum, q0, Q_BLOCK, axis=2)
        qpos = q0 + jnp.arange(Q_BLOCK)
        logits = jnp.einsum('bhqd,bhkd->bhqk', qb, k, preferred_element_type=jnp.float32) * scale
        logits = logits + cq[..., :, None] - cum[..., None, :]
        p = masked_softmax(logits, kpos[None, :] <= qpos[:, None])
        return jnp.einsum('bhqk,bhkd->bhqd', p.astype(v.dtype), v)

    out = lax.map(block, jnp.arange(s // Q_BLOCK))
    return out.transpose(1, 0, 3, 2, 4).reshape(b, s, FOX_W)

def nsa_attention(q, kc, vc, ks, vs, kw, vw, gate_logit, pe_k, w1_k, w2_k, pe_v, w1_v, w2_v):
    b, s, _ = q.shape
    G, HG, dh = NSA_KV_GROUPS, NSA_HEADS // NSA_KV_GROUPS, HEAD_DIM
    q = q.reshape(b, s, G, HG, dh).transpose(0, 2, 3, 1, 4)
    gates = jax.nn.sigmoid(gate_logit.astype(jnp.float32)).reshape(b, s, G, HG, 3).transpose(0, 2, 3, 1, 4)

    def groups(t):
        return t.reshape(b, s, G, dh).transpose(0, 2, 1, 3)

    n_cmp = (s - CMP_LEN) // CMP_STRIDE + 1
    cmp_idx = np.arange(n_cmp)[:, None] * CMP_STRIDE + np.arange(CMP_LEN)[None, :]
    cmp_end = jnp.asarray(cmp_idx[:, -1])

    def compress(t, pe, w1, w2):
        blk = groups(t)[:, :, cmp_idx]
        blk = (blk + pe).reshape(b, G, n_cmp, CMP_LEN * dh)
        return jax.nn.gelu(blk @ w1) @ w2

    k_cmp = compress(kc, pe_k, w1_k, w2_k)
    v_cmp = compress(vc, pe_v, w1_v, w2_v)
    n_sel = s // SEL_LEN
    n_top = min(SEL_TOP, n_sel)
    k_sel = groups(ks).reshape(b, G, n_sel, SEL_LEN, dh)
    v_sel = groups(vs).reshape(b, G, n_sel, SEL_LEN, dh)
    sel_map = jnp.asarray(selection_map(n_sel, n_cmp))
    pad = ((0, 0), (0, 0), (WIN, 0), (0, 0))
    k_win = jnp.pad(groups(kw), pad)
    v_win = jnp.pad(groups(vw), pad)

    slopes = jnp.asarray(alibi_slopes(NSA_HEADS)).reshape(1, G, HG, 1, 1)
    scale = dh ** -0.5
    bi = jnp.arange(b)[:, None, None, None]
    gi = jnp.arange(G)[None, :, None, None]
    sel_blk = jnp.arange(n_sel)
    n_keys_sel = n_top * SEL_LEN

    def block(i):
        q0 = i * Q_BLOCK
        qb = lax.dynamic_slice_in_dim(q, q0, Q_BLOCK, axis=3)
        gb = lax.dynamic_slice_in_dim(gates, q0, Q_BLOCK, axis=3)
        qpos = q0 + jnp.arange(Q_BLOCK)
        dist_c = (qpos[:, None] - cmp_end[None, :]).astype(jnp.float32)
        lc = jnp.einsum('bghqd,bgcd->bghqc', qb, k_cmp, preferred_element_type=jnp.float32) * scale - slopes * dist_c
        pc = masked_softmax(lc, dist_c >= 0)
        o_c = jnp.einsum('bghqc,bgcd->bghqd', pc.astype(v_cmp.dtype), v_cmp)
        imp = jnp.einsum('bghqc,jc->bgqj', pc, sel_map)
        q_blk = qpos // SEL_LEN
        valid_blk = sel_blk[None, :] * SEL_LEN <= qpos[:, None]
        forced = (sel_blk[None, :] == 0) | (sel_blk[None, :] == q_blk[:, None]) | (sel_blk[None, :] == q_blk[:, None] - 1)
        score = jnp.where(valid_blk, imp + jnp.where(forced, FORCE_BONUS, 0.0), NEG_INF)
        _, top = lax.top_k(score, n_top)
        kg = k_sel[bi, gi, top].reshape(b, G, Q_BLOCK, n_keys_sel, dh)
        vg = v_sel[bi, gi, top].reshape(b, G, Q_BLOCK, n_keys_sel, dh)
        kpos_s = (top[..., None] * SEL_LEN + jnp.arange(SEL_LEN)).reshape(b, G, 1, Q_BLOCK, n_keys_sel)
        dist_s = (qpos[:, None] - kpos_s).astype(jnp.float32)
        ls = jnp.einsum('bghqd,bgqkd->bghqk', qb, kg, preferred_element_type=jnp.float32) * scale - slopes * dist_s
        ps = masked_softmax(ls, dist_s >= 0)
        o_s = jnp.einsum('bghqk,bgqkd->bghqd', ps.astype(vg.dtype), vg)
        kb = lax.dynamic_slice_in_dim(k_win, q0, WIN + Q_BLOCK, axis=2)
        vb = lax.dynamic_slice_in_dim(v_win, q0, WIN + Q_BLOCK, axis=2)
        kpos_w = q0 - WIN + jnp.arange(WIN + Q_BLOCK)
        dist_w = qpos[:, None] - kpos_w[None, :]
        valid_w = (dist_w >= 0) & (dist_w < WIN) & (kpos_w[None, :] >= 0)
        lw = jnp.einsum('bghqd,bgkd->bghqk', qb, kb, preferred_element_type=jnp.float32) * scale - slopes * dist_w.astype(jnp.float32)
        pw = masked_softmax(lw, valid_w)
        o_w = jnp.einsum('bghqk,bgkd->bghqd', pw.astype(vb.dtype), vb)
        out = gb[..., 0:1] * o_c + gb[..., 1:2] * o_s + gb[..., 2:3] * o_w
        return out.astype(q.dtype)

    out = lax.map(block, jnp.arange(s // Q_BLOCK))
    return out.transpose(1, 0, 4, 2, 3, 5).reshape(b, s, NSA_W)

def setup_inputs(seed: int = 0) -> dict:
    key = jax.random.key(seed)
    ks = jax.random.split(key, 24)
    f32 = jnp.float32

    def nrm(k, shape, scale):
        return jax.random.normal(k, shape, f32) * scale

    res_scale = (2 * DEPTH) ** -0.5
    x = nrm(ks[0], (BATCH, SEQ, D_MODEL), 1.0)
    norm_mix_g = 1.0 + nrm(ks[1], (DEPTH, D_MODEL), 0.02)
    w_in = nrm(ks[2], (DEPTH, D_MODEL, IN_DIM), D_MODEL ** -0.5)
    b_in = nrm(ks[3], (DEPTH, IN_DIM), 0.02)
    f_bias = jax.random.uniform(ks[4], (DEPTH, FOX_HEADS), f32, 2.0, 5.0)
    b_in = b_in.at[:, FOX_F_OFFSET:FOX_F_OFFSET + FOX_HEADS].set(f_bias)
    cmp_pe_k = nrm(ks[5], (DEPTH, CMP_LEN, HEAD_DIM), 0.1)
    cmp_w1_k = nrm(ks[6], (DEPTH, CMP_LEN * HEAD_DIM, HEAD_DIM), (CMP_LEN * HEAD_DIM) ** -0.5)
    cmp_w2_k = nrm(ks[7], (DEPTH, HEAD_DIM, HEAD_DIM), HEAD_DIM ** -0.5)
    cmp_pe_v = nrm(ks[8], (DEPTH, CMP_LEN, HEAD_DIM), 0.1)
    cmp_w1_v = nrm(ks[9], (DEPTH, CMP_LEN * HEAD_DIM, HEAD_DIM), (CMP_LEN * HEAD_DIM) ** -0.5)
    cmp_w2_v = nrm(ks[10], (DEPTH, HEAD_DIM, HEAD_DIM), HEAD_DIM ** -0.5)
    sc_conv_w = nrm(ks[11], (DEPTH, CONV_K, CONV_WIDTH), CONV_K ** -0.5)
    w_br_a = nrm(ks[12], (DEPTH, FOX_W, D_MODEL), FOX_W ** -0.5)
    w_br_b = nrm(ks[13], (DEPTH, CONV_WIDTH, D_MODEL), CONV_WIDTH ** -0.5)
    w_br_c = nrm(ks[14], (DEPTH, NSA_W, D_MODEL), NSA_W ** -0.5)
    w_o = nrm(ks[15], (DEPTH, D_MODEL, D_MODEL), D_MODEL ** -0.5 * res_scale)
    norm_ffn_g = 1.0 + nrm(ks[16], (DEPTH, D_MODEL), 0.02)
    w_up = nrm(ks[17], (DEPTH, D_MODEL, 2 * D_FF), D_MODEL ** -0.5)
    ffn_conv_w = nrm(ks[18], (DEPTH, FFN_CONV_K, D_FF), FFN_CONV_K ** -0.5)
    w_down = nrm(ks[19], (DEPTH, D_FF, D_MODEL), D_FF ** -0.5 * res_scale)
    norm_final_g = 1.0 + nrm(ks[20], (D_MODEL,), 0.02)
    return {'x': x, 'norm_mix_g': norm_mix_g, 'w_in': w_in, 'b_in': b_in,
            'cmp_pe_k': cmp_pe_k, 'cmp_w1_k': cmp_w1_k, 'cmp_w2_k': cmp_w2_k,
            'cmp_pe_v': cmp_pe_v, 'cmp_w1_v': cmp_w1_v, 'cmp_w2_v': cmp_w2_v,
            'sc_conv_w': sc_conv_w, 'w_br_a': w_br_a, 'w_br_b': w_br_b, 'w_br_c': w_br_c,
            'w_o': w_o, 'norm_ffn_g': norm_ffn_g, 'w_up': w_up, 'ffn_conv_w': ffn_conv_w,
            'w_down': w_down, 'norm_final_g': norm_final_g}

def reference(x, norm_mix_g, w_in, b_in, cmp_pe_k, cmp_w1_k, cmp_w2_k, cmp_pe_v, cmp_w1_v, cmp_w2_v,
              sc_conv_w, w_br_a, w_br_b, w_br_c, w_o, norm_ffn_g, w_up, ffn_conv_w, w_down, norm_final_g):
    splits = np.cumsum(IN_SIZES)[:-1].tolist()
    for l in range(DEPTH):
        h = rmsnorm(x, norm_mix_g[l])
        z = h @ w_in[l] + b_in[l]
        (ga, gb, gc, fq, fk, fv, ff, cb, cc, cx,
         nq, nkc, nvc, nks, nvs, nkw, nvw, ng) = jnp.split(z, splits, axis=-1)
        y_a = fox_attention(fq, fk, fv, ff) @ w_br_a[l]
        y_b = (cb * causal_dwconv(cc * cx, sc_conv_w[l])) @ w_br_b[l]
        y_c = nsa_attention(nq, nkc, nvc, nks, nvs, nkw, nvw, ng,
                            cmp_pe_k[l], cmp_w1_k[l], cmp_w2_k[l],
                            cmp_pe_v[l], cmp_w1_v[l], cmp_w2_v[l]) @ w_br_c[l]
        mix = jax.nn.sigmoid(ga) * y_a + jax.nn.sigmoid(gb) * y_b + jax.nn.sigmoid(gc) * y_c
        x = x + mix @ w_o[l]
        h2 = rmsnorm(x, norm_ffn_g[l])
        u, v = jnp.split(h2 @ w_up[l], 2, axis=-1)
        u = causal_dwconv(u, ffn_conv_w[l])
        x = x + (jax.nn.silu(u) * v) @ w_down[l]
    return rmsnorm(x, norm_final_g)


_drawn_inputs = setup_inputs


def setup_inputs(seed=0):
    import zlib

    import numpy as np

    out = dict(_drawn_inputs(seed))
    spreads = {}
    factors = {'norm_mix_g': 3.742,
     'cmp_pe_k': 33.992,
     'cmp_w1_k': 2.952,
     'cmp_w2_k': 3.076,
     'cmp_pe_v': 38.144,
     'norm_ffn_g': 20.216,
     'norm_final_g': 8.749}
    for name, (base, spread) in spreads.items():
        noise = np.random.default_rng([zlib.crc32(name.encode()), seed]).standard_normal(out[name].shape)
        drawn = base * np.exp(spread * noise) if base else spread * noise
        out[name] = __import__('jax').numpy.asarray(drawn.astype(out[name].dtype))
    for name, factor in factors.items():
        out[name] = (out[name] * factor).astype(out[name].dtype)
    return out
```

```python
import concourse.bass as bass
from concourse import mybir
from contextlib import ExitStack

D_MODEL = 1024
SEQ = 512
HEAD_DIM = 64
FOX_HEADS = 8
NSA_HEADS = 8
BR_W = 512
D_FF = 2816
CMP_LEN = 32
CMP_STRIDE = 16
EPS = 1e-6
NEG = -8e30
SCALE = HEAD_DIM ** -0.5

P128 = 128
KT = D_MODEL // P128
QT = SEQ // P128
FT = D_FF // P128
PAIRS = FOX_HEADS // 2
CH = KT * P128

O_GA, O_GB, O_GC = 0, D_MODEL, 2 * D_MODEL
O_FQ = 3 * D_MODEL
O_FK = O_FQ + BR_W
O_FV = O_FK + BR_W
O_FF = O_FV + BR_W
O_CB = O_FF + FOX_HEADS
O_CC = O_CB + BR_W
O_CX = O_CC + BR_W
O_NQ = O_CX + BR_W
O_KC = O_NQ + BR_W
O_VC, O_KS, O_VS, O_KW, O_VW = (O_KC + P128 * n for n in range(1, 6))
O_NG = O_VW + P128

C_GATE = 0
C_FQ, C_FK = 24, 28
C_CB, C_CC, C_CX = 32, 36, 40
C_NQ = 44
C_NK = 48
C_SC = 52
C_GMIX, C_GFFN = 64, 72
C_PEK = 80
N_COLS1 = C_PEK + CMP_LEN
C_FFN = 0
C_PEV = 3 * FT
N_COLS2 = C_PEV + CMP_LEN

N_FOX, T_FOX = 7, 7
N_NSA, T_NSA = N_FOX + 6 * PAIRS, T_FOX + 6 * PAIRS
N_MIX, T_MIX = N_NSA + 8 * PAIRS, T_NSA + 10 * PAIRS
N_WO, T_WO = N_MIX + 8, T_MIX + 12
N_UP, T_UP = N_WO + 8, T_WO + 8
N_DN, T_DN = N_UP + 2 * FT, T_UP + 2 * FT
N_END = N_DN + FT
NSA_TILES = (0, 1, 2, 3, 5, 6, 7, 9)
Z_FOX = (1, 1)
Z_NSA = tuple(z + 3 * PAIRS for z in Z_FOX)
Z_MIX = tuple(z + 5 * PAIRS for z in Z_NSA)
Z_WO = tuple(z + 6 for z in Z_MIX)
Z_UP = tuple(z + 4 for z in Z_WO)

MIX_ORDER = (("yc", 0), ("gc", 4), ("gc", 5), ("yc", 2), ("gc", 6), ("gc", 7), ("yc", 4), ("yc", 6))

P_LEN = [P128 * (i + 1) for i in range(QT)]
P_OFF = [0, 128, 384, 768]
P_ALL = sum(P_LEN)
T_LEN = [SEQ - P128 * j for j in range(QT)]
T_OFF = [0, 512, 1024, 896]


def hybrid_block(nc, x, norm_mix_g, w_in, b_in, cmp_pe_k, cmp_w1_k, cmp_w2_k, cmp_pe_v, cmp_w1_v,
                 cmp_w2_v, sc_conv_w, w_br_a, w_br_b, w_br_c, w_o, norm_ffn_g, w_up, ffn_conv_w,
                 w_down, norm_final_g, out):
    F = mybir.dt.float32
    R = mybir.dt.float32r
    ACT = mybir.ActivationFunctionType
    ALU = mybir.AluOpType
    AX = mybir.AxisListType
    ds = bass.ds

    w_in, b_in = w_in[0], b_in[0]
    w_o, w_up, w_down = w_o[0], w_up[0], w_down[0]
    w_br = [w_br_a[0], w_br_b[0], w_br_c[0]]

    with ExitStack() as ctx:
        def sb(name, shape, dt=F, scope=ctx):
            return scope.enter_context(nc.sbuf_tensor(name, shape, dt))

        def sem(name):
            return ctx.enter_context(nc.semaphore(name))

        raw = sb("raw", [P128, 2, CH])
        w_hi = sb("w_hi", [P128, 2, CH], R)
        w_lo = sb("w_lo", [P128, 2, CH], R)
        h_hi = sb("h_hi", [P128, KT, SEQ], R)
        h_lo = sb("h_lo", [P128, KT, SEQ], R)
        ident = sb("ident", [P128, P128])
        ones = sb("ones", [P128, P128])
        cols1 = sb("cols1", [P128, N_COLS1])
        cols2 = sb("cols2", [P128, N_COLS2])
        half_b = sb("half_b", [P128, 24])
        stat = sb("stat", [P128, 4, 4])
        eps_c = sb("eps_c", [P128, 1])
        wait_cell = sb("wait_cell", [P128, 5])
        with ExitStack() as s:
            x_in = sb("x_in", [P128, QT, D_MODEL], F, s)
            x_n = sb("x_n", [P128, QT, D_MODEL], F, s)
        with ExitStack() as s:
            v_f = sb("v_f", [P128, QT, BR_W], F, s)
            v2_f = sb("v2_f", [P128, QT, 2, P128], F, s)
        br_hi = sb("br_hi", [P128, 2 * PAIRS, SEQ], R)
        br_lo = sb("br_lo", [P128, 2 * PAIRS, SEQ], R)

        att = ExitStack()
        q_hi = sb("q_hi", [P128, SEQ], R, att)
        q_lo = sb("q_lo", [P128, SEQ], R, att)
        nk_hi = sb("nk_hi", [P128, 4, SEQ], R, att)
        nk_lo = sb("nk_lo", [P128, 4, SEQ], R, att)
        vn_hi = sb("vn_hi", [P128, 2, 2, QT, P128], R, att)
        vn_lo = sb("vn_lo", [P128, 2, 2, QT, P128], R, att)
        with ExitStack() as s:
            rows1 = sb("rows1", [N_COLS1, P128], F, s)
            rows2 = sb("rows2", [N_COLS2, P128], F, s)
            fg = sb("fg", [32, SEQ], F, s)
            fe = sb("fe", [FOX_HEADS, SEQ], F, s)
            f_one = sb("f_one", [FOX_HEADS, SEQ], F, s)
        with ExitStack() as s:
            blk = sb("blk", [P128, 2, CMP_LEN, CMP_LEN], F, s)
            kc_f = sb("kc_f", [P128, SEQ], F, s)
        with ExitStack() as s:
            p_f = sb("p_f", [P128, 2, P_ALL], F, s)
        pt_lo = sb("pt_lo", [P128, 2, P_ALL], R, att)
        pt_hi = sb("pt_hi", [P128, 2, P_ALL], R, att)
        mx2 = sb("mx2", [P128, 2, QT, 2], F, att)
        mx = sb("mx", [P128, 2, QT], F, att)
        neg_mx = sb("neg_mx", [P128, 2, QT], F, att)
        p_sum = sb("p_sum", [P128, 2, QT], F, att)
        p_inv = sb("p_inv", [P128, 2, QT], F, att)
        gates = sb("gates", [P128, 3, NSA_HEADS, QT], F, att)
        c_bias = sb("c_bias", [P128, QT, 2, CMP_LEN], F, att)
        c_mask = sb("c_mask", [P128, QT, 2, CMP_LEN], F, att)
        c_p = sb("c_p", [P128, QT, 2, CMP_LEN], F, att)
        c_mx = sb("c_mx", [P128, QT, 2], F, att)
        c_sum = sb("c_sum", [P128, QT, 2], F, att)
        c_pt_hi = sb("c_pt_hi", [64, SEQ], R, att)
        c_pt_lo = sb("c_pt_lo", [64, SEQ], R, att)
        kc_hi = sb("kc_hi", [P128, CMP_LEN], R, att)
        kc_lo = sb("kc_lo", [P128, CMP_LEN], R, att)
        vc_hi = sb("vc_hi", [64, P128], R, att)
        vc_lo = sb("vc_lo", [64, P128], R, att)
        with ExitStack() as s:
            fv_hi = sb("fv_hi", [P128, QT, BR_W], R, s)
            fv_lo = sb("fv_lo", [P128, QT, BR_W], R, s)
            vp_hi = sb("vp_hi", [P128, 2, QT, P128], R, s)
            vp_lo = sb("vp_lo", [P128, 2, QT, P128], R, s)
            k_hi = sb("k_hi", [P128, SEQ], R, s)
            k_lo = sb("k_lo", [P128, SEQ], R, s)
            f_bias = sb("f_bias", [P128, 2, SEQ], F, s)
            f_diag = sb("f_diag", [P128, 2, QT, P128], F, s)
            tri = sb("tri", [P128, P128], F, s)
            conv_b = sb("conv_b", [P128, SEQ], F, s)
            conv_c = sb("conv_c", [P128, SEQ], F, s)
            conv_t = sb("conv_t", [P128, SEQ + 2], F, s)
            conv_u = sb("conv_u", [P128, SEQ], F, s)
            fg_b = sb("fg_b", [32, 1], F, s)
            ng_t = sb("ng_t", [P128, QT, 32], F, s)
            vb = sb("vb", [P128, BR_W + 2 * P128], F, s)
            w1 = sb("w1", [P128, 2, CMP_LEN, HEAD_DIM], F, s)
            w2k = sb("w2k", [P128, HEAD_DIM], F, s)
            w2v = sb("w2v", [P128, P128], F, s)
            hid_k = sb("hid_k", [P128, CMP_LEN], F, s)
            hid_v = sb("hid_v", [P128, 2 * CMP_LEN], F, s)
        with ExitStack() as s:
            mix = sb("mix", [P128, KT, SEQ], F, s)
            g_c = sb("g_c", [P128, PAIRS, SEQ], F, s)
            g_a = sb("g_a", [P128, SEQ], F, s)
            g_b = sb("g_b", [P128, SEQ], F, s)
            c_hi = sb("c_hi", [P128, PAIRS, SEQ], R, s)
            c_lo = sb("c_lo", [P128, PAIRS, SEQ], R, s)
            alibi = sb("alibi", [P128, 2, SEQ], F, s)
        att.close()

        ffn = ExitStack()
        x2 = sb("x2", [P128, KT, SEQ], F, ffn)
        with ExitStack() as s:
            x_r = sb("x_r", [P128, QT, D_MODEL], F, s)
        act_hi = sb("act_hi", [P128, FT, SEQ], R, ffn)
        act_lo = sb("act_lo", [P128, FT, SEQ], R, ffn)
        x_sq = sb("x_sq", [P128, SEQ], F, ffn)
        x_acc = sb("x_acc", [P128, SEQ], F, ffn)
        rstd = sb("rstd", [P128, SEQ], F, ffn)
        u_t = sb("u_t", [P128, SEQ + 2], F, ffn)
        u_c = sb("u_c", [P128, SEQ], F, ffn)
        v_t = sb("v_t", [P128, SEQ], F, ffn)
        y_out = sb("y_out", [P128, 2, BR_W], F, ffn)
        y_sq = sb("y_sq", [P128, BR_W], F, ffn)
        g_out = sb("g_out", [P128, D_MODEL], F, ffn)
        ffn.close()

        S = [ctx.enter_context(nc.psum_tensor(f"s_bank{n}", [P128, SEQ], F)) for n in range(5)]
        O = ctx.enter_context(nc.psum_tensor("o_bank", [P128, SEQ], F))
        Z = [ctx.enter_context(nc.psum_tensor(f"z_bank{n}", [P128, SEQ], F)) for n in range(2)]
        banks = [*S, O, *Z]

        cum_dram = nc.dram_tensor("cum_scratch", [FOX_HEADS, SEQ], F, kind="Internal").ap()

        raw_loaded = [sem("raw_loaded0"), sem("raw_loaded1")]
        hi_split = sem("hi_split")
        lo_split = sem("lo_split")
        tile_done = sem("tile_done")
        z_free = [sem("z_free0"), sem("z_free1")]
        x_loaded = [sem(f"x_loaded{t}") for t in range(QT)]
        rows_loaded = sem("rows_loaded")
        small_loaded = sem("small_loaded")
        w1_loaded = sem("w1_loaded")
        consts = sem("consts")
        raw0_zero = sem("raw0_zero")
        cols_t = sem("cols_t")
        cols_ready = sem("cols_ready")
        x_ss = sem("x_ss"); x_ms = sem("x_ms"); x_sqrt = sem("x_sqrt"); x_rs = sem("x_rs")
        x_normed = sem("x_normed")
        x_t = sem("x_t")
        h_hi_done = sem("h_hi_done"); h_lo_done = sem("h_lo_done")
        fg_ready = sem("fg_ready")
        fe_step = sem("fe_step")
        cum_stored = sem("cum_stored")
        fbias_loaded = sem("fbias_loaded")
        
        ng_t_done = sem("ng_t_done"); ng_tanh = sem("ng_tanh"); gates_ready = sem("gates_ready")
        vf_ready = sem("vf_ready"); vf_hi = sem("vf_hi"); vf_lo = sem("vf_lo")
        v2_ready = sem("v2_ready"); v2_hi = sem("v2_hi"); v2_lo = sem("v2_lo")
        q_hi_done = sem("q_hi_done"); k_hi_done = sem("k_hi_done"); nk_hi_done = sem("nk_hi_done")
        vpad = sem("vpad"); diag_ready = sem("diag_ready")
        cb_done = sem("cb_done")
        conv_t_done = sem("conv_t_done"); conv_w2 = sem("conv_w2"); conv_step = sem("conv_step")
        conv_hi = sem("conv_hi"); conv_lo = sem("conv_lo")
        a1_scored = sem("a1_scored")
        scored = sem("scored")
        masked = sem("masked")
        neg_ready = sem("neg_ready")
        exp_done = sem("exp_done")
        inv_ready = sem("inv_ready")
        normed = sem("normed")
        pt_ready = sem("pt_ready")
        pt_hi_done = sem("pt_hi_done")
        pt_lo_done = sem("pt_lo_done")
        pv_s_done = sem("pv_s_done")
        pv_done = sem("pv_done")
        o_hi_done = sem("o_hi_done"); o_lo_done = sem("o_lo_done")
        kcf = sem("kcf"); blk_ready = sem("blk_ready"); hid_done = sem("hid_done"); gelu_done = sem("gelu_done")
        cmp_done = sem("cmp_done"); cmp_hi = sem("cmp_hi"); cmp_lo = sem("cmp_lo")
        ca_scored = sem("ca_scored"); c_scored = sem("c_scored"); c_step = sem("c_step"); c_exp = sem("c_exp")
        c_ready = sem("c_ready"); c_t = sem("c_t"); c_t_hi = sem("c_t_hi"); c_t_lo = sem("c_t_lo")
        alibi_ready = sem("alibi_ready")
        mixed_a = sem("mixed_a"); mix_done = sem("mix_done"); gb_used = sem("gb_used")
        yc_free = sem("yc_free")
        mix_hi = sem("mix_hi"); mix_lo = sem("mix_lo"); gc_done = sem("gc_done")
        xr_loaded = sem("xr_loaded"); xr_t = sem("xr_t"); xr_copied = sem("xr_copied");
        xg_hi = sem("xg_hi"); xg_lo = sem("xg_lo"); sq_done = sem("sq_done"); acc_done = sem("acc_done")
        ss_done = sem("ss_done"); rs_sqrt = sem("rs_sqrt"); rs_ready = sem("rs_ready")
        u_ready = sem("u_ready"); u_w2 = sem("u_w2"); u_step = sem("u_step"); u_silu = sem("u_silu")
        v_ready = sem("v_ready"); uv_done = sem("uv_done"); act_hi_done = sem("act_hi_done"); act_lo_done = sem("act_lo_done")
        down_done = sem("down_done"); x3_done = sem("x3_done"); x3_t = sem("x3_t")
        y_sqd = sem("y_sqd"); y_ms = sem("y_ms"); y_sqrt = sem("y_sqrt"); y_rs = sem("y_rs"); y_done = sem("y_done")
        g_loaded = sem("g_loaded")
        y_stored = [sem("y_stored0"), sem("y_stored1")]

        neg_pre = sem("neg_pre")
        c_red = sem("c_red")
        N_CONST = 22

        def pt_part(tile, b):
            if b < 4:
                return tile[:, b // 2, SEQ * (b % 2):SEQ * (b % 2) + SEQ], S[b][:, :]
            return tile[:, :, 2 * SEQ:P_ALL], S[4][:, :].rearrange("p (a q) -> p a q", a=2)

        block = ctx.enter_context(nc.Block())

        w_k = w_in.rearrange("(k p) n -> p k n", p=P128)
        up_k = w_up.rearrange("(k p) n -> p k n", p=P128)
        wo_k = w_o.rearrange("(k p) n -> p k n", p=P128)

        @block.sync
        def _(sp):
            def view(slot, k):
                return raw[:, slot, :].rearrange("p (k m) -> p k m", k=k)

            def raw_free(n):
                if not isinstance(n, int) or n >= 2:
                    sp.wait_ge(lo_split, n - 1)

            def load8(n, slot, src, col):
                raw_free(n)
                for h in range(2):
                    sp.dma_start(view(slot, KT)[:, 4 * h:4 * h + 4, :],
                                 src[:, 4 * h:4 * h + 4, ds(col, P128)]).then_inc(raw_loaded[slot], 16)

            def load_nq(n, slot, t):
                raw_free(n)
                for g in range(2):
                    sp.dma_start(view(slot, KT)[:, :, 64 * g:64 * g + 64],
                                 w_k[:, :, ds(O_NQ + 256 * g + HEAD_DIM * t, HEAD_DIM)]).then_inc(raw_loaded[slot], 16)

            def load_ab(n, slot, m):
                raw_free(n)
                for b in range(2):
                    sp.dma_start(view(slot, KT)[:, 4 * b:4 * b + 4, :],
                                 w_br[b].rearrange("(k p) n -> p k n", p=P128)[:, :, ds(P128 * m, P128)]) \
                        .then_inc(raw_loaded[slot], 16)

            x_v = x[0].rearrange("(t p) n -> p t n", p=P128)
            rows = [(0, 32, b_in[O_GA:O_FV]), (C_CB, 12, b_in[O_CB:O_NQ]),
                    (C_NK, 3, b_in[O_KC:O_VS]), (C_NK + 3, 1, b_in[O_KW:O_VW]),
                    (C_SC, 12, sc_conv_w[0].rearrange("k n -> (k n)")), (C_GMIX, KT, norm_mix_g[0]),
                    (C_GFFN, KT, norm_ffn_g[0])]
            for c, n, src in rows:
                sp.dma_start(rows1[c:c + n, :], src.rearrange("(r m) -> r m", m=P128)).then_inc(rows_loaded, 16)
            for g in range(2):
                sp.dma_start(rows1[C_NQ:C_NQ + PAIRS, 64 * g:64 * g + 64],
                             b_in[O_NQ + 256 * g:O_NQ + 256 * g + 256].rearrange("(r m) -> r m", m=HEAD_DIM)) \
                    .then_inc(rows_loaded, 16)
                sp.dma_start(rows1[C_PEK:C_PEK + CMP_LEN, 64 * g:64 * g + 64], cmp_pe_k[0]).then_inc(rows_loaded, 16)
                sp.dma_start(rows2[C_PEV:C_PEV + CMP_LEN, 64 * g:64 * g + 64], cmp_pe_v[0]).then_inc(rows_loaded, 16)
            sp.dma_start(rows2[0:C_PEV, :], ffn_conv_w[0].rearrange("k (r m) -> (k r) m", m=P128)).then_inc(rows_loaded, 16)
            for t in range(QT):
                sp.dma_start(x_in[:, t, :], x_v[:, t, :]).then_inc(x_loaded[t], 16)
            sp.wait_ge(raw0_zero, 1)
            for c, o, n in ((0, O_FF, FOX_HEADS), (FOX_HEADS, O_NG, 3 * NSA_HEADS)):
                sp.dma_start(view(0, KT)[:, :, c:c + n], w_k[:, :, o:o + n]).then_inc(raw_loaded[0], 16)

            def load_v(n):
                raw_free(n)
                for kk in range(2):
                    sp.dma_start(view(n % 2, 2)[:, kk, :], w_k[:, 2 * (n - 1) + kk, O_FV:O_FF]).then_inc(raw_loaded[n % 2], 16)

            load_v(1)
            bias_v = (b_in[O_FV:O_FF], b_in[O_VS:O_KW], b_in[O_VW:O_NG])
            o = 0
            for src in bias_v:
                n = src.shape[0]
                sp.dma_start(vb[:, o:o + n], src.rearrange("(a n) -> a n", a=1).to_broadcast([P128, n])).then_inc(small_loaded, 16)
                o += n
            sp.dma_start(fg_b[0:FOX_HEADS, :], b_in[O_FF:O_CB].rearrange("(n a) -> n a", a=1)).then_inc(small_loaded, 16)
            sp.dma_start(fg_b[FOX_HEADS:32, :], b_in[O_NG:O_NG + 24].rearrange("(n a) -> n a", a=1)).then_inc(small_loaded, 16)
            for n in range(2, 5):
                load_v(n)
            for n in range(5, N_FOX):
                raw_free(n)
                for b, o in enumerate((O_VS, O_VW)):
                    sp.dma_start(view(n % 2, 4)[:, :, P128 * b:P128 * b + P128],
                                 w_k[:, 4 * (n - 5):4 * (n - 5) + 4, o:o + P128]).then_inc(raw_loaded[n % 2], 16)
            sp.wait_ge(fe_step, 6)
            sp.dma_start(cum_dram, fe[:, :]).then_inc(cum_stored, 16)
            sp.wait_ge(cum_stored, 16)
            sp.wait_ge(consts, N_CONST)
            for b, (w, w2, w2_sb) in enumerate(((cmp_w1_k, cmp_w2_k, w2k), (cmp_w1_v, cmp_w2_v, w2v))):
                for g in range(2):
                    sp.dma_start(w1[64 * g:64 * g + 64, b, :, :], w[0].rearrange("(l d) m -> d l m", d=HEAD_DIM)).then_inc(w1_loaded, 16)
                    sp.dma_start(w2_sb[64 * g:64 * g + 64, 64 * g * b:64 * g * b + 64], w2[0]).then_inc(w1_loaded, 16)

            with sp.Fori(0, PAIRS) as i:
                n = N_FOX + 6 * i
                load8(n, 1, w_k, O_FQ + P128 * i)
                sp.wait_ge(masked, i + 1)
                sp.dma_start(f_bias[:, :, :], cum_dram[ds(2 * i, 2), :].rearrange("(o h) n -> o h n", o=1)
                             .to_broadcast([P128, 2, SEQ])).then_inc(fbias_loaded, 16)
                load8(n + 1, 0, w_k, O_FK + P128 * i)
                load8(n + 2, 1, w_k, O_CB + P128 * i)
                load8(n + 3, 0, w_k, O_CC + P128 * i)
                load8(n + 4, 1, w_k, O_CX + P128 * i)
                load8(n + 5, 0, w_k, O_KC + P128 * i + P128 * ((i + 1) // 4))
            with sp.Fori(0, PAIRS) as i:
                n = N_NSA + 8 * i
                load_nq(n, 1, i)
                load8(n + 1, 0, w_k, O_GA + 2 * P128 * i)
                load8(n + 2, 1, w_k, O_GB + 2 * P128 * i)
                load_ab(n + 3, 0, 2 * i)
                load8(n + 4, 1, w_k, O_GA + P128 + 2 * P128 * i)
                load8(n + 5, 0, w_k, O_GB + P128 + 2 * P128 * i)
                load_ab(n + 6, 1, 2 * i + 1)
                load8(n + 7, 0, w_k, O_GC + P128 * i)

            def load_yc(n, m):
                raw_free(n)
                for g in range(2):
                    sp.dma_start(view(n % 2, 4)[64 * g:64 * g + 64, :, :],
                                 w_br[2].rearrange("(g t d) n -> g d t n", g=2, d=HEAD_DIM)[g, :, :, P128 * m:P128 * (m + 2)]) \
                        .then_inc(raw_loaded[n % 2], 16)

            n = N_MIX
            for step in MIX_ORDER:
                if step[0] == "yc":
                    load_yc(n, step[1])
                else:
                    load8(n, n % 2, w_k, O_GC + P128 * step[1])
                n += 1
                if step == ("gc", 5):
                    sp.wait_ge(pv_done, 2 * PAIRS + 1)
                    for t in range(QT):
                        sp.dma_start(x_r[:, t, :], x_v[:, t, :]).then_inc(xr_loaded, 16)
            for m in range(KT):
                load8(n, n % 2, wo_k, P128 * m)
                n += 1
            with sp.Fori(0, FT) as i:
                load8(N_UP + 2 * i, 1, up_k, P128 * i)
                load8(N_UP + 2 * i + 1, 0, up_k, D_FF + P128 * i)

            def load_down(n, slot, j):
                raw_free(n)
                for h in range(2):
                    sp.dma_start(view(slot, 2)[:, h, :], w_down[ds(P128 * j, P128), BR_W * h:BR_W * h + BR_W]) \
                        .then_inc(raw_loaded[slot], 16)

            with sp.Fori(0, FT // 2) as i:
                load_down(N_DN + 2 * i, 1, 2 * i)
                load_down(N_DN + 2 * i + 1, 0, 2 * i + 1)
            sp.dma_start(g_out[:, :], norm_final_g.rearrange("(a n) -> a n", a=1).to_broadcast([P128, D_MODEL])).then_inc(g_loaded, 16)
            out_v = out[0].rearrange("(t p) n -> p t n", p=P128)
            for n in range(2 * QT):
                sp.wait_ge(y_done, n + 1)
                sp.dma_start(out_v[:, n // 2, BR_W * (n % 2):BR_W * (n % 2) + BR_W], y_out[:, n % 2, :]).then_inc(y_stored[n % 2], 16)
            for b in range(2):
                sp.wait_ge(y_stored[b], 16 * QT)

        @block.gpsimd
        def _(pool):
            def split_lo(slot, n):
                pool.wait_ge(hi_split, n + 1)
                pool.tensor_tensor(w_lo[:, slot, :], raw[:, slot, :], w_hi[:, slot, :].bitcast(F), ALU.subtract) \
                    .then_inc(lo_split, 1)

            pool.memset(raw[:, 0, :], 0.0).then_inc(raw0_zero, 1)
            pool.memset(ident[:, :], 0.0).then_inc(consts, 1)
            pool.memset(ones[:, :], 1.0).then_inc(consts, 1)
            pool.wait_ge(consts, 1)
            pool.affine_select(out=ident[:, :], in_=ident[:, :], compare_op=ALU.not_equal, fill=1.0,
                               base=0, pattern=[[-1, P128]], channel_multiplier=1).then_inc(consts, 1)
            pool.memset(tri[:, :], 0.0).then_inc(consts, 1)
            pool.memset(f_one[:, :], 1.0).then_inc(consts, 1)
            pool.memset(c_mask[:, :, :, :], 1.0).then_inc(consts, 1)
            pool.iota(c_bias[:, :, :, :], [[-P128, QT], [0, 2], [CMP_STRIDE, CMP_LEN]], base=CMP_LEN - 1,
                      channel_multiplier=-1, allow_small_or_imprecise_dtypes=True).then_inc(consts, 1)
            pool.wait_ge(consts, 7)
            pool.affine_select(out=tri[:, :], in_=tri[:, :], compare_op=ALU.is_ge, fill=NEG,
                               base=0, pattern=[[-1, P128]], channel_multiplier=1).then_inc(consts, 1)
            pool.affine_select(out=c_mask[:, :, :, :], in_=c_mask[:, :, :, :], compare_op=ALU.is_ge, fill=0.0,
                               base=1 - CMP_LEN, pattern=[[P128, QT], [0, 2], [-CMP_STRIDE, CMP_LEN]],
                               channel_multiplier=1).then_inc(consts, 1)
            for a in range(2):
                pool.tensor_scalar(c_bias[:, :, a, :], c_bias[:, :, a, :], 0.5 ** (1 + 4 * a), None, ALU.mult).then_inc(consts, 1)
            pool.wait_ge(consts, 11)
            pool.affine_select(out=c_bias[:, :, :, :], in_=c_bias[:, :, :, :], compare_op=ALU.is_ge, fill=4 * NEG,
                               base=1 - CMP_LEN, pattern=[[P128, QT], [0, 2], [-CMP_STRIDE, CMP_LEN]],
                               channel_multiplier=1).then_inc(consts, 1)
            pool.memset(mx2[:, :, :, :], -3e38).then_inc(consts, 1)
            pool.memset(conv_t[:, 0:2], 0.0).then_inc(consts, 1)
            pool.memset(w2v[:, :], 0.0).then_inc(consts, 1)
            pool.memset(hid_v[:, :], 0.0).then_inc(consts, 1)
            split_lo(0, 0)
            split_lo(1, 1)
            for t in (vn_hi, vn_lo):
                pool.memset(t[:, :, :, :, :].bitcast(F), 0.0).then_inc(consts, 1)
            for t in (vp_hi, vp_lo):
                pool.memset(t[:, :, :, :].bitcast(F), 0.0).then_inc(consts, 1)
            for t in (vc_hi, vc_lo):
                pool.memset(t[:, :].bitcast(F), 0.0).then_inc(consts, 1)
            for n in range(2, N_FOX + 1):
                split_lo(n % 2, n)

            pool.wait_ge(vf_lo, QT)
            pool.wait_ge(consts, N_CONST)
            with pool.Fori(0, PAIRS) as i:
                n = N_FOX + 6 * i
                split_lo(0, n + 1)
                pool.wait_ge(pv_done, i + 1)
                for hl, (dst, src) in enumerate(((vp_hi, fv_hi), (vp_lo, fv_lo))):
                    for a in range(2):
                        pool.tensor_copy(dst[:, a, :, 64 * a:64 * a + 64],
                                         src[:, :, ds(P128 * i + 64 * a, 64)].bitcast(F)).then_inc(vpad, 1)
                split_lo(1, n + 2)
                pool.wait_ge(masked, i + 1)
                pool.wait_ge(fbias_loaded, 16 * i + 16)
                for a in range(2):
                    pool.tensor_tensor(f_diag[:, a, :, :], f_bias[:, a, :].rearrange("p (t m) -> p t m", m=P128),
                                       tri[:, :].rearrange("p (o m) -> p o m", o=1).to_broadcast([P128, QT, P128]), ALU.add) \
                        .then_inc(diag_ready, 1)
                split_lo(0, n + 3)
                split_lo(1, n + 4)
                split_lo(0, n + 5)
                split_lo(1, n + 6)
            pool.wait_ge(masked, PAIRS + 1)
            pool.wait_ge(pv_done, PAIRS + 1)
            pool.wait_ge(conv_lo, PAIRS + 1)
            pool.wait_ge(cmp_done, 2)
            for a in range(2):
                pool.iota(alibi[:, a, :], [[1, SEQ]], base=P128 - SEQ, channel_multiplier=-1,
                          allow_small_or_imprecise_dtypes=True).then_inc(alibi_ready, 1)
            for a in range(2):
                pool.wait_ge(alibi_ready, 2 + a)
                pool.tensor_scalar(alibi[:, a, :], alibi[:, a, :], 8 * 0.5 ** (1 + 4 * a), None, ALU.mult).then_inc(alibi_ready, 1)
            pool.wait_ge(alibi_ready, 4)
            pool.affine_select(out=alibi[:, :, :], in_=alibi[:, :, :], compare_op=ALU.is_ge, fill=16 * NEG,
                               base=SEQ - P128, pattern=[[0, 2], [-1, SEQ]], channel_multiplier=1).then_inc(alibi_ready, 1)
            with pool.Fori(0, (N_END - N_NSA - 1) // 2) as i:
                split_lo(0, N_NSA + 2 * i + 1)
                split_lo(1, N_NSA + 2 * i + 2)
            assert (N_END - N_NSA - 1) % 2 == 1
            split_lo((N_END - 1) % 2, N_END - 1)

        @block.tensor
        def _(pe):
            def mm3(out, w, r, first, last):
                pe.matmul(out, w[0], r[0], start=first, stop=False)
                pe.matmul(out, w[0], r[1], start=False, stop=False)
                return pe.matmul(out, w[1], r[0], start=False, stop=last)

            def wt(slot, k, k_tiles=KT, m=0):
                wide = CH // k_tiles
                o = k * wide + m
                return w_hi[:, slot, o:o + P128], w_lo[:, slot, o:o + P128]

            def project(slot, z, n, z_count, act=(h_hi, h_lo)):
                pe.wait_ge(z_free[z], z_count)
                pe.wait_ge(lo_split, n + 1)
                for k in range(KT):
                    mm = mm3(Z[z][:, :], wt(slot, k), (act[0][:, k, :], act[1][:, k, :]), k == 0, k == KT - 1)
                mm.then_inc(tile_done, 1)

            def branch(slot, z, n, z_count, br, k0):
                pe.wait_ge(z_free[z], z_count)
                pe.wait_ge(lo_split, n + 1)
                for k in range(PAIRS):
                    mm = mm3(Z[z][:, :], wt(slot, k0 + k), (br_hi[:, br + k, :], br_lo[:, br + k, :]), k == 0, k == PAIRS - 1)
                mm.then_inc(tile_done, 1)

            def scores(kh, kl, pair):
                def qk(a, i, bank, col):
                    rows = slice(64 * a, 64 * a + 64)
                    q = (q_hi[rows, P128 * i:P128 * i + P128], q_lo[rows, P128 * i:P128 * i + P128])
                    return mm3(S[bank][:, col:col + P_LEN[i]], q, (kh[rows, 0:P_LEN[i]], kl[rows, 0:P_LEN[i]]), True, True)
                qk(0, 1, 4, 0).then_inc(a1_scored, 1)
                qk(0, 3, 0, 0).then_inc(scored, 1)
                qk(0, 2, 1, 0)
                qk(0, 0, 1, P_LEN[2]).then_inc(scored, 1)
                qk(1, 3, 2, 0).then_inc(scored, 1)
                qk(1, 2, 3, 0)
                qk(1, 0, 3, P_LEN[2]).then_inc(scored, 1)
                pe.wait_ge(a1_scored, pair + 1)
                qk(1, 1, 4, P_LEN[1]).then_inc(scored, 1)

            def transposes(pair):
                pe.wait_ge(normed, pair + 1)
                def pt(a, j, bank, col):
                    for i in range(j, QT):
                        mm = pe.transpose(S[bank][:, col + P128 * (i - j):col + P128 * (i - j + 1)],
                                          p_f[:, a, P_OFF[i] + P128 * j:P_OFF[i] + P128 * (j + 1)], ident[:, :])
                    return mm
                for a in range(2):
                    pt(a, 0, 2 * a, 0).then_inc(pt_ready, 1)
                    pt(a, 1, 2 * a + 1, 0)
                    pt(a, 3, 2 * a + 1, T_LEN[1]).then_inc(pt_ready, 1)
                pt(0, 2, 4, 0)
                pt(1, 2, 4, T_LEN[2]).then_inc(pt_ready, 1)

            def product(vh, vl, pair, first, last):
                pe.wait_ge(pt_lo_done, 5 * pair + 5 + 1)
                for a in range(2):
                    for j in range(QT):
                        o = T_OFF[j]
                        mm = mm3(O[:, P128 * j:SEQ], (vh[:, a, j, :], vl[:, a, j, :]),
                                 (pt_hi[:, a, o:o + T_LEN[j]], pt_lo[:, a, o:o + T_LEN[j]]),
                                 first and a == 0 and j == 0, last and a == 1 and j == QT - 1)
                return mm

            for done in (pv_done, c_t):
                pe.sem_inc(done, 1)
            pe.wait_ge(consts, 3)
            pe.wait_ge(rows_loaded, 16 * 14)
            pe.transpose(Z[1][:, 0:N_COLS1], rows1[:, :], ident[0:N_COLS1, 0:N_COLS1])
            pe.transpose(Z[1][:, P128:P128 + N_COLS2], rows2[:, :], ident[0:N_COLS2, 0:N_COLS2]).then_inc(cols_t, 1)
            pe.wait_ge(cols_ready, 2)
            for t in range(QT):
                pe.wait_ge(x_normed, t + 1)
                for k in range(KT):
                    mm = pe.transpose(banks[k][:, P128 * t:P128 * t + P128], x_n[:, t, P128 * k:P128 * k + P128], ident[:, :])
                    if t == QT - 1:
                        mm.then_inc(x_t, 1)
            pe.wait_ge(h_lo_done, KT)
            pe.wait_ge(lo_split, 1)
            for k in range(KT):
                mm = mm3(Z[0][:, :], wt(0, k), (h_hi[:, k, :], h_lo[:, k, :]), k == 0, k == KT - 1)
            mm.then_inc(tile_done, 1)
            for n in range(1, 5):
                pe.wait_ge(lo_split, n + 1)
                for kk in range(2):
                    k = 2 * (n - 1) + kk
                    w = [p[:, n % 2, BR_W * kk:BR_W * kk + BR_W] for p in (w_hi, w_lo)]
                    for t in range(QT):
                        toks = slice(P128 * t, P128 * t + P128)
                        mm = mm3(S[t][:, :], (h_hi[:, k, toks], h_lo[:, k, toks]), w, k == 0, k == KT - 1)
                mm.then_inc(tile_done, 1)
                if n == 1:
                    pe.wait_ge(fg_ready, 1)
                    for t in range(QT):
                        mm = pe.transpose(Z[1][:, 32 * t:32 * t + 32], fg[:, P128 * t:P128 * t + P128], ident[0:32, 0:32])
                    mm.then_inc(ng_t_done, 1)
            v2_bank = [S[4], O, Z[0], Z[1]]
            pe.wait_ge(ng_tanh, 1)
            for n in range(5, N_FOX):
                pe.wait_ge(lo_split, n + 1)
                for kk in range(4):
                    k = 4 * (n - 5) + kk
                    w = [p[:, n % 2, 256 * kk:256 * kk + 256] for p in (w_hi, w_lo)]
                    for t in range(QT):
                        toks = slice(P128 * t, P128 * t + P128)
                        mm = mm3(v2_bank[t][:, 0:256], (h_hi[:, k, toks], h_lo[:, k, toks]), w, k == 0, k == KT - 1)
                mm.then_inc(tile_done, 1)
            pe.wait_ge(v2_ready, 2)
            pe.wait_ge(vf_ready, QT)

            with pe.Fori(0, PAIRS) as i:
                n, z = N_FOX + 6 * i, 3 * i
                project(1, 0, n, Z_FOX[0] + z)
                project(0, 1, n + 1, Z_FOX[1] + z)
                project(1, 0, n + 2, Z_FOX[0] + z + 1)
                pe.wait_ge(z_free[1], Z_FOX[1] + z + 1)
                pe.wait_ge(pt_lo_done, 5 * i + 1)
                scores(k_hi, k_lo, i)
                project(0, 1, n + 3, Z_FOX[1] + z + 1)
                project(1, 0, n + 4, Z_FOX[0] + z + 2)
                transposes(i)
                project(0, 1, n + 5, Z_FOX[1] + z + 2)
                pe.wait_ge(vpad, 4 * i + 4)
                pe.wait_ge(o_lo_done, i + 1)
                product(vp_hi, vp_lo, i, True, True).then_inc(pv_done, 1)

            pe.wait_ge(w1_loaded, 16 * 8)
            for b in range(2):
                pe.wait_ge(blk_ready, 2 * b + 2)
                for l in range(CMP_LEN):
                    for g in range(2):
                        rows = slice(64 * g, 64 * g + 64)
                        mm = pe.matmul(S[b][rows, 0:CMP_LEN], w1[rows, b, l, :], blk[rows, b, l, :],
                                       start=(l == 0), stop=(l == CMP_LEN - 1))
                mm.then_inc(hid_done, 1)
            pe.wait_ge(gelu_done, 1)
            for g in range(2):
                rows = slice(64 * g, 64 * g + 64)
                mm = pe.matmul(S[2][rows, 0:CMP_LEN], w2k[rows, :], hid_k[rows, :], start=True, stop=True)
            mm.then_inc(cmp_done, 1)
            pe.wait_ge(gelu_done, 3)
            pe.matmul(S[3][0:64, 0:P128], hid_v[:, :], w2v[:, :], start=True, stop=True).then_inc(cmp_done, 1)
            pe.wait_ge(cmp_lo, 2)

            with pe.Fori(0, PAIRS) as i:
                n, z = N_NSA + 8 * i, 5 * i
                z0, z1 = Z_NSA[0] + z, Z_NSA[1] + z
                project(1, 0, n, z0)
                project(0, 1, n + 1, z1)
                pe.wait_ge(z_free[0], z0 + 1)
                pe.wait_ge(pt_lo_done, 5 * (PAIRS + 2 * i) + 1)
                pe.wait_ge(o_lo_done, PAIRS + i + 1)

                def c_scores(a):
                    rows = slice(64 * a, 64 * a + 64)
                    for t in range(QT):
                        toks = slice(P128 * t, P128 * t + P128)
                        mm = mm3(O[:, 64 * t + 32 * a:64 * t + 32 * a + 32], (q_hi[rows, toks], q_lo[rows, toks]),
                                 (kc_hi[rows, :], kc_lo[rows, :]), True, True)
                    return mm
                c_scores(0).then_inc(ca_scored, 1)
                scores(nk_hi[:, 2, :], nk_lo[:, 2, :], PAIRS + 2 * i)
                pe.wait_ge(ca_scored, i + 1)
                c_scores(1).then_inc(c_scored, 1)
                project(1, 0, n + 2, z0 + 1)
                branch(0, 1, n + 3, z1 + 1, 0, 0)
                branch(0, 0, n + 3, z0 + 2, PAIRS, 4)
                transposes(PAIRS + 2 * i)
                pe.wait_ge(consts, N_CONST)
                pe.wait_ge(c_ready, i + 1)
                for t in range(QT):
                    mm = pe.transpose(O[0:64, P128 * t:P128 * t + P128],
                                      c_p[:, t, :, :].rearrange("p a c -> p (a c)"), ident[:, :])
                mm.then_inc(c_t, 1)
                project(1, 1, n + 4, z1 + 2)
                pe.wait_ge(c_t_lo, i + 1)
                mm3(O[:, :], (vc_hi[:, :], vc_lo[:, :]), (c_pt_hi[:, :], c_pt_lo[:, :]), True, False)
                product(vn_hi[:, 0, :, :, :], vn_lo[:, 0, :, :, :], PAIRS + 2 * i, False, False).then_inc(pv_s_done, 1)
                scores(nk_hi[:, 3, :], nk_lo[:, 3, :], PAIRS + 2 * i + 1)
                project(0, 0, n + 5, z0 + 3)
                branch(1, 1, n + 6, z1 + 3, 0, 0)
                branch(1, 0, n + 6, z0 + 4, PAIRS, 4)
                transposes(PAIRS + 2 * i + 1)
                project(0, 1, n + 7, z1 + 4)
                product(vn_hi[:, 1, :, :, :], vn_lo[:, 1, :, :, :], PAIRS + 2 * i + 1, False, True).then_inc(pv_done, 1)

            n, tau = N_MIX, 0
            for kind, m in MIX_ORDER:
                if kind == "gc":
                    project(n % 2, tau % 2, n, Z_MIX[tau % 2] + tau // 2)
                    tau += 1
                else:
                    pe.wait_ge(lo_split, n + 1)
                    pe.wait_ge(o_lo_done, 2 * PAIRS + 1)
                    for mt in range(2):
                        pe.wait_ge(z_free[tau % 2], Z_MIX[tau % 2] + tau // 2)
                        for k in range(PAIRS):
                            mm = mm3(Z[tau % 2][:, :], wt(n % 2, k, 4, P128 * mt), (c_hi[:, k, :], c_lo[:, k, :]),
                                     k == 0, k == PAIRS - 1)
                        mm.then_inc(tile_done, 1)
                        tau += 1
                n += 1
            pe.wait_ge(mix_lo, KT)
            pe.wait_ge(xr_loaded, 16 * QT)
            for m in range(KT):
                if m >= 4:
                    pe.wait_ge(xr_copied, m - 3)
                for t in range(QT):
                    mm = pe.transpose(S[m % 4][:, P128 * t:P128 * t + P128], x_r[:, t, P128 * m:P128 * m + P128], ident[:, :])
                mm.then_inc(xr_t, 1)
                project((N_WO + m) % 2, m % 2, N_WO + m, Z_WO[m % 2] + m // 2, (br_hi, br_lo))
            pe.wait_ge(acc_done, KT)
            pe.matmul(S[4][:, :], ones[:, :], x_acc[:, :], start=True, stop=True).then_inc(ss_done, 1)
            pe.wait_ge(xg_lo, KT)
            with pe.Fori(0, FT) as i:
                project(1, 0, N_UP + 2 * i, Z_UP[0] + i)
                project(0, 1, N_UP + 2 * i + 1, Z_UP[1] + i)

            def down(slot, n, j, first, last):
                pe.wait_ge(lo_split, n + 1)
                pe.wait_ge(act_lo_done, j + 1 + 1)
                act = (act_hi[:, j, :], act_lo[:, j, :])
                for m in range(KT):
                    mm = mm3(banks[m][:, :], wt(slot, m), act, first, last)
                    if last:
                        mm.then_inc(down_done, 1)
                if not last:
                    mm.then_inc(tile_done, 1)

            pe.wait_ge(z_free[0], Z_UP[0] + FT)
            pe.wait_ge(z_free[1], Z_UP[1] + FT)
            down(1, N_DN, 0, True, False)
            down(0, N_DN + 1, 1, False, False)
            with pe.Fori(1, FT // 2 - 1) as i:
                down(1, N_DN + 2 * i, 2 * i, False, False)
                down(0, N_DN + 2 * i + 1, 2 * i + 1, False, False)
            down(1, N_DN + FT - 2, FT - 2, False, False)
            down(0, N_DN + FT - 1, FT - 1, False, True)
            for h in range(2):
                for m in range(4 * h, 4 * h + 4):
                    pe.wait_ge(x3_done, max(m, 4 * h + 3) + 1)
                    for t in range(QT):
                        mm = pe.transpose(banks[4 * h + t][:, P128 * (m % 4):P128 * (m % 4) + P128],
                                          x2[:, m, P128 * t:P128 * t + P128], ident[:, :])
                mm.then_inc(x3_t, 1)

        @block.scalar
        def _(act):
            def split_hi(slot, n, tiles):
                act.wait_ge(raw_loaded[slot], 32 * (n // 2) + 32)
                act.wait_ge(tile_done, tiles)
                act.activation(w_hi[:, slot, :], raw[:, slot, :], ACT.Copy).then_inc(hi_split, 1)

            def split_hi_in_loop(slot, loads, tiles):
                act.wait_ge(raw_loaded[slot], 32 * loads)
                act.wait_ge(tile_done, tiles)
                act.activation(w_hi[:, slot, :], raw[:, slot, :], ACT.Copy).then_inc(hi_split, 1)

            def evac_hi(dst, src, done, bias=0.0):
                act.activation(dst, src, ACT.Identity, bias=bias).then_inc(done, 1)

            def exponentials(pair):
                act.wait_ge(neg_ready, pair + 1)
                for a in range(2):
                    for i in range(QT):
                        t = p_f[:, a, P_OFF[i]:P_OFF[i] + P_LEN[i]]
                        act.activation(t, t, ACT.Exp, bias=neg_mx[:, a, i:i + 1], accum_out=p_sum[:, a, i:i + 1]).then_inc(exp_done, 1)

            def pt_high(pair):
                for b in range(5):
                    act.wait_ge(pt_ready, 5 * pair + b + 1)
                    dst, src = pt_part(pt_hi, b)
                    act.activation(dst, src, ACT.Copy).then_inc(pt_hi_done, 1)

            for t in range(QT):
                act.wait_ge(x_loaded[t], 16)
                act.activation(x_n[:, t, :], x_in[:, t, :], ACT.Square, accum_out=stat[:, 0, t:t + 1]).then_inc(x_ss, 1)
            act.wait_ge(x_ms, 1)
            act.activation(stat[:, 2, :], stat[:, 1, :], ACT.Sqrt).then_inc(x_sqrt, 1)
            split_hi(0, 0, 0)
            split_hi(1, 1, 0)
            act.wait_ge(cols_ready, 2)
            for k in range(KT):
                act.wait_ge(x_t, k + 1)
                act.activation(h_hi[:, k, :], banks[k][:, :], ACT.Copy, scale=cols1[:, C_GMIX + k:C_GMIX + k + 1]).then_inc(h_hi_done, 1)
            act.wait_ge(small_loaded, 16 * 5)
            act.wait_ge(tile_done, 1)
            act.activation(fg[:, :], Z[0][0:32, :], ACT.Identity, bias=fg_b[:, :]).then_inc(fg_ready, 1)
            split_hi(0, 2, 1)
            act.wait_ge(fe_step, 1)
            act.activation(fe[:, :], fe[:, :], ACT.Exp).then_inc(fe_step, 1)
            act.wait_ge(fe_step, 2)
            act.activation(fe[:, :], fe[:, :], ACT.Ln, bias=1.0).then_inc(fe_step, 1)
            split_hi(1, 3, 2)
            act.wait_ge(ng_t_done, 1)
            act.activation(ng_t[:, :, :].rearrange("p t c -> p (t c)"), Z[1][:, 0:P128], ACT.Tanh, scale=0.5).then_inc(ng_tanh, 1)
            split_hi(0, 4, 3)
            split_hi(1, 5, 4)
            split_hi(0, 6, 5)
            for t in range(QT):
                act.wait_ge(vf_ready, t + 1)
                act.activation(fv_hi[:, t, :], v_f[:, t, :], ACT.Copy).then_inc(vf_hi, 1)
            split_hi(1, 7, 6)
            for z in range(2):
                act.wait_ge(z_free[z], 1)
            act.wait_ge(consts, N_CONST)
            for a in range(2):
                act.activation(vn_hi[:, :, a, :, 64 * a:64 * a + 64],
                               v2_f[:, :, :, 64 * a:64 * a + 64].rearrange("p t b d -> p b t d"), ACT.Copy).then_inc(v2_hi, 1)

            with act.Fori(0, PAIRS) as i:
                T, L = T_FOX + 6 * i, 3 * i
                split_hi_in_loop(0, L + 5, T)
                act.wait_ge(tile_done, T + 1)
                evac_hi(q_hi[:, :], Z[0][:, :], q_hi_done, cols1[:, ds(C_FQ + i, 1)])
                split_hi_in_loop(1, L + 5, T + 1)
                act.wait_ge(tile_done, T + 2)
                evac_hi(k_hi[:, :], Z[1][:, :], k_hi_done, cols1[:, ds(C_FK + i, 1)])
                split_hi_in_loop(0, L + 6, T + 2)
                act.wait_ge(conv_step, 3 * i + 1)
                act.wait_ge(tile_done, T + 3)
                act.activation(conv_b[:, :], Z[0][:, :], ACT.Identity, bias=cols1[:, ds(C_CB + i, 1)]).then_inc(z_free[0], 1)
                split_hi_in_loop(1, L + 6, T + 3)
                exponentials(i)
                act.wait_ge(tile_done, T + 4)
                act.wait_ge(conv_lo, i + 1)
                act.activation(conv_c[:, :], Z[1][:, :], ACT.Identity, bias=cols1[:, ds(C_CC + i, 1)]).then_inc(z_free[1], 1)
                split_hi_in_loop(0, L + 7, T + 4)
                split_hi_in_loop(1, L + 7, T + 5)
                pt_high(i)
                act.wait_ge(conv_t_done, i + 1)
                act.activation(conv_u[:, :], conv_t[:, 2:SEQ + 2], ACT.Copy, scale=cols1[:, ds(C_SC + 8 + i, 1)]).then_inc(conv_w2, 1)
                act.wait_ge(tile_done, T + 6)
                evac_hi(nk_hi[:, i, :], Z[1][:, :], nk_hi_done, cols1[:, ds(C_NK + i, 1)])
                act.wait_ge(conv_step, 3 * i + 3 + 1)
                act.activation(br_hi[:, PAIRS + i, :], conv_c[:, :], ACT.Copy).then_inc(conv_hi, 1)
                act.wait_ge(pv_done, i + 1 + 1)
                act.activation(br_hi[:, i, :], O[:, :], ACT.Copy).then_inc(o_hi_done, 1)

            for b, dst in enumerate(([(hid_k[:, :], S[0][:, 0:CMP_LEN])],
                                     [(hid_v[0:64, 0:CMP_LEN], S[1][0:64, 0:CMP_LEN]),
                                      (hid_v[64:128, CMP_LEN:2 * CMP_LEN], S[1][64:128, 0:CMP_LEN])])):
                act.wait_ge(hid_done, b + 1)
                for d, s in dst:
                    act.activation(d, s, ACT.Gelu_apprx_tanh).then_inc(gelu_done, 1)
            act.wait_ge(cmp_done, 1)
            act.activation(kc_hi[:, :], S[2][:, 0:CMP_LEN], ACT.Copy).then_inc(cmp_hi, 1)
            act.wait_ge(cmp_done, 2)
            act.activation(vc_hi[:, :], S[3][0:64, 0:P128], ACT.Copy).then_inc(cmp_hi, 1)

            with act.Fori(0, PAIRS) as i:
                T, L = T_NSA + 10 * i, 4 * i + N_NSA // 2
                z0, z1 = Z_NSA[0] + 5 * i, Z_NSA[1] + 5 * i
                split_hi_in_loop(0, L + 2, T)
                act.wait_ge(tile_done, T + 1)
                evac_hi(q_hi[:, :], Z[0][:, :], q_hi_done, cols1[:, ds(C_NQ + i, 1)])
                split_hi_in_loop(1, L + 2, T + 1)

                def tanh_gate(dst, z, col):
                    act.activation(dst, Z[z][:, :], ACT.Tanh, bias=half_b[:, col], scale=0.5).then_inc(z_free[z], 1)

                act.wait_ge(z_free[1], z1 - 1)
                act.wait_ge(tile_done, T + 2)
                tanh_gate(g_a[:, :], 1, ds(2 * i, 1))
                split_hi_in_loop(0, L + 3, T + 2)
                exponentials(PAIRS + 2 * i)
                act.wait_ge(c_step, 5 * i + 3)
                act.activation(c_p[:, :, :, :], c_p[:, :, :, :], ACT.Exp).then_inc(c_exp, 1)
                act.wait_ge(gb_used, 2 * i + 1)
                act.wait_ge(tile_done, T + 3)
                tanh_gate(g_b[:, :], 0, ds(8 + 2 * i, 1))
                split_hi_in_loop(1, L + 3, T + 3)
                split_hi_in_loop(0, L + 4, T + 5)
                pt_high(PAIRS + 2 * i)
                act.wait_ge(c_t, i + 1 + 1)
                act.activation(c_pt_hi[:, :], O[0:64, :], ACT.Copy).then_inc(c_t_hi, 1)
                act.wait_ge(z_free[1], z1 + 2)
                act.wait_ge(tile_done, T + 6)
                tanh_gate(g_a[:, :], 1, ds(2 * i + 1, 1))
                split_hi_in_loop(1, L + 4, T + 6)
                exponentials(PAIRS + 2 * i + 1)
                act.wait_ge(gb_used, 2 * i + 1 + 1)
                act.wait_ge(tile_done, T + 7)
                tanh_gate(g_b[:, :], 0, ds(8 + 2 * i + 1, 1))
                split_hi_in_loop(0, L + 5, T + 7)
                split_hi_in_loop(1, L + 5, T + 9)
                pt_high(PAIRS + 2 * i + 1)
                act.wait_ge(tile_done, T + 10)
                tanh_gate(g_c[:, i, :], 1, ds(16 + i, 1))
                act.wait_ge(pv_done, PAIRS + i + 1 + 1)
                act.activation(c_hi[:, i, :], O[:, :], ACT.Copy).then_inc(o_hi_done, 1)

            def mix_high(m):
                act.wait_ge(mix_done, m + 1)
                act.activation(br_hi[:, m, :], mix[:, m, :], ACT.Copy, scale=0.5).then_inc(mix_hi, 1)

            n, tau = N_MIX, 0
            pending = []
            for kind, m in MIX_ORDER:
                split_hi((n + 1) % 2, n + 1, T_MIX + tau)
                for mt in pending:
                    mix_high(mt)
                pending = []
                if kind == "gc":
                    act.wait_ge(mix_done, m - 3)
                    act.wait_ge(tile_done, T_MIX + tau + 1)
                    act.activation(g_c[:, m % PAIRS, :], Z[tau % 2][:, :], ACT.Tanh,
                                   bias=half_b[:, 16 + m:17 + m], scale=0.5).then_inc(z_free[tau % 2], 1)
                    tau += 1
                else:
                    tau += 2
                    pending = [m, m + 1]
                n += 1
            for mt in pending:
                mix_high(mt)
            for m in range(KT):
                split_hi((N_WO + m + 1) % 2, N_WO + m + 1, T_WO + m)
                act.wait_ge(xr_t, m + 1)
                act.activation(x2[:, m, :], S[m % 4][:, :], ACT.Copy).then_inc(xr_copied, 1)
                act.wait_ge(z_free[m % 2], Z_WO[m % 2] + m // 2 + 1)
                act.activation(h_hi[:, m, :], x2[:, m, :], ACT.Copy, scale=cols1[:, C_GFFN + m:C_GFFN + m + 1]).then_inc(xg_hi, 1)
            act.wait_ge(ss_done, 1)
            act.activation(rstd[:, :], S[4][:, :], ACT.Sqrt, bias=eps_c[:, :], scale=1.0 / D_MODEL).then_inc(rs_sqrt, 1)

            with act.Fori(0, FT) as i:
                T, L = T_UP + 2 * i, i + N_UP // 2
                split_hi_in_loop(0, L + 2, T)
                act.wait_ge(u_ready, i + 1)
                act.wait_ge(act_lo_done, i + 1)
                act.activation(u_c[:, :], u_t[:, 2:SEQ + 2], ACT.Copy, scale=cols2[:, ds(C_FFN + 2 * FT + i, 1)]).then_inc(u_w2, 1)
                split_hi_in_loop(1, L + 2, T + 1)
                act.wait_ge(u_step, 2 * i + 2 + 1)
                act.activation(u_c[:, :], u_c[:, :], ACT.Silu).then_inc(u_silu, 1)
                act.wait_ge(uv_done, i + 1)
                act.activation(act_hi[:, i, :], u_c[:, :], ACT.Copy).then_inc(act_hi_done, 1)
            T, L = T_DN, N_DN // 2
            with act.Fori(0, FT // 2 - 1) as i:
                split_hi_in_loop(0, L + i + 2, T + 2 * i)
                split_hi_in_loop(1, L + i + 2, T + 2 * i + 1)
            split_hi_in_loop(0, L + FT // 2 + 1, T + FT - 2)
            for h in range(2):
                act.wait_ge(x3_t, h + 1)
                for t in range(QT):
                    if h + t:
                        act.wait_ge(y_sqd, QT * h + t)
                    act.activation(y_sq[:, :], banks[QT * h + t][:, :], ACT.Square, accum_out=stat[:, h, t:t + 1]).then_inc(y_sqd, 1)
            act.wait_ge(y_ms, 2)
            act.activation(stat[:, 2, :], stat[:, 2, :], ACT.Sqrt).then_inc(y_sqrt, 1)

        @block.vector
        def _(dve):
            def sub_lo(dst, src, bias, hi, done):
                dve.scalar_tensor_tensor(dst, src, bias, hi.bitcast(F), ALU.add, ALU.subtract).then_inc(done, 1)

            def pt_low(pair):
                for b in range(5):
                    dve.wait_ge(pt_hi_done, 5 * pair + b + 1)
                    if b == 0:
                        dve.wait_ge(pt_ready, 5 * pair + 5)
                    dst, src = pt_part(pt_lo, b)
                    hi, _ = pt_part(pt_hi, b)
                    dve.tensor_tensor(dst, src, hi.bitcast(F), ALU.subtract).then_inc(pt_lo_done, 1)

            score_at = {(0, 3): (0, 0, 1), (0, 2): (1, 0, 2), (0, 0): (1, P_LEN[2], 2), (1, 3): (2, 0, 3),
                        (1, 2): (3, 0, 4), (1, 0): (3, P_LEN[2], 4), (0, 1): (4, 0, 5), (1, 1): (4, P_LEN[1], 5)}

            def mask_tile(a, i, k0, k1, bias, top):
                bank, col, _ = score_at[a, i]
                return dve.tensor_tensor_reduce(p_f[:, a, P_OFF[i] + k0:P_OFF[i] + k1], S[bank][:, col + k0:col + k1],
                                                bias, SCALE, -3e38, ALU.add, ALU.max, top)

            def wait_scores(pair, a, i):
                n = score_at[a, i][2]
                if (a, i) in ((0, 3), (0, 2), (1, 3), (1, 2), (0, 1)):
                    dve.wait_ge(scored, 5 * pair + n)
                    dve.memset(wait_cell[:, n - 1:n], 0.0)

            def invert(pair):
                dve.wait_ge(exp_done, 8 * pair + 8)
                dve.reciprocal(p_inv[:, :, :], p_sum[:, :, :]).then_inc(inv_ready, 1)

            def normalise(pair):
                for a in range(2):
                    for i in range(QT):
                        t = p_f[:, a, P_OFF[i]:P_OFF[i] + P_LEN[i]]
                        op = dve.tensor_scalar(t, t, p_inv[:, a, i:i + 1], None, ALU.mult)
                op.then_inc(normed, 1)

            for done in (pt_lo_done, o_lo_done, masked, conv_step, conv_lo, gb_used, act_lo_done, u_step):
                dve.sem_inc(done, 1)
            dve.memset(eps_c[:, :], EPS)
            dve.wait_ge(cols_t, 1)
            dve.tensor_copy(cols1[:, :], Z[1][:, 0:N_COLS1]).then_inc(cols_ready, 1)
            dve.tensor_copy(cols2[:, :], Z[1][:, P128:P128 + N_COLS2]).then_inc(cols_ready, 1)
            dve.wait_ge(cols_ready, 1)
            dve.tensor_scalar(half_b[:, :], cols1[:, C_GATE:C_GATE + 24], 0.5, None, ALU.mult)
            dve.wait_ge(x_ss, QT)
            dve.tensor_scalar(stat[:, 1, :], stat[:, 0, :], 1.0 / D_MODEL, EPS, ALU.mult, ALU.add).then_inc(x_ms, 1)
            dve.wait_ge(x_sqrt, 1)
            dve.reciprocal(stat[:, 3, :], stat[:, 2, :]).then_inc(x_rs, 1)
            dve.wait_ge(x_rs, 1)
            for t in range(QT):
                dve.tensor_scalar(x_n[:, t, :], x_in[:, t, :], stat[:, 3, t:t + 1], None, ALU.mult).then_inc(x_normed, 1)
            for k in range(KT):
                dve.wait_ge(h_hi_done, k + 1)
                dve.scalar_tensor_tensor(h_lo[:, k, :], banks[k][:, :], cols1[:, C_GMIX + k:C_GMIX + k + 1],
                                         h_hi[:, k, :].bitcast(F), ALU.mult, ALU.subtract).then_inc(h_lo_done, 1)
            dve.wait_ge(fg_ready, 1)
            f = fg[0:FOX_HEADS, :]
            dve.scalar_tensor_tensor(fe[:, :], f, -1.0, f, ALU.mult, ALU.min).then_inc(fe_step, 1)
            dve.wait_ge(fe_step, 3)
            dve.scalar_tensor_tensor(fe[:, :], fg[0:FOX_HEADS, :], 0.0, fe[:, :], ALU.min, ALU.subtract).then_inc(fe_step, 1)
            dve.wait_ge(consts, 5)
            dve.wait_ge(fe_step, 4)
            dve.tensor_tensor_scan(fe[:, :], f_one[:, :], fe[:, :], 0.0, ALU.mult, ALU.add).then_inc(fe_step, 1)
            dve.wait_ge(fe_step, 5)
            dve.tensor_scalar(fe[:, :], fe[:, :], -1.0 / SCALE, None, ALU.mult).then_inc(fe_step, 1)
            dve.wait_ge(ng_tanh, 1)
            dve.tensor_scalar(gates[:, :, :, :], ng_t[:, :, FOX_HEADS:32].rearrange("p t (h b) -> p b h t", b=3),
                              0.5, 0.5, ALU.mult, ALU.add).then_inc(gates_ready, 1)
            dve.wait_ge(small_loaded, 16 * 5)
            dve.wait_ge(tile_done, 5)
            for t in range(QT):
                dve.tensor_tensor(v_f[:, t, :], S[t][:, :], vb[:, 0:BR_W], ALU.add).then_inc(vf_ready, 1)
            for t in range(QT):
                dve.wait_ge(vf_hi, t + 1)
                dve.tensor_tensor(fv_lo[:, t, :], v_f[:, t, :], fv_hi[:, t, :].bitcast(F), ALU.subtract).then_inc(vf_lo, 1)
            dve.wait_ge(tile_done, N_FOX)
            for t, bank in enumerate((S[4], O, Z[0], Z[1])):
                dve.tensor_tensor(v2_f[:, t, :, :].rearrange("p b d -> p (b d)"), bank[:, 0:256], vb[:, BR_W:BR_W + 256], ALU.add) \
                    .then_inc((v2_ready, v2_ready, *z_free)[t], 1)
            for z in range(2):
                dve.wait_ge(z_free[z], 1)
            for a in range(2):
                dve.wait_ge(v2_hi, a + 1)
                dve.tensor_tensor(vn_lo[:, :, a, :, 64 * a:64 * a + 64],
                                  v2_f[:, :, :, 64 * a:64 * a + 64].rearrange("p t b d -> p b t d"),
                                  vn_hi[:, :, a, :, 64 * a:64 * a + 64].bitcast(F), ALU.subtract).then_inc(v2_lo, 1)

            with dve.Fori(0, PAIRS) as i:
                T = T_FOX + 6 * i
                dve.wait_ge(q_hi_done, i + 1)
                sub_lo(q_lo[:, :], Z[0][:, :], cols1[:, ds(C_FQ + i, 1)], q_hi[:, :], z_free[0])
                dve.wait_ge(k_hi_done, i + 1)
                sub_lo(k_lo[:, :], Z[1][:, :], cols1[:, ds(C_FK + i, 1)], k_hi[:, :], z_free[1])
                order = [(0, 3), (0, 2), (0, 0), (1, 3), (1, 2), (1, 0), (0, 1), (1, 1)]
                dve.wait_ge(diag_ready, 2 * i + 2)
                dve.wait_ge(consts, N_CONST)
                for s, (a, t) in enumerate(order):
                    wait_scores(i, a, t)
                    k = P128 * t
                    op = mask_tile(a, t, k, k + P128, f_diag[:, a, t, :], mx2[:, a, t, 0:1])
                    if t:
                        op = mask_tile(a, t, 0, k, f_bias[:, a, 0:k], mx2[:, a, t, 1:2])
                op.then_inc(masked, 1)
                dve.wait_ge(masked, i + 1 + 1)
                dve.tensor_reduce(mx[:, :, :], mx2[:, :, :, :], AX.X, ALU.max).then_inc(neg_pre, 1)
                dve.wait_ge(neg_pre, i + 1)
                dve.tensor_scalar(neg_mx[:, :, :], mx[:, :, :], -1.0, None, ALU.mult).then_inc(neg_ready, 1)
                invert(i)
                dve.wait_ge(inv_ready, i + 1)
                normalise(i)
                dve.wait_ge(tile_done, T + 5)
                dve.wait_ge(z_free[1], Z_FOX[1] + 3 * i + 2)
                dve.scalar_tensor_tensor(conv_t[:, 2:SEQ + 2], Z[0][:, :], cols1[:, ds(C_CX + i, 1)], conv_c[:, :],
                                         ALU.add, ALU.mult).then_inc(z_free[0], 1)
                dve.wait_ge(z_free[0], Z_FOX[0] + 3 * i + 3)
                dve.memset(conv_t[:, 0:2], 0.0).then_inc(conv_t_done, 1)
                pt_low(i)
                dve.wait_ge(conv_w2, i + 1)
                for tap in (1, 0):
                    dve.scalar_tensor_tensor(conv_u[:, :], conv_t[:, tap:SEQ + tap], cols1[:, ds(C_SC + 4 * tap + i, 1)], conv_u[:, :],
                                             ALU.mult, ALU.add).then_inc(conv_step, 1)
                    dve.wait_ge(conv_step, 3 * i + 2 - tap + 1)
                dve.tensor_tensor(conv_c[:, :], conv_u[:, :], conv_b[:, :], ALU.mult).then_inc(conv_step, 1)
                dve.wait_ge(nk_hi_done, i + 1)
                sub_lo(nk_lo[:, i, :], Z[1][:, :], cols1[:, ds(C_NK + i, 1)], nk_hi[:, i, :], z_free[1])
                dve.wait_ge(conv_hi, i + 1)
                dve.tensor_tensor(br_lo[:, PAIRS + i, :], conv_c[:, :], br_hi[:, PAIRS + i, :].bitcast(F), ALU.subtract).then_inc(conv_lo, 1)
                dve.wait_ge(o_hi_done, i + 1)
                dve.tensor_tensor(br_lo[:, i, :], O[:, :], br_hi[:, i, :].bitcast(F), ALU.subtract).then_inc(o_lo_done, 1)

            dve.wait_ge(pv_done, PAIRS + 1)
            dve.wait_ge(z_free[1], Z_NSA[1])
            for b, pe_col, pe_cols in ((0, C_PEK, cols1), (1, C_PEV, cols2)):
                if b:
                    dve.wait_ge(blk_ready, 2)
                dve.tensor_tensor(kc_f[:, :], nk_hi[:, b, :].bitcast(F), nk_lo[:, b, :].bitcast(F), ALU.add).then_inc(kcf, 1)
                dve.memset(blk[:, b, :, CMP_LEN - 1:CMP_LEN], 0.0)
                dve.wait_ge(kcf, b + 1)
                tok = kc_f[:, :].rearrange("p (c l) -> p l c", l=CMP_STRIDE)
                nw = CMP_LEN - 1
                for h in range(2):
                    dve.tensor_tensor(blk[:, b, CMP_STRIDE * h:CMP_STRIDE * (h + 1), 0:nw], tok[:, :, h:h + nw],
                                      pe_cols[:, pe_col + CMP_STRIDE * h:pe_col + CMP_STRIDE * (h + 1)]
                                      .rearrange("p (l o) -> p l o", o=1).to_broadcast([P128, CMP_STRIDE, nw]), ALU.add) \
                        .then_inc(blk_ready, 1)
            dve.wait_ge(cmp_hi, 1)
            dve.tensor_tensor(kc_lo[:, :], S[2][:, 0:CMP_LEN], kc_hi[:, :].bitcast(F), ALU.subtract).then_inc(cmp_lo, 1)
            dve.wait_ge(cmp_hi, 2)
            dve.tensor_tensor(vc_lo[:, :], S[3][0:64, 0:P128], vc_hi[:, :].bitcast(F), ALU.subtract).then_inc(cmp_lo, 1)
            dve.wait_ge(alibi_ready, 5)

            with dve.Fori(0, PAIRS) as i:
                T = T_NSA + 10 * i
                z0, z1 = Z_NSA[0] + 5 * i, Z_NSA[1] + 5 * i

                def softmax_scores(pair):
                    for a, t in [(0, 3), (0, 2), (0, 0), (1, 3), (1, 2), (1, 0), (0, 1), (1, 1)]:
                        wait_scores(pair, a, t)
                        op = mask_tile(a, t, 0, P_LEN[t], alibi[:, a, SEQ - P_LEN[t]:SEQ], mx[:, a, t:t + 1])
                    op.then_inc(masked, 1)
                    dve.wait_ge(masked, pair + 1 + 1)
                    dve.tensor_scalar(neg_mx[:, :, :], mx[:, :, :], -1.0, None, ALU.mult).then_inc(neg_ready, 1)

                def gate_inv(pair, br):
                    invert(pair)
                    dve.wait_ge(inv_ready, pair + (pair - PAIRS) + 1)
                    g = gates[:, br, :, :].rearrange("p (a h) t -> p a h t", a=2)[:, :, ds(i, 1), :] \
                        .rearrange("p a h t -> p a (h t)")
                    dve.tensor_tensor(p_inv[:, :, :], p_inv[:, :, :], g, ALU.mult).then_inc(inv_ready, 1)
                    dve.wait_ge(inv_ready, pair + (pair - PAIRS) + 2)

                dve.wait_ge(q_hi_done, PAIRS + i + 1)
                sub_lo(q_lo[:, :], Z[0][:, :], cols1[:, ds(C_NQ + i, 1)], q_hi[:, :], z_free[0])
                softmax_scores(PAIRS + 2 * i)
                flat = "p t a c -> p (t a) c"
                cp = c_p[:, :, :, :].rearrange(flat)
                dve.wait_ge(c_t, i + 1)
                dve.wait_ge(c_scored, i + 1)
                dve.scalar_tensor_tensor(c_p[:, :, :, :].rearrange("p t a c -> p (t a c)"), O[:, 0:256], SCALE,
                                         c_bias[:, :, :, :].rearrange("p t a c -> p (t a c)"), ALU.mult, ALU.add).then_inc(c_step, 1)
                dve.wait_ge(c_step, 5 * i + 1)
                dve.tensor_reduce(c_mx[:, :, :].rearrange("p t a -> p (t a)"), cp, AX.X, ALU.max).then_inc(c_step, 1)
                dve.wait_ge(c_step, 5 * i + 2)
                dve.tensor_tensor(cp, cp, c_mx[:, :, :].rearrange("p t (a o) -> p (t a) o", o=1).to_broadcast([P128, 2 * QT, CMP_LEN]),
                                  ALU.subtract).then_inc(c_step, 1)
                gate_inv(PAIRS + 2 * i, 1)
                normalise(PAIRS + 2 * i)
                dve.wait_ge(c_exp, i + 1)
                dve.tensor_reduce(c_sum[:, :, :].rearrange("p t a -> p (t a)"), cp, AX.X, ALU.add).then_inc(c_red, 1)
                dve.wait_ge(c_red, 4 * i + 1)
                dve.reciprocal(c_sum[:, :, :], c_sum[:, :, :]).then_inc(c_red, 1)
                dve.wait_ge(c_red, 4 * i + 2)
                dve.tensor_tensor(c_sum[:, :, :], c_sum[:, :, :],
                                  gates[:, 0, :, :].rearrange("p (a h) t -> p h t a", a=2)[:, ds(i, 1), :, :]
                                  .rearrange("p h t a -> p (h t) a"), ALU.mult).then_inc(c_red, 1)
                dve.tensor_tensor(cp, cp, c_mask[:, :, :, :].rearrange(flat), ALU.mult).then_inc(c_red, 1)
                dve.wait_ge(c_red, 4 * i + 4)
                dve.tensor_tensor(cp, cp, c_sum[:, :, :].rearrange("p t (a o) -> p (t a) o", o=1).to_broadcast([P128, 2 * QT, CMP_LEN]),
                                  ALU.mult).then_inc(c_ready, 1)

                def gated(m, t, z_a, z_b):
                    dve.wait_ge(z_free[1], z_a)
                    dve.wait_ge(tile_done, t + 1)
                    dve.scalar_tensor_tensor(mix[:, m, :], g_a[:, :], 1.0, Z[1][:, :], ALU.add, ALU.mult).then_inc(z_free[1], 1)
                    dve.wait_ge(z_free[0], z_b)
                    dve.wait_ge(tile_done, t + 2)
                    dve.scalar_tensor_tensor(g_b[:, :], g_b[:, :], 1.0, Z[0][:, :], ALU.add, ALU.mult).then_inc(z_free[0], 1)
                    dve.wait_ge(z_free[1], z_a + 1)
                    dve.wait_ge(z_free[0], z_b + 1)
                    dve.tensor_tensor(mix[:, m, :], mix[:, m, :], g_b[:, :], ALU.add).then_inc(gb_used, 1)

                gated(2 * i, T + 3, z1 + 1, z0 + 2)
                pt_low(PAIRS + 2 * i)
                dve.wait_ge(c_t_hi, i + 1)
                dve.tensor_tensor(c_pt_lo[:, :], O[0:64, :], c_pt_hi[:, :].bitcast(F), ALU.subtract).then_inc(c_t_lo, 1)
                dve.wait_ge(pv_s_done, i + 1)
                softmax_scores(PAIRS + 2 * i + 1)
                dve.wait_ge(masked, PAIRS + 2 * i + 2 + 1)
                dve.tensor_scalar(alibi[:, :, :], alibi[:, :, :], 0.5, None, ALU.mult).then_inc(c_step, 1)
                dve.tensor_scalar(c_bias[:, :, :, :], c_bias[:, :, :, :], 0.5, None, ALU.mult).then_inc(c_step, 1)
                dve.wait_ge(c_step, 5 * i + 5)
                gate_inv(PAIRS + 2 * i + 1, 2)
                normalise(PAIRS + 2 * i + 1)
                gated(2 * i + 1, T + 7, z1 + 3, z0 + 4)
                pt_low(PAIRS + 2 * i + 1)
                dve.wait_ge(o_hi_done, PAIRS + i + 1)
                dve.tensor_tensor(c_lo[:, i, :], O[:, :], c_hi[:, i, :].bitcast(F), ALU.subtract).then_inc(o_lo_done, 1)

            tau = 0
            for kind, m in MIX_ORDER:
                if kind == "gc":
                    tau += 1
                    continue
                for mt in (m, m + 1):
                    z = tau % 2
                    dve.wait_ge(z_free[z], Z_MIX[z] + tau // 2)
                    dve.wait_ge(tile_done, T_MIX + tau + 1)
                    g = g_c[:, mt % PAIRS, :]
                    dve.scalar_tensor_tensor(g, g, 1.0, Z[z][:, :], ALU.add, ALU.mult).then_inc(z_free[z], 1)
                    dve.wait_ge(z_free[z], Z_MIX[z] + tau // 2 + 1)
                    dve.tensor_tensor(mix[:, mt, :], mix[:, mt, :], g, ALU.add).then_inc(mix_done, 1)
                    dve.wait_ge(mix_hi, mt + 1)
                    dve.scalar_tensor_tensor(br_lo[:, mt, :], mix[:, mt, :], 0.5, br_hi[:, mt, :].bitcast(F),
                                             ALU.mult, ALU.subtract).then_inc(mix_lo, 1)
                    tau += 1
            for m in range(KT):
                z = m % 2
                dve.wait_ge(xr_copied, m + 1)
                dve.wait_ge(tile_done, T_WO + m + 1)
                dve.tensor_tensor(x2[:, m, :], Z[z][:, :], x2[:, m, :], ALU.add).then_inc(z_free[z], 1)
                dve.wait_ge(z_free[z], Z_WO[z] + m // 2 + 1)
                if m:
                    dve.wait_ge(acc_done, m)
                sq = x_sq if m else x_acc
                dve.tensor_tensor(sq[:, :], x2[:, m, :], x2[:, m, :], ALU.mult).then_inc(sq_done if m else acc_done, 1)
                if m:
                    dve.wait_ge(sq_done, m)
                    dve.tensor_tensor(x_acc[:, :], x_acc[:, :], x_sq[:, :], ALU.add).then_inc(acc_done, 1)
                dve.wait_ge(xg_hi, m + 1)
                dve.scalar_tensor_tensor(h_lo[:, m, :], x2[:, m, :], cols1[:, C_GFFN + m:C_GFFN + m + 1], h_hi[:, m, :].bitcast(F),
                                         ALU.mult, ALU.subtract).then_inc(xg_lo, 1)
            dve.memset(u_t[:, 0:2], 0.0).then_inc(rs_ready, 1)
            dve.wait_ge(rs_sqrt, 1)
            dve.reciprocal(rstd[:, :], rstd[:, :]).then_inc(rs_ready, 1)
            dve.wait_ge(rs_ready, 2)

            with dve.Fori(0, FT) as i:
                T = T_UP + 2 * i
                dve.wait_ge(u_step, 2 * i + 1)
                dve.wait_ge(tile_done, T + 1)
                dve.tensor_tensor(u_t[:, 2:SEQ + 2], Z[0][:, :], rstd[:, :], ALU.mult).then_inc(z_free[0], 1)
                dve.wait_ge(z_free[0], Z_UP[0] + i + 1)
                dve.memset(u_t[:, 0:2], 0.0).then_inc(u_ready, 1)
                dve.wait_ge(u_w2, i + 1)
                for tap in (1, 0):
                    dve.scalar_tensor_tensor(u_c[:, :], u_t[:, tap:SEQ + tap], cols2[:, ds(C_FFN + FT * tap + i, 1)], u_c[:, :],
                                             ALU.mult, ALU.add).then_inc(u_step, 1)
                    dve.wait_ge(u_step, 2 * i + 2 - tap + 1)
                dve.wait_ge(tile_done, T + 2)
                dve.tensor_tensor(v_t[:, :], Z[1][:, :], rstd[:, :], ALU.mult).then_inc(z_free[1], 1)
                dve.wait_ge(z_free[1], Z_UP[1] + i + 1)
                dve.wait_ge(u_silu, i + 1)
                dve.tensor_tensor(u_c[:, :], u_c[:, :], v_t[:, :], ALU.mult).then_inc(uv_done, 1)
                dve.wait_ge(act_hi_done, i + 1)
                dve.tensor_tensor(act_lo[:, i, :], u_c[:, :], act_hi[:, i, :].bitcast(F), ALU.subtract).then_inc(act_lo_done, 1)

            for m in range(KT):
                dve.wait_ge(down_done, m + 1)
                dve.tensor_tensor(x2[:, m, :], banks[m][:, :], x2[:, m, :], ALU.add).then_inc(x3_done, 1)
            dve.wait_ge(y_sqd, 2 * QT)
            dve.tensor_tensor(stat[:, 2, :], stat[:, 0, :], stat[:, 1, :], ALU.add).then_inc(y_ms, 1)
            dve.wait_ge(y_ms, 1)
            dve.tensor_scalar(stat[:, 2, :], stat[:, 2, :], 1.0 / D_MODEL, EPS, ALU.mult, ALU.add).then_inc(y_ms, 1)
            dve.wait_ge(y_sqrt, 1)
            dve.reciprocal(stat[:, 3, :], stat[:, 2, :]).then_inc(y_rs, 1)
            dve.wait_ge(y_rs, 1)
            dve.wait_ge(g_loaded, 16)
            for n in range(2 * QT):
                t, h = n // 2, n % 2
                if n >= 2:
                    dve.wait_ge(y_stored[h], 16 * (n // 2))
                dve.scalar_tensor_tensor(y_out[:, h, :], banks[QT * h + t][:, :], stat[:, 3, t:t + 1],
                                         g_out[:, BR_W * h:BR_W * h + BR_W], ALU.mult, ALU.mult).then_inc(y_done, 1)


_INS = ["x", "norm_mix_g", "w_in", "b_in", "cmp_pe_k", "cmp_w1_k", "cmp_w2_k", "cmp_pe_v", "cmp_w1_v",
        "cmp_w2_v", "sc_conv_w", "w_br_a", "w_br_b", "w_br_c", "w_o", "norm_ffn_g", "w_up", "ffn_conv_w",
        "w_down", "norm_final_g"]


def kernel(**inputs):
    import numpy as np
    import concourse.bacc as bacc
    from concourse import mybir
    from concourse.bass_utils import run_bass_kernel_spmd

    nc = bacc.Bacc("TRN2", target_bir_lowering=False, num_devices=1, dynamic_dma_scratch_size=1024)
    arrays, args = {}, []
    for name in _INS:
        a = np.ascontiguousarray(inputs[name])
        arrays[f"in_{name}"] = a
        args.append(nc.dram_tensor(f"in_{name}", a.shape, mybir.dt.from_np(a.dtype), kind="ExternalInput").ap())
    out = nc.dram_tensor("out_0", (1, SEQ, D_MODEL), mybir.dt.float32, kind="ExternalOutput").ap()
    hybrid_block(nc, *args, out)
    r = run_bass_kernel_spmd(nc, [arrays], core_ids=[0])
    return r.results[0]["out_0"]
```

```python
import concourse.bass as bass
from concourse import mybir
from contextlib import ExitStack

D_MODEL = 1024
SEQ = 512
HEAD_DIM = 64
FOX_HEADS = 8
NSA_HEADS = 8
BR_W = 512
D_FF = 2816
CMP_LEN = 32
CMP_STRIDE = 16
EPS = 1e-6
NEG = -8e30
SCALE = HEAD_DIM ** -0.5

P128 = 128
KT = D_MODEL // P128
QT = SEQ // P128
FT = D_FF // P128
PAIRS = FOX_HEADS // 2
CH = KT * P128

O_GA, O_GB, O_GC = 0, D_MODEL, 2 * D_MODEL
O_FQ = 3 * D_MODEL
O_FK = O_FQ + BR_W
O_FV = O_FK + BR_W
O_FF = O_FV + BR_W
O_CB = O_FF + FOX_HEADS
O_CC = O_CB + BR_W
O_CX = O_CC + BR_W
O_NQ = O_CX + BR_W
O_KC = O_NQ + BR_W
O_VC, O_KS, O_VS, O_KW, O_VW = (O_KC + P128 * n for n in range(1, 6))
O_NG = O_VW + P128

C_GATE = 0
C_FQ, C_FK = 24, 28
C_CB, C_CC, C_CX = 32, 36, 40
C_NQ = 44
C_NK = 48
C_SC = 52
C_GMIX, C_GFFN = 64, 72
C_PEK = 80
N_COLS1 = C_PEK + CMP_LEN
C_FFN = 0
C_PEV = 3 * FT
N_COLS2 = C_PEV + CMP_LEN

N_FOX, T_FOX = 7, 7
N_CMP, T_CMP = N_FOX + 6 * PAIRS, T_FOX + 6 * PAIRS
N_NSA, T_NSA = N_CMP + 2, T_CMP + 2
N_MIX, T_MIX = N_NSA + 8 * PAIRS, T_NSA + 10 * PAIRS
N_WO, T_WO = N_MIX + 6, T_MIX + 10
N_UP, T_UP = N_WO + 8, T_WO + 8
N_DN, T_DN = N_UP + 2 * FT, T_UP + 2 * FT
N_END = N_DN + FT
NSA_TILES = (0, 1, 2, 3, 5, 6, 7, 9)
Z_FOX = (1, 1)
Z_CMP = tuple(z + 3 * PAIRS for z in Z_FOX)
Z_NSA = tuple(z + 1 for z in Z_CMP)
Z_MIX = tuple(z + 5 * PAIRS for z in Z_NSA)
Z_WO = tuple(z + 5 for z in Z_MIX)
Z_UP = tuple(z + 4 for z in Z_WO)

MIX_ORDER = (("gc", 6), ("yc", 0), ("yc", 2), ("gc", 7), ("yc", 4), ("yc", 6))

Y_DVE, Y_POOL = (0, 1, 2, 3, 6, 7), (4, 5)
Y_STORES = [(0, 1, 0), (0, 2, 1), (1, 1, 4), (0, 3, 2), (0, 4, 3), (1, 2, 5), (0, 5, 6), (0, 6, 7)]

N_BLK = SEQ // CMP_STRIDE
CZ_W = 2 * N_BLK + 2

P_LEN = [P128 * (i + 1) for i in range(QT)]
P_OFF = [0, 128, 384, 768]
P_ALL = sum(P_LEN)
T_LEN = [SEQ - P128 * j for j in range(QT)]
T_OFF = [0, 512, 1024, 896]


def hybrid_block(nc, x, norm_mix_g, w_in, b_in, cmp_pe_k, cmp_w1_k, cmp_w2_k, cmp_pe_v, cmp_w1_v,
                 cmp_w2_v, sc_conv_w, w_br_a, w_br_b, w_br_c, w_o, norm_ffn_g, w_up, ffn_conv_w,
                 w_down, norm_final_g, out):
    F = mybir.dt.float32
    R = mybir.dt.float32r
    ACT = mybir.ActivationFunctionType
    ALU = mybir.AluOpType
    AX = mybir.AxisListType
    ds = bass.ds

    w_in, b_in = w_in[0], b_in[0]
    w_o, w_up, w_down = w_o[0], w_up[0], w_down[0]
    w_br = [w_br_a[0], w_br_b[0], w_br_c[0]]

    with ExitStack() as ctx:
        def sb(name, shape, dt=F, scope=ctx):
            return scope.enter_context(nc.sbuf_tensor(name, shape, dt))

        def sem(name):
            return ctx.enter_context(nc.semaphore(name))

        raw = sb("raw", [P128, 2, CH])
        w_hi = sb("w_hi", [P128, 2, CH], R)
        w_lo = sb("w_lo", [P128, 2, CH], R)
        with ExitStack() as s:
            y_out = sb("y_out", [P128, 2 * QT, BR_W], F, s)
            y_raw = sb("y_raw", [P128, 2 * QT, BR_W], F, s)
        h_hi = sb("h_hi", [P128, KT, SEQ], R)
        h_lo = sb("h_lo", [P128, KT, SEQ], R)
        ident = sb("ident", [P128, P128])
        ones = sb("ones", [P128, P128])
        cols1 = sb("cols1", [P128, N_COLS1])
        cols2 = sb("cols2", [P128, N_COLS2])
        half_b = sb("half_b", [P128, 24])
        stat = sb("stat", [P128, 4, 4])
        eps_c = sb("eps_c", [P128, 1])
        act_cell = sb("act_cell", [P128, 5])
        wait_cell = sb("wait_cell", [P128, 5])
        with ExitStack() as s:
            x_in = sb("x_in", [P128, QT, D_MODEL], F, s)
            x_n = sb("x_n", [P128, QT, D_MODEL], F, s)
        with ExitStack() as s:
            v_f = sb("v_f", [P128, QT, BR_W], F, s)
            v2_f = sb("v2_f", [P128, QT, 2, P128], F, s)
        br_hi = sb("br_hi", [P128, 2 * PAIRS, SEQ], R)
        br_lo = sb("br_lo", [P128, 2 * PAIRS, SEQ], R)

        att = ExitStack()
        q_hi = sb("q_hi", [P128, SEQ], R, att)
        q_lo = sb("q_lo", [P128, SEQ], R, att)
        nk_hi = sb("nk_hi", [P128, 4, SEQ], R, att)
        nk_lo = sb("nk_lo", [P128, 4, SEQ], R, att)
        vn_hi = sb("vn_hi", [P128, 2, 2, QT, P128], R, att)
        vn_lo = sb("vn_lo", [P128, 2, 2, QT, P128], R, att)
        with ExitStack() as s:
            rows1 = sb("rows1", [N_COLS1, P128], F, s)
            rows2 = sb("rows2", [N_COLS2, P128], F, s)
            fg = sb("fg", [32, SEQ], F, s)
            fe = sb("fe", [FOX_HEADS, SEQ], F, s)
            f_one = sb("f_one", [FOX_HEADS, SEQ], F, s)
        with ExitStack() as s:
            cz = sb("cz", [P128, 2, CMP_STRIDE, CZ_W], F, s)
            sel = sb("sel", [CZ_W, 2, 2 * N_BLK], F, s)
            hid_f = sb("hid_f", [CZ_W, 2, 2, HEAD_DIM], F, s)
            hid_k = sb("hid_k", [HEAD_DIM, 2 * N_BLK], F, s)
        with ExitStack() as s:
            p_f = sb("p_f", [P128, 2, P_ALL], F, s)
        pt_lo = sb("pt_lo", [P128, 2, P_ALL], R, att)
        pt_hi = sb("pt_hi", [P128, 2, P_ALL], R, att)
        mx2 = sb("mx2", [P128, 2, QT, 2], F, att)
        mx = sb("mx", [P128, 2, QT], F, att)
        neg_mx = sb("neg_mx", [P128, 2, QT], F, att)
        p_sum = sb("p_sum", [P128, 2, QT], F, att)
        p_inv = sb("p_inv", [P128, 2, QT], F, att)
        gates = sb("gates", [P128, 3, NSA_HEADS, QT], F, att)
        c_bias = sb("c_bias", [P128, QT, 2, CMP_LEN], F, att)
        c_mask = sb("c_mask", [P128, QT, 2, CMP_LEN], F, att)
        c_pad = sb("c_pad", [P128, QT + 1, 2, CMP_LEN], F, att)
        c_p = c_pad[:, 0:QT, :, :]
        c_mx = sb("c_mx", [P128, QT, 2], F, att)
        c_sum = sb("c_sum", [P128, QT, 2], F, att)
        c_pt_hi = sb("c_pt_hi", [64, SEQ], R, att)
        c_pt_lo = sb("c_pt_lo", [64, SEQ], R, att)
        kc_hi = sb("kc_hi", [P128, 2 * N_BLK], R, att)
        kc_lo = sb("kc_lo", [P128, 2 * N_BLK], R, att)
        vc_hi = sb("vc_hi", [64, P128], R, att)
        vc_lo = sb("vc_lo", [64, P128], R, att)
        with ExitStack() as s:
            fv_hi = sb("fv_hi", [P128, QT, BR_W], R, s)
            fv_lo = sb("fv_lo", [P128, QT, BR_W], R, s)
            vp_hi = sb("vp_hi", [P128, 2, QT, P128], R, s)
            vp_lo = sb("vp_lo", [P128, 2, QT, P128], R, s)
            k_hi = sb("k_hi", [P128, SEQ], R, s)
            k_lo = sb("k_lo", [P128, SEQ], R, s)
            f_bias = sb("f_bias", [P128, 2, SEQ], F, s)
            f_diag = sb("f_diag", [P128, 2, QT, P128], F, s)
            tri = sb("tri", [P128, P128], F, s)
            conv_b = sb("conv_b", [P128, SEQ], F, s)
            conv_c = sb("conv_c", [P128, SEQ], F, s)
            conv_t = sb("conv_t", [P128, SEQ + 2], F, s)
            conv_u = sb("conv_u", [P128, SEQ], F, s)
            fg_b = sb("fg_b", [32, 1], F, s)
            ng_t = sb("ng_t", [P128, QT, 32], F, s)
            vb = sb("vb", [P128, BR_W + 2 * P128], F, s)
            w1 = sb("w1", [P128, 2, CMP_STRIDE, 2, HEAD_DIM], F, s)
            w2k = sb("w2k", [HEAD_DIM, 2, P128], F, s)
            w2v = sb("w2v", [HEAD_DIM, HEAD_DIM], F, s)
            hid_v = sb("hid_v", [HEAD_DIM, 2, 2 * N_BLK], F, s)
        with ExitStack() as s:
            g_c = sb("g_c", [P128, KT, SEQ], F, s)
            mix = sb("mix", [P128, KT, SEQ], F, s)
            c_hi = sb("c_hi", [P128, PAIRS, SEQ], R, s)
            c_lo = sb("c_lo", [P128, PAIRS, SEQ], R, s)
            g_a = sb("g_a", [P128, SEQ], F, s)
            g_b = sb("g_b", [P128, SEQ], F, s)
            alibi = sb("alibi", [P128, 2, SEQ], F, s)
        att.close()

        ffn = ExitStack()
        x2 = sb("x2", [P128, KT, SEQ], F, ffn)
        with ExitStack() as s:
            x_r = sb("x_r", [P128, QT, D_MODEL], F, s)
        act_hi = sb("act_hi", [P128, FT, SEQ], R, ffn)
        act_lo = sb("act_lo", [P128, FT, SEQ], R, ffn)
        x_sq = sb("x_sq", [P128, SEQ], F, ffn)
        x_acc = sb("x_acc", [P128, SEQ], F, ffn)
        rstd = sb("rstd", [P128, SEQ], F, ffn)
        u_t = sb("u_t", [P128, SEQ + 2], F, ffn)
        u_c = sb("u_c", [P128, SEQ], F, ffn)
        v_t = sb("v_t", [P128, SEQ], F, ffn)
        g_out = sb("g_out", [P128, D_MODEL], F, ffn)
        ffn.close()

        S = [ctx.enter_context(nc.psum_tensor(f"s_bank{n}", [P128, SEQ], F)) for n in range(5)]
        O = ctx.enter_context(nc.psum_tensor("o_bank", [P128, SEQ], F))
        Z = [ctx.enter_context(nc.psum_tensor(f"z_bank{n}", [P128, SEQ], F)) for n in range(2)]
        banks = [*S, O, *Z]

        cum_dram = nc.dram_tensor("cum_scratch", [FOX_HEADS, SEQ], F, kind="Internal").ap()

        raw_loaded = [sem("raw_loaded0"), sem("raw_loaded1")]
        hi_split = sem("hi_split")
        lo_split = sem("lo_split")
        tile_done = sem("tile_done")
        z_free = [sem("z_free0"), sem("z_free1")]
        x_loaded = [sem(f"x_loaded{t}") for t in range(QT)]
        rows_loaded = sem("rows_loaded")
        small_loaded = sem("small_loaded")
        w1_loaded = sem("w1_loaded")
        consts = sem("consts")
        raw0_zero = sem("raw0_zero"); rows_zero = sem("rows_zero")
        cols_t = sem("cols_t")
        cols_ready = sem("cols_ready")
        x_ss = sem("x_ss"); x_ms = sem("x_ms"); x_sqrt = sem("x_sqrt"); x_rs = sem("x_rs")
        x_normed = sem("x_normed")
        x_t = sem("x_t")
        h_hi_done = sem("h_hi_done"); h_lo_done = sem("h_lo_done")
        fg_ready = sem("fg_ready")
        fe_step = sem("fe_step")
        cum_stored = sem("cum_stored")
        fbias_loaded = sem("fbias_loaded")
        
        ng_t_done = sem("ng_t_done"); ng_tanh = sem("ng_tanh"); gates_ready = sem("gates_ready")
        vf_ready = sem("vf_ready"); vf_hi = sem("vf_hi"); vf_lo = sem("vf_lo")
        v2_ready = sem("v2_ready"); v2_hi = sem("v2_hi"); v2_lo = sem("v2_lo")
        q_hi_done = sem("q_hi_done"); k_hi_done = sem("k_hi_done"); nk_hi_done = sem("nk_hi_done")
        vpad = sem("vpad"); diag_ready = sem("diag_ready")
        cb_done = sem("cb_done")
        conv_t_done = sem("conv_t_done"); conv_w2 = sem("conv_w2"); conv_step = sem("conv_step")
        conv_hi = sem("conv_hi"); conv_lo = sem("conv_lo")
        a1_scored = sem("a1_scored")
        scored = sem("scored")
        masked = sem("masked")
        neg_ready = sem("neg_ready")
        exp_done = sem("exp_done")
        inv_ready = sem("inv_ready")
        normed = sem("normed")
        pt_ready = sem("pt_ready")
        pt_hi_done = sem("pt_hi_done")
        pt_lo_done = sem("pt_lo_done")
        pv_s_done = sem("pv_s_done")
        pv_done = sem("pv_done")
        o_hi_done = sem("o_hi_done"); o_lo_done = sem("o_lo_done")
        cz_ready = sem("cz_ready"); hid_done = sem("hid_done"); hid_ready = sem("hid_ready"); sel_ready = sem("sel_ready"); hid_sum = sem("hid_sum")
        gelu_done = sem("gelu_done")
        cmp_done = sem("cmp_done"); cmp_hi = sem("cmp_hi"); cmp_lo = sem("cmp_lo")
        c_scored = sem("c_scored"); c_step = sem("c_step"); c_exp = sem("c_exp")
        c_ready = sem("c_ready"); c_t = sem("c_t"); c_t_hi = sem("c_t_hi"); c_t_lo = sem("c_t_lo")
        alibi_ready = sem("alibi_ready"); alibi_scaled = sem("alibi_scaled")
        mixed_a = sem("mixed_a"); mix_done = sem("mix_done"); gb_used = sem("gb_used")
        yc_free = sem("yc_free")
        mix_hi = sem("mix_hi"); mix_lo = sem("mix_lo"); gc_done = sem("gc_done")
        xr_loaded = sem("xr_loaded"); xr_t = sem("xr_t"); xr_copied = sem("xr_copied");
        xg_hi = sem("xg_hi"); xg_lo = sem("xg_lo"); sq_done = sem("sq_done"); acc_done = sem("acc_done")
        ss_done = sem("ss_done"); rs_sqrt = sem("rs_sqrt"); rs_ready = sem("rs_ready")
        u_ready = sem("u_ready"); u_w2 = sem("u_w2"); u_step = sem("u_step"); u_silu = sem("u_silu")
        v_ready = sem("v_ready"); uv_done = sem("uv_done"); act_hi_done = sem("act_hi_done"); act_lo_done = sem("act_lo_done")
        down_done = sem("down_done"); x3_done = sem("x3_done"); x3_t = sem("x3_t")
        y_sqd = sem("y_sqd"); y_ms = sem("y_ms"); y_sqrt = sem("y_sqrt"); y_rs = sem("y_rs")
        g_loaded = sem("g_loaded")
        y_scaled = sem("y_scaled"); y_dve = sem("y_dve"); y_pool = sem("y_pool"); y_stored = sem("y_stored")

        neg_pre = sem("neg_pre")
        c_red = sem("c_red")
        eps_ready = sem("eps_ready")
        N_CONST = 23
        K_ORDER = (0, 2, 3, 4, 5, 6, 7, 1)
        x_bank = [banks[(k + 6) % KT] for k in range(KT)]

        def pt_part(tile, b):
            if b < 4:
                return tile[:, b // 2, SEQ * (b % 2):SEQ * (b % 2) + SEQ], S[b][:, :]
            return tile[:, :, 2 * SEQ:P_ALL], S[4][:, :].rearrange("p (a q) -> p a q", a=2)

        block = ctx.enter_context(nc.Block())

        w_k = w_in.rearrange("(k p) n -> p k n", p=P128)
        up_k = w_up.rearrange("(k p) n -> p k n", p=P128)
        wo_k = w_o.rearrange("(k p) n -> p k n", p=P128)

        @block.sync
        def _(sp):
            def view(slot, k):
                return raw[:, slot, :].rearrange("p (k m) -> p k m", k=k)

            def raw_free(n):
                if not isinstance(n, int) or n >= 2:
                    sp.wait_ge(lo_split, n - 1)

            def load8(n, slot, src, col):
                raw_free(n)
                for h in range(2):
                    sp.dma_start(view(slot, KT)[:, 4 * h:4 * h + 4, :],
                                 src[:, 4 * h:4 * h + 4, ds(col, P128)]).then_inc(raw_loaded[slot], 16)

            def load_nq(n, slot, t):
                raw_free(n)
                for g in range(2):
                    sp.dma_start(view(slot, KT)[:, :, 64 * g:64 * g + 64],
                                 w_k[:, :, ds(O_NQ + 256 * g + HEAD_DIM * t, HEAD_DIM)]).then_inc(raw_loaded[slot], 16)

            def load_ab(n, slot, m):
                raw_free(n)
                for b in range(2):
                    sp.dma_start(view(slot, KT)[:, 4 * b:4 * b + 4, :],
                                 w_br[b].rearrange("(k p) n -> p k n", p=P128)[:, :, ds(P128 * m, P128)]) \
                        .then_inc(raw_loaded[slot], 16)

            x_v = x[0].rearrange("(t p) n -> p t n", p=P128)
            rows = [(0, 32, b_in[O_GA:O_FV]), (C_CB, 12, b_in[O_CB:O_NQ]),
                    (C_NK, 3, b_in[O_KC:O_VS]), (C_NK + 3, 1, b_in[O_KW:O_VW]),
                    (C_SC, 12, sc_conv_w[0].rearrange("k n -> (k n)")), (C_GMIX, KT, norm_mix_g[0]),
                    (C_GFFN, KT, norm_ffn_g[0])]
            for t in range(QT):
                sp.dma_start(x_in[:, t, :], x_v[:, t, :]).then_inc(x_loaded[t], 16)
            sp.wait_ge(raw0_zero, 1)
            for c, o, n in ((0, O_FF, FOX_HEADS), (FOX_HEADS, O_NG, 3 * NSA_HEADS)):
                sp.dma_start(view(0, KT)[:, :, c:c + n], w_k[:, :, o:o + n]).then_inc(raw_loaded[0], 16)

            sp.wait_ge(rows_zero, 2)
            for c, n, src in rows:
                sp.dma_start(rows1[c:c + n, :], src.rearrange("(r m) -> r m", m=P128)).then_inc(rows_loaded, 16)
            for g in range(2):
                sp.dma_start(rows1[C_NQ:C_NQ + PAIRS, 64 * g:64 * g + 64],
                             b_in[O_NQ + 256 * g:O_NQ + 256 * g + 256].rearrange("(r m) -> r m", m=HEAD_DIM)) \
                    .then_inc(rows_loaded, 16)
            sp.dma_start(rows1[C_PEK:C_PEK + CMP_LEN, 0:HEAD_DIM], cmp_pe_k[0]).then_inc(rows_loaded, 16)
            sp.dma_start(rows2[C_PEV:C_PEV + CMP_LEN, 0:HEAD_DIM], cmp_pe_v[0]).then_inc(rows_loaded, 16)
            sp.dma_start(rows2[0:C_PEV, :], ffn_conv_w[0].rearrange("k (r m) -> (k r) m", m=P128)).then_inc(rows_loaded, 16)
            def load_v(n):
                raw_free(n)
                for kk in range(2):
                    sp.dma_start(view(n % 2, 2)[:, kk, :], w_k[:, 2 * (n - 1) + kk, O_FV:O_FF]).then_inc(raw_loaded[n % 2], 16)

            load_v(1)
            bias_v = (b_in[O_FV:O_FF], b_in[O_VS:O_KW], b_in[O_VW:O_NG])
            o = 0
            for src in bias_v:
                n = src.shape[0]
                sp.dma_start(vb[:, o:o + n], src.rearrange("(a n) -> a n", a=1).to_broadcast([P128, n])).then_inc(small_loaded, 16)
                o += n
            sp.dma_start(fg_b[0:FOX_HEADS, :], b_in[O_FF:O_CB].rearrange("(n a) -> n a", a=1)).then_inc(small_loaded, 16)
            sp.dma_start(fg_b[FOX_HEADS:32, :], b_in[O_NG:O_NG + 24].rearrange("(n a) -> n a", a=1)).then_inc(small_loaded, 16)
            for n in range(2, 5):
                load_v(n)
                if n == 2:
                    continue
                b = n - 3
                for g in range(2):
                    for h in range(2):
                        sp.dma_start(w1[64 * g:64 * g + 64, b, :, h, :],
                                     (cmp_w1_k, cmp_w1_v)[b][0].rearrange("(h r d) m -> h d r m", h=2, d=HEAD_DIM)[h]) \
                            .then_inc(w1_loaded, 16)
                    if n == 3:
                        sp.wait_ge(consts, N_CONST)
                        sp.dma_start(w2k[:, g, 64 * g:64 * g + 64], cmp_w2_k[0]).then_inc(w1_loaded, 16)
            sp.dma_start(w2v[:, :], cmp_w2_v[0]).then_inc(w1_loaded, 16)
            for n in range(5, N_FOX):
                raw_free(n)
                for b, o in enumerate((O_VS, O_VW)):
                    sp.dma_start(view(n % 2, 4)[:, :, P128 * b:P128 * b + P128],
                                 w_k[:, 4 * (n - 5):4 * (n - 5) + 4, o:o + P128]).then_inc(raw_loaded[n % 2], 16)
            sp.wait_ge(fe_step, 6)
            sp.dma_start(cum_dram, fe[:, :]).then_inc(cum_stored, 16)
            sp.wait_ge(cum_stored, 16)
            with sp.Fori(0, PAIRS) as i:
                n = N_FOX + 6 * i
                load8(n, 1, w_k, O_FQ + P128 * i)
                sp.wait_ge(masked, i + 1)
                sp.dma_start(f_bias[:, :, :], cum_dram[ds(2 * i, 2), :].rearrange("(o h) n -> o h n", o=1)
                             .to_broadcast([P128, 2, SEQ])).then_inc(fbias_loaded, 16)
                load8(n + 1, 0, w_k, O_FK + P128 * i)
                load8(n + 2, 1, w_k, O_CB + P128 * i)
                load8(n + 3, 0, w_k, O_CC + P128 * i)
                load8(n + 4, 1, w_k, O_CX + P128 * i)
                load8(n + 5, 0, w_k, O_KC + P128 * i + P128 * ((i + 1) // 4))
            for c in range(2):
                load8(N_CMP + c, (N_CMP + c) % 2, w_k, O_GC + P128 * (4 + c))
            with sp.Fori(0, PAIRS) as i:
                n = N_NSA + 8 * i
                load_nq(n, 1, i)
                load8(n + 1, 0, w_k, O_GA + 2 * P128 * i)
                load8(n + 2, 1, w_k, O_GB + 2 * P128 * i)
                load_ab(n + 3, 0, 2 * i)
                load8(n + 4, 1, w_k, O_GA + P128 + 2 * P128 * i)
                load8(n + 5, 0, w_k, O_GB + P128 + 2 * P128 * i)
                load_ab(n + 6, 1, 2 * i + 1)
                load8(n + 7, 0, w_k, O_GC + P128 * i)

            def load_yc(n, m):
                raw_free(n)
                for g in range(2):
                    sp.dma_start(view(n % 2, 4)[64 * g:64 * g + 64, :, :],
                                 w_br[2].rearrange("(g t d) n -> g d t n", g=2, d=HEAD_DIM)[g, :, :, P128 * m:P128 * (m + 2)]) \
                        .then_inc(raw_loaded[n % 2], 16)

            n = N_MIX
            for step in MIX_ORDER:
                if step[0] == "yc":
                    load_yc(n, step[1])
                else:
                    load8(n, n % 2, w_k, O_GC + P128 * step[1])
                n += 1
                if step == ("yc", 2):
                    sp.wait_ge(pv_done, 2 * PAIRS + 1)
                    for t in range(QT):
                        sp.dma_start(x_r[:, t, :], x_v[:, t, :]).then_inc(xr_loaded, 16)
            for m in range(KT):
                load8(n, n % 2, wo_k, P128 * m)
                n += 1
            with sp.Fori(0, FT) as i:
                load8(N_UP + 2 * i, 1, up_k, P128 * i)
                load8(N_UP + 2 * i + 1, 0, up_k, D_FF + P128 * i)

            def load_down(n, slot, j):
                raw_free(n)
                for h in range(2):
                    sp.dma_start(view(slot, 2)[:, h, :], w_down[ds(P128 * j, P128), BR_W * h:BR_W * h + BR_W]) \
                        .then_inc(raw_loaded[slot], 16)

            with sp.Fori(0, FT // 2) as i:
                load_down(N_DN + 2 * i, 1, 2 * i)
                load_down(N_DN + 2 * i + 1, 0, 2 * i + 1)
            sp.dma_start(g_out[:, :], norm_final_g.rearrange("(a n) -> a n", a=1).to_broadcast([P128, D_MODEL])).then_inc(g_loaded, 16)
            out_v = out[0].rearrange("(t p) n -> p t n", p=P128)
            for done, count, n in Y_STORES:
                sp.wait_ge((y_dve, y_pool)[done], count)
                t, h = n % QT, n // QT
                sp.dma_start(out_v[:, t, BR_W * h:BR_W * h + BR_W], y_out[:, n, :]).then_inc(y_stored, 16)
            sp.wait_ge(y_stored, 16 * 2 * QT)

        @block.gpsimd
        def _(pool):
            def split_lo(slot, n):
                pool.wait_ge(hi_split, n + 1)
                pool.tensor_tensor(w_lo[:, slot, :], raw[:, slot, :], w_hi[:, slot, :].bitcast(F), ALU.subtract) \
                    .then_inc(lo_split, 1)

            pool.memset(rows1[:, HEAD_DIM:P128], 0.0).then_inc(rows_zero, 1)
            pool.memset(rows2[:, HEAD_DIM:P128], 0.0).then_inc(rows_zero, 1)
            pool.memset(raw[:, 0, :], 0.0).then_inc(raw0_zero, 1)
            pool.memset(ident[:, :], 0.0).then_inc(consts, 1)
            pool.memset(ones[:, :], 1.0).then_inc(consts, 1)
            pool.wait_ge(consts, 1)
            pool.affine_select(out=ident[:, :], in_=ident[:, :], compare_op=ALU.not_equal, fill=1.0,
                               base=0, pattern=[[-1, P128]], channel_multiplier=1).then_inc(consts, 1)
            pool.memset(tri[:, :], 0.0).then_inc(consts, 1)
            pool.memset(f_one[:, :], 1.0).then_inc(consts, 1)
            pool.memset(c_mask[:, :, :, :], 1.0).then_inc(consts, 1)
            pool.iota(c_bias[:, :, :, :], [[-P128, QT], [0, 2], [CMP_STRIDE, CMP_LEN]], base=CMP_LEN - 1,
                      channel_multiplier=-1, allow_small_or_imprecise_dtypes=True).then_inc(consts, 1)
            pool.wait_ge(consts, 7)
            pool.affine_select(out=tri[:, :], in_=tri[:, :], compare_op=ALU.is_ge, fill=NEG,
                               base=0, pattern=[[-1, P128]], channel_multiplier=1).then_inc(consts, 1)
            pool.affine_select(out=c_mask[:, :, :, :], in_=c_mask[:, :, :, :], compare_op=ALU.is_ge, fill=0.0,
                               base=1 - CMP_LEN, pattern=[[P128, QT], [0, 2], [-CMP_STRIDE, CMP_LEN]],
                               channel_multiplier=1).then_inc(consts, 1)
            for a in range(2):
                pool.tensor_scalar(c_bias[:, :, a, :], c_bias[:, :, a, :], 0.5 ** (1 + 4 * a), None, ALU.mult).then_inc(consts, 1)
            pool.wait_ge(consts, 11)
            pool.affine_select(out=c_bias[:, :, :, :], in_=c_bias[:, :, :, :], compare_op=ALU.is_ge, fill=4 * NEG,
                               base=1 - CMP_LEN, pattern=[[P128, QT], [0, 2], [-CMP_STRIDE, CMP_LEN]],
                               channel_multiplier=1).then_inc(consts, 1)
            pool.memset(mx2[:, :, :, :], -3e38).then_inc(consts, 1)
            pool.memset(c_pad[:, QT:QT + 1, :, :], 0.0).then_inc(consts, 1)
            pool.memset(conv_t[:, 0:2], 0.0).then_inc(consts, 1)
            pool.memset(w2k[:, :, :], 0.0).then_inc(consts, 1)
            pool.memset(hid_v[:, :, :], 0.0).then_inc(consts, 1)
            split_lo(0, 0)
            split_lo(1, 1)
            for t in (vn_hi, vn_lo):
                pool.memset(t[:, :, :, :, :].bitcast(F), 0.0).then_inc(consts, 1)
            for t in (vp_hi, vp_lo):
                pool.memset(t[:, :, :, :].bitcast(F), 0.0).then_inc(consts, 1)
            for t in (vc_hi, vc_lo):
                pool.memset(t[:, :].bitcast(F), 0.0).then_inc(consts, 1)
            for n in range(2, N_FOX + 1):
                split_lo(n % 2, n)

            pool.wait_ge(vf_lo, QT)
            pool.wait_ge(consts, N_CONST)
            with pool.Fori(0, PAIRS) as i:
                n = N_FOX + 6 * i
                split_lo(0, n + 1)
                pool.wait_ge(pv_done, i + 1)
                for hl, (dst, src) in enumerate(((vp_hi, fv_hi), (vp_lo, fv_lo))):
                    for a in range(2):
                        pool.tensor_copy(dst[:, a, :, 64 * a:64 * a + 64],
                                         src[:, :, ds(P128 * i + 64 * a, 64)].bitcast(F)).then_inc(vpad, 1)
                split_lo(1, n + 2)
                pool.wait_ge(masked, i + 1)
                pool.wait_ge(fbias_loaded, 16 * i + 16)
                for a in range(2):
                    pool.tensor_tensor(f_diag[:, a, :, :], f_bias[:, a, :].rearrange("p (t m) -> p t m", m=P128),
                                       tri[:, :].rearrange("p (o m) -> p o m", o=1).to_broadcast([P128, QT, P128]), ALU.add) \
                        .then_inc(diag_ready, 1)
                split_lo(0, n + 3)
                split_lo(1, n + 4)
                split_lo(0, n + 5)
                split_lo(1, n + 6)
            assert N_NSA % 2 == 1 and N_END % 2 == 1
            for n in range(N_CMP + 1, N_NSA + 2):
                split_lo(n % 2, n)
            pool.wait_ge(masked, PAIRS + 1)
            pool.wait_ge(pv_done, PAIRS + 1)
            pool.wait_ge(conv_lo, PAIRS + 1)
            pool.wait_ge(cmp_done, 2)
            for a in range(2):
                pool.iota(alibi[:, a, :], [[1, SEQ]], base=P128 - SEQ, channel_multiplier=-1,
                          allow_small_or_imprecise_dtypes=True).then_inc(alibi_ready, 1)
            pool.wait_ge(alibi_ready, 2)
            pool.affine_select(out=alibi[:, :, :], in_=alibi[:, :, :], compare_op=ALU.is_ge, fill=64 * NEG,
                               base=SEQ - P128, pattern=[[0, 2], [-1, SEQ]], channel_multiplier=1).then_inc(alibi_ready, 1)
            with pool.Fori(0, (N_END - N_NSA - 2) // 2) as i:
                split_lo(1, N_NSA + 2 * i + 2)
                split_lo(0, N_NSA + 2 * i + 3)
            pool.wait_ge(g_loaded, 16)
            for c, n in enumerate(Y_POOL):
                pool.wait_ge(y_scaled, c + 1)
                h = n // QT
                pool.tensor_tensor(y_out[:, n, :], y_raw[:, n, :], g_out[:, BR_W * h:BR_W * h + BR_W], ALU.mult)                     .then_inc(y_pool, 1)

        @block.tensor
        def _(pe):
            def mm3(out, w, r, first, last):
                pe.matmul(out, w[0], r[0], start=first, stop=False)
                pe.matmul(out, w[0], r[1], start=False, stop=False)
                return pe.matmul(out, w[1], r[0], start=False, stop=last)

            def wt(slot, k, k_tiles=KT, m=0):
                wide = CH // k_tiles
                o = k * wide + m
                return w_hi[:, slot, o:o + P128], w_lo[:, slot, o:o + P128]

            def project(slot, z, n, z_count, act=(h_hi, h_lo), ready=None):
                pe.wait_ge(z_free[z], z_count)
                pe.wait_ge(lo_split, n + 1)
                for k in range(KT):
                    if ready:
                        pe.wait_ge(ready, k + 1)
                    mm = mm3(Z[z][:, :], wt(slot, k), (act[0][:, k, :], act[1][:, k, :]), k == 0, k == KT - 1)
                mm.then_inc(tile_done, 1)

            def branch(slot, z, n, z_count, br, k0):
                pe.wait_ge(z_free[z], z_count)
                pe.wait_ge(lo_split, n + 1)
                for k in range(PAIRS):
                    mm = mm3(Z[z][:, :], wt(slot, k0 + k), (br_hi[:, br + k, :], br_lo[:, br + k, :]), k == 0, k == PAIRS - 1)
                mm.then_inc(tile_done, 1)

            def scores(kh, kl, pair):
                def qk(a, i, bank, col):
                    rows = slice(64 * a, 64 * a + 64)
                    q = (q_hi[rows, P128 * i:P128 * i + P128], q_lo[rows, P128 * i:P128 * i + P128])
                    return mm3(S[bank][:, col:col + P_LEN[i]], q, (kh[rows, 0:P_LEN[i]], kl[rows, 0:P_LEN[i]]), True, True)
                qk(0, 1, 4, 0).then_inc(a1_scored, 1)
                qk(0, 3, 0, 0).then_inc(scored, 1)
                qk(0, 2, 1, 0)
                qk(0, 0, 1, P_LEN[2]).then_inc(scored, 1)
                qk(1, 3, 2, 0).then_inc(scored, 1)
                qk(1, 2, 3, 0)
                qk(1, 0, 3, P_LEN[2]).then_inc(scored, 1)
                pe.wait_ge(a1_scored, pair + 1)
                qk(1, 1, 4, P_LEN[1]).then_inc(scored, 1)

            def transposes(pair):
                pe.wait_ge(normed, pair + 1)
                def pt(a, j, bank, col):
                    for i in range(j, QT):
                        mm = pe.transpose(S[bank][:, col + P128 * (i - j):col + P128 * (i - j + 1)],
                                          p_f[:, a, P_OFF[i] + P128 * j:P_OFF[i] + P128 * (j + 1)], ident[:, :])
                    return mm
                for a in range(2):
                    pt(a, 0, 2 * a, 0).then_inc(pt_ready, 1)
                    pt(a, 1, 2 * a + 1, 0)
                    pt(a, 3, 2 * a + 1, T_LEN[1]).then_inc(pt_ready, 1)
                pt(0, 2, 4, 0)
                pt(1, 2, 4, T_LEN[2]).then_inc(pt_ready, 1)

            def product(vh, vl, pair, first, last):
                pe.wait_ge(pt_lo_done, 5 * pair + 5 + 1)
                for a in range(2):
                    for j in range(QT):
                        o = T_OFF[j]
                        mm = mm3(O[:, P128 * j:SEQ], (vh[:, a, j, :], vl[:, a, j, :]),
                                 (pt_hi[:, a, o:o + T_LEN[j]], pt_lo[:, a, o:o + T_LEN[j]]),
                                 first and a == 0 and j == 0, last and a == 1 and j == QT - 1)
                return mm

            for done in (pv_done, c_t):
                pe.sem_inc(done, 1)
            def x_tile(k, t):
                return pe.transpose(x_bank[k][:, P128 * t:P128 * t + P128], x_n[:, t, P128 * k:P128 * k + P128], ident[:, :])

            pe.wait_ge(consts, 3)
            for t in range(QT):
                pe.wait_ge(x_normed, t + 1)
                for k in K_ORDER[:-1]:
                    mm = x_tile(k, t)
                    if t == QT - 1:
                        mm.then_inc(x_t, 1)
            pe.wait_ge(rows_loaded, 16 * 12)
            pe.transpose(Z[1][:, 0:N_COLS1], rows1[:, :], ident[0:N_COLS1, 0:N_COLS1])
            pe.transpose(Z[1][:, P128:P128 + N_COLS2], rows2[:, :], ident[0:N_COLS2, 0:N_COLS2]).then_inc(cols_t, 1)
            pe.wait_ge(cols_ready, 2)
            for t in range(QT):
                mm = x_tile(K_ORDER[-1], t)
            mm.then_inc(x_t, 1)
            pe.wait_ge(lo_split, 1)
            for c, k in enumerate(K_ORDER):
                pe.wait_ge(h_lo_done, c + 1)
                mm = mm3(Z[0][:, :], wt(0, k), (h_hi[:, k, :], h_lo[:, k, :]), c == 0, c == KT - 1)
            mm.then_inc(tile_done, 1)
            for n in range(1, 5):
                pe.wait_ge(lo_split, n + 1)
                for kk in range(2):
                    k = 2 * (n - 1) + kk
                    w = [p[:, n % 2, BR_W * kk:BR_W * kk + BR_W] for p in (w_hi, w_lo)]
                    for t in range(QT):
                        toks = slice(P128 * t, P128 * t + P128)
                        mm = mm3(S[t][:, :], (h_hi[:, k, toks], h_lo[:, k, toks]), w, k == 0, k == KT - 1)
                mm.then_inc(tile_done, 1)
                if n == 1:
                    pe.wait_ge(fg_ready, 1)
                    for t in range(QT):
                        mm = pe.transpose(Z[1][:, 32 * t:32 * t + 32], fg[:, P128 * t:P128 * t + P128], ident[0:32, 0:32])
                    mm.then_inc(ng_t_done, 1)
            v2_bank = [S[4], O, Z[0], Z[1]]
            pe.wait_ge(ng_tanh, 1)
            for n in range(5, N_FOX):
                pe.wait_ge(lo_split, n + 1)
                for kk in range(4):
                    k = 4 * (n - 5) + kk
                    w = [p[:, n % 2, 256 * kk:256 * kk + 256] for p in (w_hi, w_lo)]
                    for t in range(QT):
                        toks = slice(P128 * t, P128 * t + P128)
                        mm = mm3(v2_bank[t][:, 0:256], (h_hi[:, k, toks], h_lo[:, k, toks]), w, k == 0, k == KT - 1)
                mm.then_inc(tile_done, 1)

            with pe.Fori(0, PAIRS) as i:
                n, z = N_FOX + 6 * i, 3 * i
                project(1, 0, n, Z_FOX[0] + z)
                project(0, 1, n + 1, Z_FOX[1] + z)
                project(1, 0, n + 2, Z_FOX[0] + z + 1)
                pe.wait_ge(z_free[1], Z_FOX[1] + z + 1)
                pe.wait_ge(vf_ready, QT)
                pe.wait_ge(v2_ready, 2)
                pe.wait_ge(pt_lo_done, 5 * i + 1)
                scores(k_hi, k_lo, i)
                project(0, 1, n + 3, Z_FOX[1] + z + 1)
                project(1, 0, n + 4, Z_FOX[0] + z + 2)
                transposes(i)
                project(0, 1, n + 5, Z_FOX[1] + z + 2)
                pe.wait_ge(vpad, 4 * i + 4)
                pe.wait_ge(o_lo_done, i + 1)
                product(vp_hi, vp_lo, i, True, True).then_inc(pv_done, 1)

            project(N_CMP % 2, 0, N_CMP, Z_CMP[0])
            pe.wait_ge(w1_loaded, 16 * 11)
            for b in range(2):
                pe.wait_ge(cz_ready, 3 * b + 3)
                for r in range(CMP_STRIDE):
                    mm = pe.matmul(S[b][0:CZ_W, 0:P128], cz[:, b, r, :], w1[:, b, r, :, :].rearrange("p h m -> p (h m)"),
                                   start=(r == 0), stop=(r == CMP_STRIDE - 1))
                mm.then_inc(hid_done, 1)
            pe.wait_ge(sel_ready, 2)
            for b in range(2):
                pe.wait_ge(hid_ready, b + 1)
                for h in range(2):
                    mm = pe.matmul(S[2 + b][0:64, 0:2 * N_BLK], hid_f[:, b, h, :], sel[:, h, :], start=(h == 0), stop=(h == 1))
                mm.then_inc(hid_sum, 1)
            project((N_CMP + 1) % 2, 1, N_CMP + 1, Z_CMP[1])
            pe.wait_ge(gelu_done, 1)
            for g in range(2):
                mm = pe.matmul(S[4][:, N_BLK * g:N_BLK * g + N_BLK], w2k[:, g, :], hid_k[:, N_BLK * g:N_BLK * g + N_BLK],
                               start=True, stop=True)
            mm.then_inc(cmp_done, 1)
            pe.wait_ge(gelu_done, 3)
            for g in range(2):
                mm = pe.matmul(O[0:64, 64 * g:64 * g + 64], hid_v[:, g, :], w2v[:, :], start=True, stop=True)
            mm.then_inc(cmp_done, 1)

            with pe.Fori(0, PAIRS) as i:
                n, z = N_NSA + 8 * i, 5 * i
                z0, z1 = Z_NSA[0] + z, Z_NSA[1] + z
                project(1, 0, n, z0)
                project(0, 1, n + 1, z1)
                pe.wait_ge(z_free[0], z0 + 1)
                pe.wait_ge(pt_lo_done, 5 * (PAIRS + 2 * i) + 1)
                pe.wait_ge(o_lo_done, PAIRS + i + 1)

                pe.wait_ge(cmp_lo, 2)
                scores(nk_hi[:, 2, :], nk_lo[:, 2, :], PAIRS + 2 * i)
                for t in range(QT):
                    toks = slice(P128 * t, P128 * t + P128)
                    mm = mm3(O[:, 64 * t:64 * t + 64], (q_hi[:, toks], q_lo[:, toks]), (kc_hi[:, :], kc_lo[:, :]), True, True)
                mm.then_inc(c_scored, 1)
                project(1, 0, n + 2, z0 + 1)
                branch(0, 1, n + 3, z1 + 1, 0, 0)
                branch(0, 0, n + 3, z0 + 2, PAIRS, 4)
                transposes(PAIRS + 2 * i)
                pe.wait_ge(consts, N_CONST)
                pe.wait_ge(c_ready, i + 1)
                for t in range(QT):
                    mm = pe.transpose(O[:, P128 * t:P128 * t + P128],
                                      c_pad[:, t:t + 2, :, :].rearrange("p t a c -> p (t a c)"), ident[:, :])
                mm.then_inc(c_t, 1)
                project(1, 1, n + 4, z1 + 2)
                pe.wait_ge(c_t_lo, i + 1)
                mm3(O[:, :], (vc_hi[:, :], vc_lo[:, :]), (c_pt_hi[:, :], c_pt_lo[:, :]), True, False)
                product(vn_hi[:, 0, :, :, :], vn_lo[:, 0, :, :, :], PAIRS + 2 * i, False, False).then_inc(pv_s_done, 1)
                scores(nk_hi[:, 3, :], nk_lo[:, 3, :], PAIRS + 2 * i + 1)
                project(0, 0, n + 5, z0 + 3)
                branch(1, 1, n + 6, z1 + 3, 0, 0)
                branch(1, 0, n + 6, z0 + 4, PAIRS, 4)
                transposes(PAIRS + 2 * i + 1)
                project(0, 1, n + 7, z1 + 4)
                product(vn_hi[:, 1, :, :, :], vn_lo[:, 1, :, :, :], PAIRS + 2 * i + 1, False, True).then_inc(pv_done, 1)

            n, tau = N_MIX, 0
            for kind, m in MIX_ORDER:
                if kind == "gc":
                    project(n % 2, tau % 2, n, Z_MIX[tau % 2] + tau // 2)
                    tau += 1
                else:
                    pe.wait_ge(lo_split, n + 1)
                    pe.wait_ge(o_lo_done, 2 * PAIRS + 1)
                    for mt in range(2):
                        pe.wait_ge(z_free[tau % 2], Z_MIX[tau % 2] + tau // 2)
                        for k in range(PAIRS):
                            mm = mm3(Z[tau % 2][:, :], wt(n % 2, k, 4, P128 * mt), (c_hi[:, k, :], c_lo[:, k, :]),
                                     k == 0, k == PAIRS - 1)
                        mm.then_inc(tile_done, 1)
                        tau += 1
                n += 1
            pe.wait_ge(xr_loaded, 16 * QT)
            for m in range(KT):
                if m >= 4:
                    pe.wait_ge(xr_copied, m - 3)
                for t in range(QT):
                    mm = pe.transpose(S[m % 4][:, P128 * t:P128 * t + P128], x_r[:, t, P128 * m:P128 * m + P128], ident[:, :])
                mm.then_inc(xr_t, 1)
                project((N_WO + m) % 2, m % 2, N_WO + m, Z_WO[m % 2] + m // 2, (br_hi, br_lo),
                        None if m else mix_lo)
            project(1, 0, N_UP, Z_UP[0], ready=xg_lo)
            pe.wait_ge(acc_done, KT)
            pe.matmul(S[4][:, :], ones[:, :], x_acc[:, :], start=True, stop=True).then_inc(ss_done, 1)
            project(0, 1, N_UP + 1, Z_UP[1])
            with pe.Fori(1, FT) as i:
                project(1, 0, N_UP + 2 * i, Z_UP[0] + i)
                project(0, 1, N_UP + 2 * i + 1, Z_UP[1] + i)

            def down(slot, n, j, first, last):
                pe.wait_ge(lo_split, n + 1)
                pe.wait_ge(act_lo_done, j + 1 + 1)
                act = (act_hi[:, j, :], act_lo[:, j, :])
                for m in range(KT):
                    if first and m >= 6:
                        pe.wait_ge(z_free[m - 6], Z_UP[m - 6] + FT)
                    mm = mm3(banks[m][:, :], wt(slot, m), act, first, last)
                mm.then_inc(tile_done, 1)

            down(1, N_DN, 0, True, False)
            down(0, N_DN + 1, 1, False, False)
            with pe.Fori(1, FT // 2 - 1) as i:
                down(1, N_DN + 2 * i, 2 * i, False, False)
                down(0, N_DN + 2 * i + 1, 2 * i + 1, False, False)
            down(1, N_DN + FT - 2, FT - 2, False, False)

            def back(m, t):
                return pe.transpose(banks[QT * (m // 4) + t][:, P128 * (m % 4):P128 * (m % 4) + P128],
                                    x2[:, m, P128 * t:P128 * t + P128], ident[:, :])

            pe.wait_ge(lo_split, N_END)
            pe.wait_ge(act_lo_done, FT + 1)
            for m in range(KT):
                mm3(banks[m][:, :], wt((N_END - 1) % 2, m), (act_hi[:, FT - 1, :], act_lo[:, FT - 1, :]), False, True).then_inc(down_done, 1)
                if m == 5:
                    pe.wait_ge(x3_done, 4)
                    for t in range(QT):
                        for k in range(4):
                            mm = back(k, t)
                        mm.then_inc(x3_t, 1)
            pe.wait_ge(x3_done, KT - 1)
            for t in range(QT - 1):
                for m in range(4, KT - 1):
                    back(m, t)
            pe.wait_ge(x3_done, KT)
            for t in range(QT - 1):
                back(KT - 1, t).then_inc(x3_t, 1)
            for m in range(4, KT):
                mm = back(m, QT - 1)
            mm.then_inc(x3_t, 1)

        @block.scalar
        def _(act):
            def split_hi(slot, n, tiles):
                act.wait_ge(raw_loaded[slot], 32 * (n // 2) + 32)
                act.wait_ge(tile_done, tiles)
                act.activation(w_hi[:, slot, :], raw[:, slot, :], ACT.Copy).then_inc(hi_split, 1)

            def split_hi_in_loop(slot, loads, tiles):
                act.wait_ge(raw_loaded[slot], 32 * loads)
                act.wait_ge(tile_done, tiles)
                act.activation(w_hi[:, slot, :], raw[:, slot, :], ACT.Copy).then_inc(hi_split, 1)

            def evac_hi(dst, src, done, bias=0.0):
                act.activation(dst, src, ACT.Identity, bias=bias).then_inc(done, 1)

            def exponentials(pair):
                act.wait_ge(neg_ready, pair + 1)
                for a in range(2):
                    for i in range(QT):
                        t = p_f[:, a, P_OFF[i]:P_OFF[i] + P_LEN[i]]
                        act.activation(t, t, ACT.Exp, bias=neg_mx[:, a, i:i + 1], accum_out=p_sum[:, a, i:i + 1]).then_inc(exp_done, 1)

            def pt_high(pair):
                for b in range(5):
                    act.wait_ge(pt_ready, 5 * pair + b + 1)
                    dst, src = pt_part(pt_hi, b)
                    act.activation(dst, src, ACT.Copy).then_inc(pt_hi_done, 1)

            act.wait_ge(eps_ready, 1)
            act.activation(act_cell[:, 0:1], eps_c[:, :], ACT.Sqrt)
            for t in range(QT):
                act.wait_ge(x_loaded[t], 16)
                act.activation(x_n[:, t, :], x_in[:, t, :], ACT.Square, accum_out=stat[:, 0, t:t + 1]).then_inc(x_ss, 1)
                act.wait_ge(x_ss, t + 1)
                act.activation(stat[:, 2, t:t + 1], stat[:, 0, t:t + 1], ACT.Sqrt, bias=eps_c[:, :], scale=1.0 / D_MODEL).then_inc(x_sqrt, 1)
            split_hi(0, 0, 0)
            act.wait_ge(cols_ready, 2)
            for c, k in enumerate(K_ORDER):
                act.wait_ge(x_t, c + 1)
                act.activation(h_hi[:, k, :], x_bank[k][:, :], ACT.Copy, scale=cols1[:, C_GMIX + k:C_GMIX + k + 1]).then_inc(h_hi_done, 1)
                if c == 3:
                    split_hi(1, 1, 0)
            act.wait_ge(small_loaded, 16 * 5)
            act.wait_ge(tile_done, 1)
            act.activation(fg[:, :], Z[0][0:32, :], ACT.Identity, bias=fg_b[:, :]).then_inc(fg_ready, 1)
            split_hi(0, 2, 1)
            act.wait_ge(fe_step, 1)
            act.activation(fe[:, :], fe[:, :], ACT.Exp).then_inc(fe_step, 1)
            act.wait_ge(fe_step, 2)
            act.activation(fe[:, :], fe[:, :], ACT.Ln, bias=1.0).then_inc(fe_step, 1)
            split_hi(1, 3, 2)
            act.wait_ge(ng_t_done, 1)
            act.activation(ng_t[:, :, :].rearrange("p t c -> p (t c)"), Z[1][:, 0:P128], ACT.Tanh, scale=0.5).then_inc(ng_tanh, 1)
            split_hi(0, 4, 3)
            split_hi(1, 5, 4)
            split_hi(0, 6, 5)
            for t in range(QT):
                act.wait_ge(vf_ready, t + 1)
                act.activation(fv_hi[:, t, :], v_f[:, t, :], ACT.Copy).then_inc(vf_hi, 1)
            split_hi(1, 7, 6)
            for z in range(2):
                act.wait_ge(z_free[z], 1)
            act.wait_ge(consts, N_CONST)
            for a in range(2):
                act.activation(vn_hi[:, :, a, :, 64 * a:64 * a + 64],
                               v2_f[:, :, :, 64 * a:64 * a + 64].rearrange("p t b d -> p b t d"), ACT.Copy).then_inc(v2_hi, 1)

            with act.Fori(0, PAIRS) as i:
                T, L = T_FOX + 6 * i, 3 * i
                split_hi_in_loop(0, L + 5, T)
                act.wait_ge(tile_done, T + 1)
                evac_hi(q_hi[:, :], Z[0][:, :], q_hi_done, cols1[:, ds(C_FQ + i, 1)])
                split_hi_in_loop(1, L + 5, T + 1)
                act.wait_ge(tile_done, T + 2)
                evac_hi(k_hi[:, :], Z[1][:, :], k_hi_done, cols1[:, ds(C_FK + i, 1)])
                split_hi_in_loop(0, L + 6, T + 2)
                act.wait_ge(conv_step, 3 * i + 1)
                act.wait_ge(tile_done, T + 3)
                act.activation(conv_b[:, :], Z[0][:, :], ACT.Identity, bias=cols1[:, ds(C_CB + i, 1)]).then_inc(z_free[0], 1)
                split_hi_in_loop(1, L + 6, T + 3)
                exponentials(i)
                act.wait_ge(tile_done, T + 4)
                act.wait_ge(conv_lo, i + 1)
                act.activation(conv_c[:, :], Z[1][:, :], ACT.Identity, bias=cols1[:, ds(C_CC + i, 1)]).then_inc(z_free[1], 1)
                split_hi_in_loop(0, L + 7, T + 4)
                split_hi_in_loop(1, L + 7, T + 5)
                pt_high(i)
                act.wait_ge(conv_t_done, i + 1)
                act.activation(conv_u[:, :], conv_t[:, 2:SEQ + 2], ACT.Copy, scale=cols1[:, ds(C_SC + 8 + i, 1)]).then_inc(conv_w2, 1)
                act.wait_ge(tile_done, T + 6)
                evac_hi(nk_hi[:, i, :], Z[1][:, :], nk_hi_done, cols1[:, ds(C_NK + i, 1)])
                act.wait_ge(conv_step, 3 * i + 3 + 1)
                act.activation(br_hi[:, PAIRS + i, :], conv_c[:, :], ACT.Copy).then_inc(conv_hi, 1)
                act.wait_ge(pv_done, i + 1 + 1)
                act.activation(br_hi[:, i, :], O[:, :], ACT.Copy).then_inc(o_hi_done, 1)

            def gate_c(m, z, tiles):
                act.wait_ge(tile_done, tiles)
                act.activation(g_c[:, m, :], Z[z][:, :], ACT.Tanh, bias=half_b[:, 16 + m:17 + m], scale=0.5).then_inc(z_free[z], 1)

            split_hi((N_CMP + 1) % 2, N_CMP + 1, T_CMP)
            act.wait_ge(vpad, 4 * PAIRS)
            gate_c(4, 0, T_CMP + 1)
            split_hi(N_NSA % 2, N_NSA, T_CMP + 1)
            act.activation(act_cell[:, 1:2], eps_c[:, :], ACT.Gelu_apprx_tanh)
            for b, dst in enumerate(([(hid_k[:, :], slice(0, 2 * N_BLK))],
                                     [(hid_v[:, g, N_BLK * g:N_BLK * g + N_BLK], slice(N_BLK * g, N_BLK * g + N_BLK)) for g in range(2)])):
                act.wait_ge(hid_sum, b + 1)
                for d, cols in dst:
                    act.activation(d, S[2 + b][0:64, cols], ACT.Gelu_apprx_tanh).then_inc(gelu_done, 1)
            act.activation(act_cell[:, 2:3], eps_c[:, :], ACT.Exp)
            gate_c(5, 1, T_CMP + 2)
            act.wait_ge(cmp_done, 1)
            act.activation(kc_hi[:, :], S[4][:, 0:2 * N_BLK], ACT.Copy).then_inc(cmp_hi, 1)
            act.wait_ge(cmp_done, 2)
            act.activation(vc_hi[:, :], O[0:64, 0:P128], ACT.Copy).then_inc(cmp_hi, 1)
            with act.Fori(0, PAIRS) as i:
                T, L = T_NSA + 10 * i, 4 * i + N_NSA // 2
                z0, z1 = Z_NSA[0] + 5 * i, Z_NSA[1] + 5 * i
                split_hi_in_loop(0, L + 2, T)
                act.wait_ge(tile_done, T + 1)
                evac_hi(q_hi[:, :], Z[0][:, :], q_hi_done, cols1[:, ds(C_NQ + i, 1)])
                split_hi_in_loop(1, L + 2, T + 1)

                def tanh_gate(dst, z, col):
                    act.activation(dst, Z[z][:, :], ACT.Tanh, bias=half_b[:, col], scale=0.5).then_inc(z_free[z], 1)

                act.wait_ge(z_free[1], z1 - 1)
                act.wait_ge(tile_done, T + 2)
                tanh_gate(g_a[:, :], 1, ds(2 * i, 1))
                split_hi_in_loop(0, L + 3, T + 2)
                exponentials(PAIRS + 2 * i)
                act.wait_ge(c_step, 5 * i + 3)
                act.activation(c_p[:, :, :, :], c_p[:, :, :, :], ACT.Exp).then_inc(c_exp, 1)
                act.wait_ge(gb_used, 2 * i + 1)
                act.wait_ge(tile_done, T + 3)
                tanh_gate(g_b[:, :], 0, ds(8 + 2 * i, 1))
                split_hi_in_loop(1, L + 3, T + 3)
                split_hi_in_loop(0, L + 4, T + 5)
                pt_high(PAIRS + 2 * i)
                act.wait_ge(c_t, i + 1 + 1)
                act.activation(c_pt_hi[:, :], O[0:64, :], ACT.Copy).then_inc(c_t_hi, 1)
                act.wait_ge(z_free[1], z1 + 2)
                act.wait_ge(tile_done, T + 6)
                tanh_gate(g_a[:, :], 1, ds(2 * i + 1, 1))
                split_hi_in_loop(1, L + 4, T + 6)
                exponentials(PAIRS + 2 * i + 1)
                act.wait_ge(gb_used, 2 * i + 1 + 1)
                act.wait_ge(tile_done, T + 7)
                tanh_gate(g_b[:, :], 0, ds(8 + 2 * i + 1, 1))
                split_hi_in_loop(0, L + 5, T + 7)
                split_hi_in_loop(1, L + 5, T + 9)
                pt_high(PAIRS + 2 * i + 1)
                act.wait_ge(tile_done, T + 10)
                tanh_gate(g_c[:, i, :], 1, ds(16 + i, 1))
                act.wait_ge(pv_done, PAIRS + i + 1 + 1)
                act.activation(c_hi[:, i, :], O[:, :], ACT.Copy).then_inc(o_hi_done, 1)

            def mix_high(m):
                act.wait_ge(mix_done, m + 1)
                act.activation(br_hi[:, m, :], mix[:, m, :], ACT.Copy, scale=0.5).then_inc(mix_hi, 1)

            n, tau = N_MIX, 0
            pending = []
            for kind, m in MIX_ORDER:
                split_hi((n + 1) % 2, n + 1, T_MIX + tau)
                for mt in pending:
                    mix_high(mt)
                pending = []
                if kind == "gc":
                    gate_c(m, tau % 2, T_MIX + tau + 1)
                    tau += 1
                else:
                    tau += 2
                    pending = [m, m + 1]
                n += 1
            for mt in pending:
                mix_high(mt)
            for m in range(KT):
                split_hi((N_WO + m + 1) % 2, N_WO + m + 1, T_WO + m)
                act.wait_ge(xr_t, m + 1)
                act.activation(x2[:, m, :], S[m % 4][:, :], ACT.Copy).then_inc(xr_copied, 1)
                act.wait_ge(z_free[m % 2], Z_WO[m % 2] + m // 2 + 1)
                act.activation(h_hi[:, m, :], x2[:, m, :], ACT.Copy, scale=cols1[:, C_GFFN + m:C_GFFN + m + 1]).then_inc(xg_hi, 1)
            split_hi((N_UP + 1) % 2, N_UP + 1, T_UP)
            act.wait_ge(ss_done, 1)
            act.activation(rstd[:, :], S[4][:, :], ACT.Sqrt, bias=eps_c[:, :], scale=1.0 / D_MODEL).then_inc(rs_sqrt, 1)

            act.activation(act_cell[:, 3:4], eps_c[:, :], ACT.Silu)
            with act.Fori(0, FT) as i:
                T, L = T_UP + 2 * i, i + N_UP // 2
                split_hi_in_loop(1, L + 2, T + 1)
                act.wait_ge(u_ready, i + 1)
                act.wait_ge(act_lo_done, i + 1)
                act.activation(u_c[:, :], u_t[:, 2:SEQ + 2], ACT.Copy, scale=cols2[:, ds(C_FFN + 2 * FT + i, 1)]).then_inc(u_w2, 1)
                act.wait_ge(u_step, 2 * i + 2 + 1)
                act.activation(u_c[:, :], u_c[:, :], ACT.Silu).then_inc(u_silu, 1)
                split_hi_in_loop(0, L + 3, T + 2)
                act.wait_ge(uv_done, i + 1)
                act.activation(act_hi[:, i, :], u_c[:, :], ACT.Copy).then_inc(act_hi_done, 1)
            T, L = T_DN, N_DN // 2
            with act.Fori(0, FT // 2 - 1) as i:
                split_hi_in_loop(1, L + i + 2, T + 2 * i + 1)
                split_hi_in_loop(0, L + i + 3, T + 2 * i + 2)
            act.activation(act_cell[:, 4:5], eps_c[:, :], ACT.Sqrt)
            for n in range(2 * QT):
                act.wait_ge(x3_t, n + 1)
                act.activation(y_raw[:, n, :], banks[n][:, :], ACT.Square, accum_out=stat[:, n // QT, n % QT:n % QT + 1]).then_inc(y_sqd, 1)
            act.wait_ge(y_ms, 1)
            act.activation(stat[:, 2, :], stat[:, 2, :], ACT.Sqrt, bias=eps_c[:, :], scale=1.0 / D_MODEL).then_inc(y_sqrt, 1)
            act.wait_ge(y_rs, 1)
            act.wait_ge(y_sqd, 2 * QT)
            for n in Y_POOL:
                act.activation(y_raw[:, n, :], banks[n][:, :], ACT.Copy, scale=stat[:, 3, n % QT:n % QT + 1]).then_inc(y_scaled, 1)

        @block.vector
        def _(dve):
            def sub_lo(dst, src, bias, hi, done):
                dve.scalar_tensor_tensor(dst, src, bias, hi.bitcast(F), ALU.add, ALU.subtract).then_inc(done, 1)

            def pt_low(pair):
                for b in range(5):
                    dve.wait_ge(pt_hi_done, 5 * pair + b + 1)
                    if b == 0:
                        dve.wait_ge(pt_ready, 5 * pair + 5)
                    dst, src = pt_part(pt_lo, b)
                    hi, _ = pt_part(pt_hi, b)
                    dve.tensor_tensor(dst, src, hi.bitcast(F), ALU.subtract).then_inc(pt_lo_done, 1)

            score_at = {(0, 3): (0, 0, 1), (0, 2): (1, 0, 2), (0, 0): (1, P_LEN[2], 2), (1, 3): (2, 0, 3),
                        (1, 2): (3, 0, 4), (1, 0): (3, P_LEN[2], 4), (0, 1): (4, 0, 5), (1, 1): (4, P_LEN[1], 5)}

            def mask_tile(a, i, k0, k1, bias, top):
                bank, col, _ = score_at[a, i]
                return dve.tensor_tensor_reduce(p_f[:, a, P_OFF[i] + k0:P_OFF[i] + k1], S[bank][:, col + k0:col + k1],
                                                bias, SCALE, -3e38, ALU.add, ALU.max, top)

            def wait_scores(pair, a, i):
                n = score_at[a, i][2]
                if (a, i) in ((0, 3), (0, 2), (1, 3), (1, 2), (0, 1)):
                    dve.wait_ge(scored, 5 * pair + n)
                    dve.memset(wait_cell[:, n - 1:n], 0.0)

            def invert(pair):
                dve.wait_ge(exp_done, 8 * pair + 8)
                dve.reciprocal(p_inv[:, :, :], p_sum[:, :, :]).then_inc(inv_ready, 1)

            def normalise(pair):
                for a in range(2):
                    for i in range(QT):
                        t = p_f[:, a, P_OFF[i]:P_OFF[i] + P_LEN[i]]
                        op = dve.tensor_scalar(t, t, p_inv[:, a, i:i + 1], None, ALU.mult)
                op.then_inc(normed, 1)

            for done in (pt_lo_done, o_lo_done, masked, conv_step, conv_lo, gb_used, act_lo_done, u_step):
                dve.sem_inc(done, 1)
            dve.memset(eps_c[:, :], EPS).then_inc(eps_ready, 1)
            for t in range(QT):
                dve.wait_ge(x_sqrt, t + 1)
                dve.reciprocal(stat[:, 3, t:t + 1], stat[:, 2, t:t + 1]).then_inc(x_rs, 1)
                dve.wait_ge(x_rs, t + 1)
                dve.tensor_scalar(x_n[:, t, :], x_in[:, t, :], stat[:, 3, t:t + 1], None, ALU.mult).then_inc(x_normed, 1)
            dve.wait_ge(cols_t, 1)
            dve.tensor_copy(cols1[:, :], Z[1][:, 0:N_COLS1]).then_inc(cols_ready, 1)
            dve.tensor_copy(cols2[:, :], Z[1][:, P128:P128 + N_COLS2]).then_inc(cols_ready, 1)
            dve.wait_ge(cols_ready, 1)
            dve.tensor_scalar(half_b[:, :], cols1[:, C_GATE:C_GATE + 24], 0.5, None, ALU.mult)
            for c, k in enumerate(K_ORDER):
                dve.wait_ge(h_hi_done, c + 1)
                dve.scalar_tensor_tensor(h_lo[:, k, :], x_bank[k][:, :], cols1[:, C_GMIX + k:C_GMIX + k + 1],
                                         h_hi[:, k, :].bitcast(F), ALU.mult, ALU.subtract).then_inc(h_lo_done, 1)
            dve.wait_ge(fg_ready, 1)
            f = fg[0:FOX_HEADS, :]
            dve.scalar_tensor_tensor(fe[:, :], f, -1.0, f, ALU.mult, ALU.min).then_inc(fe_step, 1)
            dve.wait_ge(fe_step, 3)
            dve.scalar_tensor_tensor(fe[:, :], fg[0:FOX_HEADS, :], 0.0, fe[:, :], ALU.min, ALU.subtract).then_inc(fe_step, 1)
            dve.wait_ge(consts, 5)
            dve.wait_ge(fe_step, 4)
            dve.tensor_tensor_scan(fe[:, :], f_one[:, :], fe[:, :], 0.0, ALU.mult, ALU.add).then_inc(fe_step, 1)
            dve.wait_ge(fe_step, 5)
            dve.tensor_scalar(fe[:, :], fe[:, :], -1.0 / SCALE, None, ALU.mult).then_inc(fe_step, 1)
            dve.wait_ge(ng_tanh, 1)
            dve.tensor_scalar(gates[:, :, :, :], ng_t[:, :, FOX_HEADS:32].rearrange("p t (h b) -> p b h t", b=3),
                              0.5, 0.5, ALU.mult, ALU.add).then_inc(gates_ready, 1)
            dve.wait_ge(small_loaded, 16 * 5)
            dve.wait_ge(tile_done, 5)
            for t in range(QT):
                dve.tensor_tensor(v_f[:, t, :], S[t][:, :], vb[:, 0:BR_W], ALU.add).then_inc(vf_ready, 1)
            for t in range(QT):
                dve.wait_ge(vf_hi, t + 1)
                dve.tensor_tensor(fv_lo[:, t, :], v_f[:, t, :], fv_hi[:, t, :].bitcast(F), ALU.subtract).then_inc(vf_lo, 1)
            dve.wait_ge(tile_done, N_FOX)
            for t, bank in enumerate((S[4], O, Z[0], Z[1])):
                dve.tensor_tensor(v2_f[:, t, :, :].rearrange("p b d -> p (b d)"), bank[:, 0:256], vb[:, BR_W:BR_W + 256], ALU.add) \
                    .then_inc((v2_ready, v2_ready, *z_free)[t], 1)
            for z in range(2):
                dve.wait_ge(z_free[z], 1)
            for a in range(2):
                dve.wait_ge(v2_hi, a + 1)
                dve.tensor_tensor(vn_lo[:, :, a, :, 64 * a:64 * a + 64],
                                  v2_f[:, :, :, 64 * a:64 * a + 64].rearrange("p t b d -> p b t d"),
                                  vn_hi[:, :, a, :, 64 * a:64 * a + 64].bitcast(F), ALU.subtract).then_inc(v2_lo, 1)

            with dve.Fori(0, PAIRS) as i:
                T = T_FOX + 6 * i
                dve.wait_ge(q_hi_done, i + 1)
                sub_lo(q_lo[:, :], Z[0][:, :], cols1[:, ds(C_FQ + i, 1)], q_hi[:, :], z_free[0])
                dve.wait_ge(k_hi_done, i + 1)
                sub_lo(k_lo[:, :], Z[1][:, :], cols1[:, ds(C_FK + i, 1)], k_hi[:, :], z_free[1])
                order = [(0, 3), (0, 2), (0, 0), (1, 3), (1, 2), (1, 0), (0, 1), (1, 1)]
                dve.wait_ge(diag_ready, 2 * i + 2)
                dve.wait_ge(consts, N_CONST)
                for s, (a, t) in enumerate(order):
                    wait_scores(i, a, t)
                    k = P128 * t
                    op = mask_tile(a, t, k, k + P128, f_diag[:, a, t, :], mx2[:, a, t, 0:1])
                    if t:
                        op = mask_tile(a, t, 0, k, f_bias[:, a, 0:k], mx2[:, a, t, 1:2])
                op.then_inc(masked, 1)
                dve.wait_ge(masked, i + 1 + 1)
                dve.tensor_reduce(mx[:, :, :], mx2[:, :, :, :], AX.X, ALU.max).then_inc(neg_pre, 1)
                dve.wait_ge(neg_pre, i + 1)
                dve.tensor_scalar(neg_mx[:, :, :], mx[:, :, :], -1.0, None, ALU.mult).then_inc(neg_ready, 1)
                invert(i)
                dve.wait_ge(inv_ready, i + 1)
                normalise(i)
                dve.wait_ge(tile_done, T + 5)
                dve.wait_ge(z_free[1], Z_FOX[1] + 3 * i + 2)
                dve.scalar_tensor_tensor(conv_t[:, 2:SEQ + 2], Z[0][:, :], cols1[:, ds(C_CX + i, 1)], conv_c[:, :],
                                         ALU.add, ALU.mult).then_inc(z_free[0], 1)
                dve.wait_ge(z_free[0], Z_FOX[0] + 3 * i + 3)
                dve.memset(conv_t[:, 0:2], 0.0).then_inc(conv_t_done, 1)
                pt_low(i)
                dve.wait_ge(conv_w2, i + 1)
                for tap in (1, 0):
                    dve.scalar_tensor_tensor(conv_u[:, :], conv_t[:, tap:SEQ + tap], cols1[:, ds(C_SC + 4 * tap + i, 1)], conv_u[:, :],
                                             ALU.mult, ALU.add).then_inc(conv_step, 1)
                    dve.wait_ge(conv_step, 3 * i + 2 - tap + 1)
                dve.tensor_tensor(conv_c[:, :], conv_u[:, :], conv_b[:, :], ALU.mult).then_inc(conv_step, 1)
                dve.wait_ge(nk_hi_done, i + 1)
                sub_lo(nk_lo[:, i, :], Z[1][:, :], cols1[:, ds(C_NK + i, 1)], nk_hi[:, i, :], z_free[1])
                dve.wait_ge(conv_hi, i + 1)
                dve.tensor_tensor(br_lo[:, PAIRS + i, :], conv_c[:, :], br_hi[:, PAIRS + i, :].bitcast(F), ALU.subtract).then_inc(conv_lo, 1)
                dve.wait_ge(o_hi_done, i + 1)
                dve.tensor_tensor(br_lo[:, i, :], O[:, :], br_hi[:, i, :].bitcast(F), ALU.subtract).then_inc(o_lo_done, 1)

            dve.wait_ge(pv_done, PAIRS + 1)
            dve.wait_ge(z_free[1], Z_CMP[1])
            for b, pe_col, pe_cols in ((0, C_PEK, cols1), (1, C_PEV, cols2)):
                for g in range(2):
                    dve.memset(cz[64 * g:64 * g + 64, b, :, N_BLK * (1 - g):N_BLK * (2 - g)], 0.0)
                    rows = slice(64 * g, 64 * g + 64)
                    dve.tensor_tensor(cz[rows, b, :, N_BLK * g:N_BLK * g + N_BLK],
                                      nk_hi[rows, b, :].bitcast(F).rearrange("p (c r) -> p r c", r=CMP_STRIDE),
                                      nk_lo[rows, b, :].bitcast(F).rearrange("p (c r) -> p r c", r=CMP_STRIDE), ALU.add) \
                        .then_inc(cz_ready, 1)
                dve.tensor_copy(cz[:, b, :, 2 * N_BLK:CZ_W],
                                pe_cols[:, pe_col:pe_col + CMP_LEN].rearrange("p (h r) -> p r h", h=2)).then_inc(cz_ready, 1)
            for h in range(2):
                dve.tensor_scalar(sel[:, h, :], ident[0:CZ_W, h:h + 2 * N_BLK], ident[0:CZ_W, 2 * N_BLK + h:2 * N_BLK + h + 1],
                                  None, ALU.add).then_inc(sel_ready, 1)
            for b in range(2):
                dve.wait_ge(hid_done, b + 1)
                dve.tensor_copy(hid_f[:, b, :, :], S[b][0:CZ_W, 0:P128].rearrange("p (h m) -> p h m", h=2)).then_inc(hid_ready, 1)
            dve.wait_ge(cmp_hi, 1)
            dve.tensor_tensor(kc_lo[:, :], S[4][:, 0:2 * N_BLK], kc_hi[:, :].bitcast(F), ALU.subtract).then_inc(cmp_lo, 1)
            dve.wait_ge(cmp_hi, 2)
            dve.tensor_tensor(vc_lo[:, :], O[0:64, 0:P128], vc_hi[:, :].bitcast(F), ALU.subtract).then_inc(cmp_lo, 1)
            dve.wait_ge(alibi_ready, 3)
            for a in range(2):
                dve.tensor_scalar(alibi[:, a, :], alibi[:, a, :], 0.5 ** (1 + 4 * a) / SCALE, None, ALU.mult).then_inc(alibi_scaled, 1)
            dve.wait_ge(alibi_scaled, 2)

            with dve.Fori(0, PAIRS) as i:
                T = T_NSA + 10 * i
                z0, z1 = Z_NSA[0] + 5 * i, Z_NSA[1] + 5 * i

                def softmax_scores(pair):
                    for a, t in [(0, 3), (0, 2), (0, 0), (1, 3), (1, 2), (1, 0), (0, 1), (1, 1)]:
                        wait_scores(pair, a, t)
                        op = mask_tile(a, t, 0, P_LEN[t], alibi[:, a, SEQ - P_LEN[t]:SEQ], mx[:, a, t:t + 1])
                    op.then_inc(masked, 1)
                    dve.wait_ge(masked, pair + 1 + 1)
                    dve.tensor_scalar(neg_mx[:, :, :], mx[:, :, :], -1.0, None, ALU.mult).then_inc(neg_ready, 1)

                def gate_inv(pair, br):
                    invert(pair)
                    dve.wait_ge(inv_ready, pair + (pair - PAIRS) + 1)
                    g = gates[:, br, :, :].rearrange("p (a h) t -> p a h t", a=2)[:, :, ds(i, 1), :] \
                        .rearrange("p a h t -> p a (h t)")
                    dve.tensor_tensor(p_inv[:, :, :], p_inv[:, :, :], g, ALU.mult).then_inc(inv_ready, 1)
                    dve.wait_ge(inv_ready, pair + (pair - PAIRS) + 2)

                dve.wait_ge(q_hi_done, PAIRS + i + 1)
                sub_lo(q_lo[:, :], Z[0][:, :], cols1[:, ds(C_NQ + i, 1)], q_hi[:, :], z_free[0])
                softmax_scores(PAIRS + 2 * i)
                flat = "p t a c -> p (t a) c"
                cp = c_p[:, :, :, :].rearrange(flat)
                dve.wait_ge(c_t, i + 1)
                dve.wait_ge(c_scored, i + 1)
                dve.scalar_tensor_tensor(c_p[:, :, :, :].rearrange("p t a c -> p (t a c)"), O[:, 0:256], SCALE,
                                         c_bias[:, :, :, :].rearrange("p t a c -> p (t a c)"), ALU.mult, ALU.add).then_inc(c_step, 1)
                dve.wait_ge(c_step, 5 * i + 1)
                dve.tensor_reduce(c_mx[:, :, :].rearrange("p t a -> p (t a)"), cp, AX.X, ALU.max).then_inc(c_step, 1)
                dve.wait_ge(c_step, 5 * i + 2)
                dve.tensor_tensor(cp, cp, c_mx[:, :, :].rearrange("p t (a o) -> p (t a) o", o=1).to_broadcast([P128, 2 * QT, CMP_LEN]),
                                  ALU.subtract).then_inc(c_step, 1)
                gate_inv(PAIRS + 2 * i, 1)
                normalise(PAIRS + 2 * i)
                dve.wait_ge(c_exp, i + 1)
                dve.tensor_reduce(c_sum[:, :, :].rearrange("p t a -> p (t a)"), cp, AX.X, ALU.add).then_inc(c_red, 1)
                dve.wait_ge(c_red, 4 * i + 1)
                dve.reciprocal(c_sum[:, :, :], c_sum[:, :, :]).then_inc(c_red, 1)
                dve.wait_ge(c_red, 4 * i + 2)
                dve.tensor_tensor(c_sum[:, :, :], c_sum[:, :, :],
                                  gates[:, 0, :, :].rearrange("p (a h) t -> p h t a", a=2)[:, ds(i, 1), :, :]
                                  .rearrange("p h t a -> p (h t) a"), ALU.mult).then_inc(c_red, 1)
                dve.tensor_tensor(cp, cp, c_mask[:, :, :, :].rearrange(flat), ALU.mult).then_inc(c_red, 1)
                dve.wait_ge(c_red, 4 * i + 4)
                dve.tensor_tensor(cp, cp, c_sum[:, :, :].rearrange("p t (a o) -> p (t a) o", o=1).to_broadcast([P128, 2 * QT, CMP_LEN]),
                                  ALU.mult).then_inc(c_ready, 1)

                def gated(m, t, z_a, z_b):
                    dve.wait_ge(z_free[1], z_a)
                    dve.wait_ge(tile_done, t + 1)
                    dve.scalar_tensor_tensor(mix[:, m, :], g_a[:, :], 1.0, Z[1][:, :], ALU.add, ALU.mult).then_inc(z_free[1], 1)
                    dve.wait_ge(z_free[0], z_b)
                    dve.wait_ge(tile_done, t + 2)
                    dve.scalar_tensor_tensor(g_b[:, :], g_b[:, :], 1.0, Z[0][:, :], ALU.add, ALU.mult).then_inc(z_free[0], 1)
                    dve.wait_ge(z_free[1], z_a + 1)
                    dve.wait_ge(z_free[0], z_b + 1)
                    dve.tensor_tensor(mix[:, m, :], mix[:, m, :], g_b[:, :], ALU.add).then_inc(gb_used, 1)

                gated(2 * i, T + 3, z1 + 1, z0 + 2)
                pt_low(PAIRS + 2 * i)
                dve.wait_ge(c_t_hi, i + 1)
                dve.tensor_tensor(c_pt_lo[:, :], O[0:64, :], c_pt_hi[:, :].bitcast(F), ALU.subtract).then_inc(c_t_lo, 1)
                dve.wait_ge(pv_s_done, i + 1)
                softmax_scores(PAIRS + 2 * i + 1)
                dve.wait_ge(masked, PAIRS + 2 * i + 2 + 1)
                dve.tensor_scalar(alibi[:, :, :], alibi[:, :, :], 0.5, None, ALU.mult).then_inc(c_step, 1)
                dve.tensor_scalar(c_bias[:, :, :, :], c_bias[:, :, :, :], 0.5, None, ALU.mult).then_inc(c_step, 1)
                dve.wait_ge(c_step, 5 * i + 5)
                gate_inv(PAIRS + 2 * i + 1, 2)
                normalise(PAIRS + 2 * i + 1)
                gated(2 * i + 1, T + 7, z1 + 3, z0 + 4)
                pt_low(PAIRS + 2 * i + 1)
                dve.wait_ge(o_hi_done, PAIRS + i + 1)
                dve.tensor_tensor(c_lo[:, i, :], O[:, :], c_hi[:, i, :].bitcast(F), ALU.subtract).then_inc(o_lo_done, 1)

            tau = 0
            for kind, m in MIX_ORDER:
                if kind == "gc":
                    tau += 1
                    continue
                for mt in (m, m + 1):
                    z = tau % 2
                    dve.wait_ge(z_free[z], Z_MIX[z] + tau // 2)
                    dve.wait_ge(tile_done, T_MIX + tau + 1)
                    g = g_c[:, mt, :]
                    dve.scalar_tensor_tensor(g, g, 1.0, Z[z][:, :], ALU.add, ALU.mult).then_inc(z_free[z], 1)
                    dve.wait_ge(z_free[z], Z_MIX[z] + tau // 2 + 1)
                    dve.tensor_tensor(mix[:, mt, :], mix[:, mt, :], g, ALU.add).then_inc(mix_done, 1)
                    tau += 1
                for mt in (m, m + 1):
                    dve.wait_ge(mix_hi, mt + 1)
                    dve.scalar_tensor_tensor(br_lo[:, mt, :], mix[:, mt, :], 0.5, br_hi[:, mt, :].bitcast(F),
                                             ALU.mult, ALU.subtract).then_inc(mix_lo, 1)
            for m in range(KT):
                z = m % 2
                dve.wait_ge(xr_copied, m + 1)
                dve.wait_ge(tile_done, T_WO + m + 1)
                dve.tensor_tensor(x2[:, m, :], Z[z][:, :], x2[:, m, :], ALU.add).then_inc(z_free[z], 1)
                dve.wait_ge(z_free[z], Z_WO[z] + m // 2 + 1)
                dve.wait_ge(xg_hi, m + 1)
                dve.scalar_tensor_tensor(h_lo[:, m, :], x2[:, m, :], cols1[:, C_GFFN + m:C_GFFN + m + 1], h_hi[:, m, :].bitcast(F),
                                         ALU.mult, ALU.subtract).then_inc(xg_lo, 1)
                if m:
                    dve.wait_ge(acc_done, m)
                sq = x_sq if m else x_acc
                dve.tensor_tensor(sq[:, :], x2[:, m, :], x2[:, m, :], ALU.mult).then_inc(sq_done if m else acc_done, 1)
                if m:
                    dve.wait_ge(sq_done, m)
                    dve.tensor_tensor(x_acc[:, :], x_acc[:, :], x_sq[:, :], ALU.add).then_inc(acc_done, 1)
            dve.memset(u_t[:, 0:2], 0.0).then_inc(rs_ready, 1)
            dve.wait_ge(rs_sqrt, 1)
            dve.reciprocal(rstd[:, :], rstd[:, :]).then_inc(rs_ready, 1)
            dve.wait_ge(rs_ready, 2)

            with dve.Fori(0, FT) as i:
                T = T_UP + 2 * i
                dve.wait_ge(u_step, 2 * i + 1)
                dve.wait_ge(tile_done, T + 1)
                dve.tensor_tensor(u_t[:, 2:SEQ + 2], Z[0][:, :], rstd[:, :], ALU.mult).then_inc(z_free[0], 1)
                dve.wait_ge(z_free[0], Z_UP[0] + i + 1)
                dve.memset(u_t[:, 0:2], 0.0).then_inc(u_ready, 1)
                dve.wait_ge(u_w2, i + 1)
                for tap in (1, 0):
                    dve.scalar_tensor_tensor(u_c[:, :], u_t[:, tap:SEQ + tap], cols2[:, ds(C_FFN + FT * tap + i, 1)], u_c[:, :],
                                             ALU.mult, ALU.add).then_inc(u_step, 1)
                    dve.wait_ge(u_step, 2 * i + 2 - tap + 1)
                dve.wait_ge(tile_done, T + 2)
                dve.tensor_tensor(v_t[:, :], Z[1][:, :], rstd[:, :], ALU.mult).then_inc(z_free[1], 1)
                dve.wait_ge(z_free[1], Z_UP[1] + i + 1)
                dve.wait_ge(u_silu, i + 1)
                dve.tensor_tensor(u_c[:, :], u_c[:, :], v_t[:, :], ALU.mult).then_inc(uv_done, 1)
                dve.wait_ge(act_hi_done, i + 1)
                dve.tensor_tensor(act_lo[:, i, :], u_c[:, :], act_hi[:, i, :].bitcast(F), ALU.subtract).then_inc(act_lo_done, 1)

            for m in range(KT):
                dve.wait_ge(down_done, m + 1)
                dve.tensor_tensor(x2[:, m, :], banks[m][:, :], x2[:, m, :], ALU.add).then_inc(x3_done, 1)
            dve.wait_ge(y_sqd, 2 * QT)
            dve.tensor_tensor(stat[:, 2, :], stat[:, 0, :], stat[:, 1, :], ALU.add).then_inc(y_ms, 1)
            dve.wait_ge(y_sqrt, 1)
            dve.reciprocal(stat[:, 3, :], stat[:, 2, :]).then_inc(y_rs, 1)
            dve.wait_ge(y_rs, 1)
            dve.wait_ge(g_loaded, 16)
            for n in Y_DVE:
                h = n // QT
                dve.scalar_tensor_tensor(y_out[:, n, :], banks[n][:, :], stat[:, 3, n % QT:n % QT + 1],
                                         g_out[:, BR_W * h:BR_W * h + BR_W], ALU.mult, ALU.mult).then_inc(y_dve, 1)


_INS = ["x", "norm_mix_g", "w_in", "b_in", "cmp_pe_k", "cmp_w1_k", "cmp_w2_k", "cmp_pe_v", "cmp_w1_v",
        "cmp_w2_v", "sc_conv_w", "w_br_a", "w_br_b", "w_br_c", "w_o", "norm_ffn_g", "w_up", "ffn_conv_w",
        "w_down", "norm_final_g"]


def kernel(**inputs):
    import numpy as np
    import concourse.bacc as bacc
    from concourse import mybir
    from concourse.bass_utils import run_bass_kernel_spmd

    nc = bacc.Bacc("TRN2", target_bir_lowering=False, num_devices=1, dynamic_dma_scratch_size=1024)
    arrays, args = {}, []
    for name in _INS:
        a = np.ascontiguousarray(inputs[name])
        arrays[f"in_{name}"] = a
        args.append(nc.dram_tensor(f"in_{name}", a.shape, mybir.dt.from_np(a.dtype), kind="ExternalInput").ap())
    out = nc.dram_tensor("out_0", (1, SEQ, D_MODEL), mybir.dt.float32, kind="ExternalOutput").ap()
    hybrid_block(nc, *args, out)
    r = run_bass_kernel_spmd(nc, [arrays], core_ids=[0])
    return r.results[0]["out_0"]
```

```python
import concourse.bass as bass
from concourse import mybir
from contextlib import ExitStack

D_MODEL = 1024
SEQ = 512
HEAD_DIM = 64
FOX_HEADS = 8
NSA_HEADS = 8
BR_W = 512
D_FF = 2816
CMP_LEN = 32
CMP_STRIDE = 16
EPS = 1e-6
NEG = -8e30
SCALE = HEAD_DIM ** -0.5

P128 = 128
KT = D_MODEL // P128
QT = SEQ // P128
FT = D_FF // P128
PAIRS = FOX_HEADS // 2
CH = KT * P128

O_GA, O_GB, O_GC = 0, D_MODEL, 2 * D_MODEL
O_FQ = 3 * D_MODEL
O_FK = O_FQ + BR_W
O_FV = O_FK + BR_W
O_FF = O_FV + BR_W
O_CB = O_FF + FOX_HEADS
O_CC = O_CB + BR_W
O_CX = O_CC + BR_W
O_NQ = O_CX + BR_W
O_KC = O_NQ + BR_W
O_VC, O_KS, O_VS, O_KW, O_VW = (O_KC + P128 * n for n in range(1, 6))
O_NG = O_VW + P128

C_GATE = 0
C_FQ, C_FK = 24, 28
C_CB, C_CC, C_CX = 32, 36, 40
C_NQ = 44
C_NK = 48
C_SC = 52
C_GMIX, C_GFFN = 64, 72
C_PEK = 80
N_COLS1 = C_PEK + CMP_LEN
C_FFN = 0
C_PEV = 3 * FT
N_COLS2 = C_PEV + CMP_LEN

N_V2 = 3
V2_V = 2 * P128
V2_W = V2_V + FOX_HEADS + 3 * NSA_HEADS
V2_K = ((0, 2), (2, 5), (5, KT))

N_FOX, T_FOX = 7, 7
N_CMP, T_CMP = N_FOX + 6 * PAIRS, T_FOX + 6 * PAIRS
N_NSA, T_NSA = N_CMP + 2, T_CMP + 2
N_MIX, T_MIX = N_NSA + 8 * PAIRS, T_NSA + 10 * PAIRS
N_WO, T_WO = N_MIX + 6, T_MIX + 10
N_UP, T_UP = N_WO + 8, T_WO + 8
N_DN, T_DN = N_UP + 2 * FT, T_UP + 2 * FT
N_END = N_DN + FT
Z_FOX = (1, 1)
Z_CMP = tuple(z + 3 * PAIRS for z in Z_FOX)
Z_NSA = tuple(z + 1 for z in Z_CMP)
Z_MIX = tuple(z + 5 * PAIRS for z in Z_NSA)
Z_WO = tuple(z + 5 for z in Z_MIX)
Z_UP = tuple(z + 4 for z in Z_WO)

MIX_ORDER = (("gc", 6), ("yc", 0), ("yc", 2), ("gc", 7), ("yc", 4), ("yc", 6))


N_BLK = SEQ // CMP_STRIDE
CZ_W = 2 * N_BLK + 2

P_LEN = [P128 * (i + 1) for i in range(QT)]
P_OFF = [0, 128, 384, 768]
P_ALL = sum(P_LEN)
T_LEN = [SEQ - P128 * j for j in range(QT)]
T_OFF = [0, 512, 1024, 896]


def hybrid_block(nc, x, norm_mix_g, w_in, b_in, cmp_pe_k, cmp_w1_k, cmp_w2_k, cmp_pe_v, cmp_w1_v,
                 cmp_w2_v, sc_conv_w, w_br_a, w_br_b, w_br_c, w_o, norm_ffn_g, w_up, ffn_conv_w,
                 w_down, norm_final_g, out):
    F = mybir.dt.float32
    R = mybir.dt.float32r
    ACT = mybir.ActivationFunctionType
    ALU = mybir.AluOpType
    AX = mybir.AxisListType
    ds = bass.ds

    w_in, b_in = w_in[0], b_in[0]
    w_o, w_up, w_down = w_o[0], w_up[0], w_down[0]
    w_br = [w_br_a[0], w_br_b[0], w_br_c[0]]

    with ExitStack() as ctx:
        def sb(name, shape, dt=F, scope=ctx):
            return scope.enter_context(nc.sbuf_tensor(name, shape, dt))

        def sem(name):
            return ctx.enter_context(nc.semaphore(name))

        raw = sb("raw", [P128, 2, CH])
        w_hi = sb("w_hi", [P128, 2, CH], R)
        w_lo = sb("w_lo", [P128, 2, CH], R)
        with ExitStack() as s:
            y_out = sb("y_out", [P128, 2 * QT, BR_W], F, s)
            y_sq = sb("y_sq", [P128, 2 * QT, BR_W], F, s)
        h_hi = sb("h_hi", [P128, KT, SEQ], R)
        h_lo = sb("h_lo", [P128, KT, SEQ], R)
        ident = sb("ident", [P128, P128])
        ones = sb("ones", [P128, P128])
        cols1 = sb("cols1", [P128, N_COLS1])
        cols2 = sb("cols2", [P128, N_COLS2])
        half_b = sb("half_b", [P128, 24])
        stat = sb("stat", [P128, 4, 4])
        eps_c = sb("eps_c", [P128, 1])
        act_cell = sb("act_cell", [P128, 6])
        wait_cell = sb("wait_cell", [P128, 5])
        with ExitStack() as s:
            x_in = sb("x_in", [P128, QT, D_MODEL], F, s)
            x_n = sb("x_n", [P128, QT, D_MODEL], F, s)
        with ExitStack() as s:
            v_f = sb("v_f", [P128, QT, BR_W], F, s)
            v2_f = sb("v2_f", [P128, QT, 2, P128], F, s)
        br_hi = sb("br_hi", [P128, 2 * PAIRS, SEQ], R)
        br_lo = sb("br_lo", [P128, 2 * PAIRS, SEQ], R)

        att = ExitStack()
        q_hi = sb("q_hi", [P128, SEQ], R, att)
        q_lo = sb("q_lo", [P128, SEQ], R, att)
        nk_hi = sb("nk_hi", [P128, 4, SEQ], R, att)
        nk_lo = sb("nk_lo", [P128, 4, SEQ], R, att)
        vn_hi = sb("vn_hi", [P128, 2, 2, QT, P128], R, att)
        vn_lo = sb("vn_lo", [P128, 2, 2, QT, P128], R, att)
        with ExitStack() as s:
            rows1 = sb("rows1", [N_COLS1, P128], F, s)
            rows2 = sb("rows2", [N_COLS2, P128], F, s)
            fg = sb("fg", [FOX_HEADS, SEQ], F, s)
            fe = sb("fe", [FOX_HEADS, SEQ], F, s)
            f_one = sb("f_one", [FOX_HEADS, SEQ], F, s)
        with ExitStack() as s:
            cz = sb("cz", [P128, 2, CMP_STRIDE, CZ_W], F, s)
            sel = sb("sel", [CZ_W, 2, 2 * N_BLK], F, s)
            hid_f = sb("hid_f", [CZ_W, 2, 2, HEAD_DIM], F, s)
            hid_k = sb("hid_k", [HEAD_DIM, 2 * N_BLK], F, s)
        with ExitStack() as s:
            p_f = sb("p_f", [P128, 2, P_ALL], F, s)
        pt_lo = sb("pt_lo", [P128, 2, P_ALL], R, att)
        pt_hi = sb("pt_hi", [P128, 2, P_ALL], R, att)
        mx2 = sb("mx2", [P128, 2, QT, 2], F, att)
        mx = sb("mx", [P128, 2, QT], F, att)
        neg_mx = sb("neg_mx", [P128, 2, QT], F, att)
        p_sum = sb("p_sum", [P128, 2, QT], F, att)
        p_inv = sb("p_inv", [P128, 2, QT], F, att)
        gates = sb("gates", [P128, 3, NSA_HEADS, QT], F, att)
        c_bias = sb("c_bias", [P128, QT, 2, CMP_LEN], F, att)
        c_mask = sb("c_mask", [P128, QT, 2, CMP_LEN], F, att)
        c_pad = sb("c_pad", [P128, QT + 1, 2, CMP_LEN], F, att)
        c_p = c_pad[:, 0:QT, :, :]
        c_mx = sb("c_mx", [P128, QT, 2], F, att)
        c_sum = sb("c_sum", [P128, QT, 2], F, att)
        c_pt_hi = sb("c_pt_hi", [64, SEQ], R, att)
        c_pt_lo = sb("c_pt_lo", [64, SEQ], R, att)
        kc_hi = sb("kc_hi", [P128, 2 * N_BLK], R, att)
        kc_lo = sb("kc_lo", [P128, 2 * N_BLK], R, att)
        vc_hi = sb("vc_hi", [64, P128], R, att)
        vc_lo = sb("vc_lo", [64, P128], R, att)
        with ExitStack() as s:
            fv_hi = sb("fv_hi", [P128, QT, BR_W], R, s)
            fv_lo = sb("fv_lo", [P128, QT, BR_W], R, s)
            vp_hi = sb("vp_hi", [P128, 2, QT, P128], R, s)
            vp_lo = sb("vp_lo", [P128, 2, QT, P128], R, s)
            k_hi = sb("k_hi", [P128, SEQ], R, s)
            k_lo = sb("k_lo", [P128, SEQ], R, s)
            f_bias = sb("f_bias", [P128, 2, SEQ], F, s)
            f_diag = sb("f_diag", [P128, 2, QT, P128], F, s)
            tri = sb("tri", [P128, P128], F, s)
            conv_b = sb("conv_b", [P128, SEQ], F, s)
            conv_c = sb("conv_c", [P128, SEQ], F, s)
            conv_t = sb("conv_t", [P128, SEQ + 2], F, s)
            conv_u = sb("conv_u", [P128, SEQ], F, s)
            lg_t = sb("lg_t", [P128, QT, V2_W - V2_V], F, s)
            vb = sb("vb", [P128, BR_W + V2_W], F, s)
            w1 = sb("w1", [P128, 2, CMP_STRIDE, 2, HEAD_DIM], F, s)
            w2k = sb("w2k", [HEAD_DIM, 2, P128], F, s)
            w2v = sb("w2v", [HEAD_DIM, HEAD_DIM], F, s)
            hid_v = sb("hid_v", [HEAD_DIM, 2, 2 * N_BLK], F, s)
        with ExitStack() as s:
            g_c = sb("g_c", [P128, KT, SEQ], F, s)
            mix = sb("mix", [P128, KT, SEQ], F, s)
            c_hi = sb("c_hi", [P128, PAIRS, SEQ], R, s)
            c_lo = sb("c_lo", [P128, PAIRS, SEQ], R, s)
            g_a = sb("g_a", [P128, SEQ], F, s)
            g_b = sb("g_b", [P128, SEQ], F, s)
            alibi = sb("alibi", [P128, 2, SEQ], F, s)
        att.close()

        ffn = ExitStack()
        x2 = sb("x2", [P128, KT, SEQ], F, ffn)
        with ExitStack() as s:
            x_r = sb("x_r", [P128, QT, D_MODEL], F, s)
        act_hi = sb("act_hi", [P128, FT, SEQ], R, ffn)
        act_lo = sb("act_lo", [P128, FT, SEQ], R, ffn)
        x_sq = sb("x_sq", [P128, SEQ], F, ffn)
        x_acc = sb("x_acc", [P128, SEQ], F, ffn)
        rstd = sb("rstd", [P128, SEQ], F, ffn)
        u_t = sb("u_t", [P128, SEQ + 2], F, ffn)
        u_c = sb("u_c", [P128, SEQ], F, ffn)
        v_t = sb("v_t", [P128, SEQ], F, ffn)
        g_out = sb("g_out", [P128, D_MODEL], F, ffn)
        ffn.close()

        S = [ctx.enter_context(nc.psum_tensor(f"s_bank{n}", [P128, SEQ], F)) for n in range(5)]
        O = ctx.enter_context(nc.psum_tensor("o_bank", [P128, SEQ], F))
        Z = [ctx.enter_context(nc.psum_tensor(f"z_bank{n}", [P128, SEQ], F)) for n in range(2)]
        banks = [*S, O, *Z]

        cum_dram = nc.dram_tensor("cum_scratch", [FOX_HEADS, SEQ], F, kind="Internal").ap()

        raw_loaded = [sem("raw_loaded0"), sem("raw_loaded1")]
        hi_split = sem("hi_split")
        lo_split = sem("lo_split")
        tile_done = sem("tile_done")
        z_free = [sem("z_free0"), sem("z_free1")]
        x_loaded = [sem(f"x_loaded{t}") for t in range(QT)]
        rows_loaded = sem("rows_loaded")
        small_loaded = sem("small_loaded")
        w1_loaded = sem("w1_loaded")
        consts = sem("consts")
        N_CONST = 23
        rows_zero = sem("rows_zero")
        lg_loaded = [sem(f"lg_loaded{n}") for n in range(N_V2)]
        cols_t = sem("cols_t")
        cols_ready = sem("cols_ready")
        x_ss = sem("x_ss"); x_sqrt = sem("x_sqrt"); x_rs = sem("x_rs")
        x_normed = sem("x_normed")
        x_t = sem("x_t")
        h_hi_done = sem("h_hi_done"); h_lo_done = sem("h_lo_done")
        fe_step = sem("fe_step")
        cum_stored = sem("cum_stored")
        fbias_loaded = sem("fbias_loaded")

        lg_ready = sem("lg_ready")
        fg_t = sem("fg_t")
        ng_tanh = sem("ng_tanh"); gates_ready = sem("gates_ready")
        vf_ready = sem("vf_ready"); vf_hi = sem("vf_hi"); vf_lo = sem("vf_lo")
        v2_ready = sem("v2_ready"); v2_hi = sem("v2_hi"); v2_lo = sem("v2_lo")
        q_hi_done = sem("q_hi_done"); k_hi_done = sem("k_hi_done"); nk_hi_done = sem("nk_hi_done")
        vpad = sem("vpad"); diag_ready = sem("diag_ready")

        conv_t_done = sem("conv_t_done"); conv_w2 = sem("conv_w2"); conv_step = sem("conv_step")
        conv_hi = sem("conv_hi"); conv_lo = sem("conv_lo")
        a1_scored = sem("a1_scored")
        scored = sem("scored")
        masked = sem("masked")
        neg_ready = sem("neg_ready")
        exp_done = sem("exp_done")
        inv_ready = sem("inv_ready")
        normed = sem("normed")
        pt_ready = sem("pt_ready")
        pt_hi_done = sem("pt_hi_done")
        pt_lo_done = sem("pt_lo_done")
        pv_s_done = sem("pv_s_done")
        pv_done = sem("pv_done")
        o_hi_done = sem("o_hi_done"); o_lo_done = sem("o_lo_done")
        cz_ready = sem("cz_ready"); hid_done = sem("hid_done"); hid_ready = sem("hid_ready")
        sel_ready = sem("sel_ready"); hid_sum = sem("hid_sum")
        gelu_done = sem("gelu_done")
        cmp_done = sem("cmp_done"); cmp_hi = sem("cmp_hi"); cmp_lo = sem("cmp_lo")
        c_scored = sem("c_scored"); c_step = sem("c_step"); c_exp = sem("c_exp")
        c_ready = sem("c_ready"); c_t = sem("c_t"); c_t_hi = sem("c_t_hi"); c_t_lo = sem("c_t_lo")
        alibi_ready = sem("alibi_ready"); alibi_scaled = sem("alibi_scaled")
        mix_done = sem("mix_done"); gb_used = sem("gb_used")

        mix_hi = sem("mix_hi"); mix_lo = sem("mix_lo")
        xr_loaded = sem("xr_loaded"); xr_t = sem("xr_t"); xr_copied = sem("xr_copied")
        xg_hi = sem("xg_hi"); xg_lo = sem("xg_lo"); sq_done = sem("sq_done"); acc_done = sem("acc_done")
        ss_done = sem("ss_done"); rs_sqrt = sem("rs_sqrt"); rs_ready = sem("rs_ready")
        u_ready = sem("u_ready"); u_w2 = sem("u_w2"); u_step = sem("u_step"); u_silu = sem("u_silu")
        uv_done = sem("uv_done"); act_hi_done = sem("act_hi_done"); act_lo_done = sem("act_lo_done")
        down_done = sem("down_done"); x3_done = sem("x3_done"); x3_t = sem("x3_t")
        y_sqd = sem("y_sqd"); y_ms = sem("y_ms"); y_sqrt = sem("y_sqrt"); y_rs = sem("y_rs")
        g_loaded = sem("g_loaded")
        y_gained = sem("y_gained"); y_low = sem("y_low"); y_high = sem("y_high"); y_stored = sem("y_stored")

        neg_pre = sem("neg_pre")
        c_red = sem("c_red")
        eps_ready = sem("eps_ready")
        x_bank = [S[4], O, Z[0], S[3], S[0], S[1], S[2], Z[1]]
        v2_bank = x_bank[0:QT]

        def pt_part(tile, b):
            if b < 4:
                return tile[:, b // 2, SEQ * (b % 2):SEQ * (b % 2) + SEQ], S[b][:, :]
            return tile[:, :, 2 * SEQ:P_ALL], S[4][:, :].rearrange("p (a q) -> p a q", a=2)

        block = ctx.enter_context(nc.Block())

        w_k = w_in.rearrange("(k p) n -> p k n", p=P128)
        up_k = w_up.rearrange("(k p) n -> p k n", p=P128)
        wo_k = w_o.rearrange("(k p) n -> p k n", p=P128)

        @block.sync
        def _(sp):
            def view(slot, k):
                return raw[:, slot, :].rearrange("p (k m) -> p k m", k=k)

            def raw_free(n):
                if not isinstance(n, int) or n >= 2:
                    sp.wait_ge(lo_split, n - 1)

            def load8(n, slot, src, col):
                raw_free(n)
                for h in range(2):
                    sp.dma_start(view(slot, KT)[:, 4 * h:4 * h + 4, :],
                                 src[:, 4 * h:4 * h + 4, ds(col, P128)]).then_inc(raw_loaded[slot], 16)

            def load_nq(n, slot, t):
                raw_free(n)
                for g in range(2):
                    sp.dma_start(view(slot, KT)[:, :, 64 * g:64 * g + 64],
                                 w_k[:, :, ds(O_NQ + 256 * g + HEAD_DIM * t, HEAD_DIM)]).then_inc(raw_loaded[slot], 16)

            def load_ab(n, slot, m):
                raw_free(n)
                for b in range(2):
                    sp.dma_start(view(slot, KT)[:, 4 * b:4 * b + 4, :],
                                 w_br[b].rearrange("(k p) n -> p k n", p=P128)[:, :, ds(P128 * m, P128)]) \
                        .then_inc(raw_loaded[slot], 16)

            x_v = x[0].rearrange("(t p) n -> p t n", p=P128)
            rows = [(0, 32, b_in[O_GA:O_FV]), (C_CB, 12, b_in[O_CB:O_NQ]),
                    (C_NK, 3, b_in[O_KC:O_VS]), (C_NK + 3, 1, b_in[O_KW:O_VW]),
                    (C_SC, 12, sc_conv_w[0].rearrange("k n -> (k n)")), (C_GMIX, KT, norm_mix_g[0]),
                    (C_GFFN, KT, norm_ffn_g[0])]
            for t in range(QT):
                sp.dma_start(x_in[:, t, :], x_v[:, t, :]).then_inc(x_loaded[t], 16)
            def load_v2(n, logits):
                k0, k1 = V2_K[n]
                to = raw[:, n % 2, 0:V2_W * (k1 - k0)].rearrange("p (k m) -> p k m", m=V2_W)
                if logits:
                    cols, done = ((V2_V, O_FF, FOX_HEADS), (V2_V + FOX_HEADS, O_NG, 3 * NSA_HEADS)), lg_loaded[n]
                else:
                    cols, done = ((0, O_VS, P128), (P128, O_VW, P128)), raw_loaded[n % 2]
                for c, o, m in cols:
                    sp.dma_start(to[:, :, c:c + m], w_k[:, k0:k1, o:o + m]).then_inc(done, 16)

            load_v2(0, False)
            sp.wait_ge(rows_zero, 2)
            for c, n, src in rows:
                sp.dma_start(rows1[c:c + n, :], src.rearrange("(r m) -> r m", m=P128)).then_inc(rows_loaded, 16)
            for g in range(2):
                sp.dma_start(rows1[C_NQ:C_NQ + PAIRS, 64 * g:64 * g + 64],
                             b_in[O_NQ + 256 * g:O_NQ + 256 * g + 256].rearrange("(r m) -> r m", m=HEAD_DIM)) \
                    .then_inc(rows_loaded, 16)
            sp.dma_start(rows1[C_PEK:C_PEK + CMP_LEN, 0:HEAD_DIM], cmp_pe_k[0]).then_inc(rows_loaded, 16)
            sp.dma_start(rows2[C_PEV:C_PEV + CMP_LEN, 0:HEAD_DIM], cmp_pe_v[0]).then_inc(rows_loaded, 16)
            sp.dma_start(rows2[0:C_PEV, :], ffn_conv_w[0].rearrange("k (r m) -> (k r) m", m=P128)).then_inc(rows_loaded, 16)
            def load_v(n):
                raw_free(n)
                for kk in range(2):
                    sp.dma_start(view(n % 2, 2)[:, kk, :], w_k[:, 2 * (n - N_V2) + kk, O_FV:O_FF]).then_inc(raw_loaded[n % 2], 16)

            load_v2(0, True)
            load_v2(1, False)
            load_v2(1, True)
            bias_v = (b_in[O_FV:O_FF], b_in[O_VS:O_KW], b_in[O_VW:O_NG], b_in[O_FF:O_CB], b_in[O_NG:O_NG + 3 * NSA_HEADS])
            o = 0
            for src in bias_v:
                n = src.shape[0]
                sp.dma_start(vb[:, o:o + n], src.rearrange("(a n) -> a n", a=1).to_broadcast([P128, n])).then_inc(small_loaded, 16)
                o += n
            raw_free(2)
            load_v2(2, False)
            load_v2(2, True)
            for n in range(N_V2, N_FOX):
                load_v(n)
            sp.wait_ge(consts, N_CONST)
            for g in range(2):
                sp.dma_start(w2k[:, g, 64 * g:64 * g + 64], cmp_w2_k[0]).then_inc(w1_loaded, 16)
            sp.dma_start(w2v[:, :], cmp_w2_v[0]).then_inc(w1_loaded, 16)
            sp.wait_ge(fe_step, 6)
            sp.dma_start(cum_dram, fe[:, :]).then_inc(cum_stored, 16)
            sp.wait_ge(cum_stored, 16)
            with sp.Fori(0, PAIRS) as i:
                n = N_FOX + 6 * i
                def load_w1(b):
                    for g in range(2):
                        for h in range(2):
                            sp.dma_start(w1[64 * g:64 * g + 64, b, ds(4 * i, 4), h, :],
                                         (cmp_w1_k, cmp_w1_v)[b][0].rearrange("(h r d) m -> h d r m", h=2, d=HEAD_DIM)[h, :, ds(4 * i, 4), :]) \
                                .then_inc(w1_loaded, 16)

                load8(n, 1, w_k, O_FQ + P128 * i)
                sp.wait_ge(masked, i + 1)
                sp.dma_start(f_bias[:, :, :], cum_dram[ds(2 * i, 2), :].rearrange("(o h) n -> o h n", o=1)
                             .to_broadcast([P128, 2, SEQ])).then_inc(fbias_loaded, 16)
                load8(n + 1, 0, w_k, O_FK + P128 * i)
                load8(n + 2, 1, w_k, O_CB + P128 * i)
                load8(n + 3, 0, w_k, O_CC + P128 * i)
                load_w1(0)
                load8(n + 4, 1, w_k, O_CX + P128 * i)
                load_w1(1)
                load8(n + 5, 0, w_k, O_KC + P128 * i + P128 * ((i + 1) // 4))
            for c in range(2):
                load8(N_CMP + c, (N_CMP + c) % 2, w_k, O_GC + P128 * (4 + c))
            with sp.Fori(0, PAIRS) as i:
                n = N_NSA + 8 * i
                load_nq(n, 1, i)
                load8(n + 1, 0, w_k, O_GA + 2 * P128 * i)
                load8(n + 2, 1, w_k, O_GB + 2 * P128 * i)
                load_ab(n + 3, 0, 2 * i)
                load8(n + 4, 1, w_k, O_GA + P128 + 2 * P128 * i)
                load8(n + 5, 0, w_k, O_GB + P128 + 2 * P128 * i)
                load_ab(n + 6, 1, 2 * i + 1)
                load8(n + 7, 0, w_k, O_GC + P128 * i)

            def load_yc(n, m):
                raw_free(n)
                for g in range(2):
                    sp.dma_start(view(n % 2, 4)[64 * g:64 * g + 64, :, :],
                                 w_br[2].rearrange("(g t d) n -> g d t n", g=2, d=HEAD_DIM)[g, :, :, P128 * m:P128 * (m + 2)]) \
                        .then_inc(raw_loaded[n % 2], 16)

            n = N_MIX
            for step in MIX_ORDER:
                if step[0] == "yc":
                    load_yc(n, step[1])
                else:
                    load8(n, n % 2, w_k, O_GC + P128 * step[1])
                n += 1
                if step == ("yc", 2):
                    sp.wait_ge(pv_done, 2 * PAIRS + 1)
                    for t in range(QT):
                        sp.dma_start(x_r[:, t, :], x_v[:, t, :]).then_inc(xr_loaded, 16)
            for m in range(KT):
                load8(n, n % 2, wo_k, P128 * m)
                n += 1
            with sp.Fori(0, FT) as i:
                load8(N_UP + 2 * i, 1, up_k, P128 * i)
                load8(N_UP + 2 * i + 1, 0, up_k, D_FF + P128 * i)

            def load_down(n, slot, j):
                raw_free(n)
                for h in range(2):
                    sp.dma_start(view(slot, 2)[:, h, :], w_down[ds(P128 * j, P128), BR_W * h:BR_W * h + BR_W]) \
                        .then_inc(raw_loaded[slot], 16)

            with sp.Fori(0, FT // 2) as i:
                load_down(N_DN + 2 * i, 1, 2 * i)
                load_down(N_DN + 2 * i + 1, 0, 2 * i + 1)
            sp.dma_start(g_out[:, :], norm_final_g.rearrange("(a n) -> a n", a=1).to_broadcast([P128, D_MODEL])).then_inc(g_loaded, 16)
            out_v = out[0].rearrange("(t p) n -> p t n", p=P128)
            for t in range(QT):
                sp.wait_ge(y_high, t + 1)
                sp.wait_ge(y_low, t + 1)
                sp.dma_start(out_v[:, t, :].rearrange("p (h n) -> p h n", h=2),
                             y_out[:, :, :].rearrange("p (h t) n -> p t h n", h=2)[:, t, :, :]).then_inc(y_stored, 16)
            sp.wait_ge(y_stored, 16 * QT)

        @block.gpsimd
        def _(pool):
            def split_lo(slot, n, wide=CH):
                pool.wait_ge(hi_split, n + 1)
                pool.tensor_tensor(w_lo[:, slot, 0:wide], raw[:, slot, 0:wide], w_hi[:, slot, 0:wide].bitcast(F), ALU.subtract) \
                    .then_inc(lo_split, 1)

            pool.memset(rows1[:, HEAD_DIM:P128], 0.0).then_inc(rows_zero, 1)
            pool.memset(rows2[:, HEAD_DIM:P128], 0.0).then_inc(rows_zero, 1)
            pool.memset(ident[:, :], 0.0).then_inc(consts, 1)
            pool.memset(ones[:, :], 1.0).then_inc(consts, 1)
            pool.wait_ge(consts, 1)
            pool.affine_select(out=ident[:, :], in_=ident[:, :], compare_op=ALU.not_equal, fill=1.0,
                               base=0, pattern=[[-1, P128]], channel_multiplier=1).then_inc(consts, 1)
            pool.memset(tri[:, :], 0.0).then_inc(consts, 1)
            pool.memset(f_one[:, :], 1.0).then_inc(consts, 1)
            pool.memset(c_mask[:, :, :, :], 1.0).then_inc(consts, 1)
            pool.iota(c_bias[:, :, :, :], [[-P128, QT], [0, 2], [CMP_STRIDE, CMP_LEN]], base=CMP_LEN - 1,
                      channel_multiplier=-1, allow_small_or_imprecise_dtypes=True).then_inc(consts, 1)
            pool.wait_ge(consts, 7)
            pool.affine_select(out=tri[:, :], in_=tri[:, :], compare_op=ALU.is_ge, fill=NEG,
                               base=0, pattern=[[-1, P128]], channel_multiplier=1).then_inc(consts, 1)
            pool.affine_select(out=c_mask[:, :, :, :], in_=c_mask[:, :, :, :], compare_op=ALU.is_ge, fill=0.0,
                               base=1 - CMP_LEN, pattern=[[P128, QT], [0, 2], [-CMP_STRIDE, CMP_LEN]],
                               channel_multiplier=1).then_inc(consts, 1)
            for a in range(2):
                pool.tensor_scalar(c_bias[:, :, a, :], c_bias[:, :, a, :], 0.5 ** (1 + 4 * a), None, ALU.mult).then_inc(consts, 1)
            pool.wait_ge(consts, 11)
            pool.affine_select(out=c_bias[:, :, :, :], in_=c_bias[:, :, :, :], compare_op=ALU.is_ge, fill=4 * NEG,
                               base=1 - CMP_LEN, pattern=[[P128, QT], [0, 2], [-CMP_STRIDE, CMP_LEN]],
                               channel_multiplier=1).then_inc(consts, 1)
            pool.memset(mx2[:, :, :, :], -3e38).then_inc(consts, 1)
            pool.memset(c_pad[:, QT:QT + 1, :, :], 0.0).then_inc(consts, 1)
            pool.memset(conv_t[:, 0:2], 0.0).then_inc(consts, 1)
            pool.memset(w2k[:, :, :], 0.0).then_inc(consts, 1)
            pool.memset(hid_v[:, :, :], 0.0).then_inc(consts, 1)
            def split_lo_v2(n):
                split_lo(n % 2, n, V2_W * (V2_K[n][1] - V2_K[n][0]))
            split_lo_v2(0)
            for t in (vp_hi, vp_lo):
                pool.memset(t[:, :, :, :].bitcast(F), 0.0).then_inc(consts, 1)
            split_lo_v2(1)
            pool.memset(vn_hi[:, :, :, :, :].bitcast(F), 0.0).then_inc(consts, 1)
            split_lo_v2(2)
            pool.memset(vn_lo[:, :, :, :, :].bitcast(F), 0.0).then_inc(consts, 1)
            for t in (vc_hi, vc_lo):
                pool.memset(t[:, :].bitcast(F), 0.0).then_inc(consts, 1)
            for n in range(N_V2, N_FOX + 1):
                split_lo(n % 2, n)

            pool.wait_ge(consts, N_CONST)
            with pool.Fori(0, PAIRS) as i:
                n = N_FOX + 6 * i
                split_lo(0, n + 1)
                split_lo(1, n + 2)
                pool.wait_ge(masked, i + 1)
                pool.wait_ge(fbias_loaded, 16 * i + 16)
                for a in range(2):
                    pool.tensor_tensor(f_diag[:, a, :, :], f_bias[:, a, :].rearrange("p (t m) -> p t m", m=P128),
                                       tri[:, :].rearrange("p (o m) -> p o m", o=1).to_broadcast([P128, QT, P128]), ALU.add) \
                        .then_inc(diag_ready, 1)
                split_lo(0, n + 3)
                pool.wait_ge(vf_lo, QT)
                pool.wait_ge(pv_done, i + 1)
                for dst, src in ((vp_hi, fv_hi), (vp_lo, fv_lo)):
                    for a in range(2):
                        pool.tensor_copy(dst[:, a, :, 64 * a:64 * a + 64],
                                         src[:, :, ds(P128 * i + 64 * a, 64)].bitcast(F)).then_inc(vpad, 1)
                split_lo(1, n + 4)
                split_lo(0, n + 5)
                split_lo(1, n + 6)
            assert N_NSA % 2 == 1 and N_END % 2 == 1
            for n in range(N_CMP + 1, N_NSA + 2):
                split_lo(n % 2, n)
            pool.wait_ge(masked, PAIRS + 1)
            pool.wait_ge(pv_done, PAIRS + 1)
            pool.wait_ge(conv_lo, PAIRS + 1)
            pool.wait_ge(cmp_done, 2)
            for a in range(2):
                pool.iota(alibi[:, a, :], [[1, SEQ]], base=P128 - SEQ, channel_multiplier=-1,
                          allow_small_or_imprecise_dtypes=True).then_inc(alibi_ready, 1)
            pool.wait_ge(alibi_ready, 2)
            pool.affine_select(out=alibi[:, :, :], in_=alibi[:, :, :], compare_op=ALU.is_ge, fill=64 * NEG,
                               base=SEQ - P128, pattern=[[0, 2], [-1, SEQ]], channel_multiplier=1).then_inc(alibi_ready, 1)
            with pool.Fori(0, (N_END - N_NSA - 2) // 2) as i:
                split_lo(1, N_NSA + 2 * i + 2)
                split_lo(0, N_NSA + 2 * i + 3)

        @block.tensor
        def _(pe):
            def mm3(out, w, r, first, last):
                pe.matmul(out, w[0], r[0], start=first, stop=False)
                pe.matmul(out, w[0], r[1], start=False, stop=False)
                return pe.matmul(out, w[1], r[0], start=False, stop=last)

            def wt(slot, k, k_tiles=KT, m=0):
                wide = CH // k_tiles
                o = k * wide + m
                return w_hi[:, slot, o:o + P128], w_lo[:, slot, o:o + P128]

            def project(slot, z, n, z_count, act=(h_hi, h_lo), ready=None):
                pe.wait_ge(z_free[z], z_count)
                pe.wait_ge(lo_split, n + 1)
                for k in range(KT):
                    if ready:
                        pe.wait_ge(ready, k + 1)
                    mm = mm3(Z[z][:, :], wt(slot, k), (act[0][:, k, :], act[1][:, k, :]), k == 0, k == KT - 1)
                mm.then_inc(tile_done, 1)

            def branch(slot, z, n, z_count, br, k0):
                pe.wait_ge(z_free[z], z_count)
                pe.wait_ge(lo_split, n + 1)
                for k in range(PAIRS):
                    mm = mm3(Z[z][:, :], wt(slot, k0 + k), (br_hi[:, br + k, :], br_lo[:, br + k, :]), k == 0, k == PAIRS - 1)
                mm.then_inc(tile_done, 1)

            def scores(kh, kl, pair):
                def qk(heads, i, place):
                    for part in range(3):
                        for a in heads:
                            rows, toks = slice(64 * a, 64 * a + 64), slice(P128 * i, P128 * i + P128)
                            bank, col = place[a]
                            mm = pe.matmul(S[bank][:, col:col + P_LEN[i]], (q_hi, q_hi, q_lo)[part][rows, toks],
                                           (kh, kl, kh)[part][rows, 0:P_LEN[i]], start=(part == 0), stop=(part == 2))
                            if part == 2 and i != 2:
                                mm.then_inc(a1_scored if heads == (0,) else scored, 1)
                qk((0,), 1, {0: (4, 0)})
                qk((0, 1), 3, {0: (0, 0), 1: (2, 0)})
                qk((0, 1), 2, {0: (1, 0), 1: (3, 0)})
                qk((0, 1), 0, {0: (1, P_LEN[2]), 1: (3, P_LEN[2])})
                pe.wait_ge(a1_scored, pair + 1)
                qk((1,), 1, {1: (4, P_LEN[1])})

            def transposes(pair):
                pe.wait_ge(normed, pair + 1)
                def pt(a, j, bank, col):
                    for i in range(j, QT):
                        mm = pe.transpose(S[bank][:, col + P128 * (i - j):col + P128 * (i - j + 1)],
                                          p_f[:, a, P_OFF[i] + P128 * j:P_OFF[i] + P128 * (j + 1)], ident[:, :])
                    return mm
                for a in range(2):
                    pt(a, 0, 2 * a, 0).then_inc(pt_ready, 1)
                    pt(a, 1, 2 * a + 1, 0)
                    pt(a, 3, 2 * a + 1, T_LEN[1]).then_inc(pt_ready, 1)
                pt(0, 2, 4, 0)
                pt(1, 2, 4, T_LEN[2]).then_inc(pt_ready, 1)

            def product(vh, vl, pair, first, last):
                pe.wait_ge(pt_lo_done, 5 * pair + 5 + 1)
                for a in range(2):
                    for j in range(QT):
                        o = T_OFF[j]
                        mm = mm3(O[:, P128 * j:SEQ], (vh[:, a, j, :], vl[:, a, j, :]),
                                 (pt_hi[:, a, o:o + T_LEN[j]], pt_lo[:, a, o:o + T_LEN[j]]),
                                 first and a == 0 and j == 0, last and a == 1 and j == QT - 1)
                return mm

            for done in (pv_done, c_t):
                pe.sem_inc(done, 1)
            def x_tile(k, t):
                return pe.transpose(x_bank[k][:, P128 * t:P128 * t + P128], x_n[:, t, P128 * k:P128 * k + P128], ident[:, :])

            pe.wait_ge(consts, 3)
            for t in range(QT):
                pe.wait_ge(x_normed, t + 1)
                for k in range(KT - 1):
                    mm = x_tile(k, t)
                    if t == QT - 1:
                        mm.then_inc(x_t, 1)
            pe.wait_ge(rows_loaded, 16 * 12)
            pe.transpose(Z[1][:, 0:N_COLS1], rows1[:, :], ident[0:N_COLS1, 0:N_COLS1])
            pe.transpose(Z[1][:, P128:P128 + N_COLS2], rows2[:, :], ident[0:N_COLS2, 0:N_COLS2]).then_inc(cols_t, 1)
            pe.wait_ge(cols_ready, 2)
            for t in range(QT):
                mm = x_tile(KT - 1, t)
            mm.then_inc(x_t, 1)
            for n, (k0, k1) in enumerate(V2_K):
                pe.wait_ge(lo_split, n + 1)
                for k in range(k0, k1):
                    if k:
                        pe.wait_ge(h_lo_done, max(k + 1, QT))
                    o = V2_W * (k - k0)
                    w = [p[:, n % 2, o:o + V2_W] for p in (w_hi, w_lo)]
                    for t in range(QT):
                        if k == 0:
                            pe.wait_ge(h_lo_done, t + 1)
                        toks = slice(P128 * t, P128 * t + P128)
                        mm = mm3(v2_bank[t][:, 0:V2_W], (h_hi[:, k, toks], h_lo[:, k, toks]), w, k == 0, k == KT - 1)
                mm.then_inc(tile_done, 1)
            for n in range(N_V2, N_FOX):
                pe.wait_ge(lo_split, n + 1)
                for kk in range(2):
                    k = 2 * (n - N_V2) + kk
                    w = [p[:, n % 2, BR_W * kk:BR_W * kk + BR_W] for p in (w_hi, w_lo)]
                    for t in range(QT):
                        if k == 0 and t == QT - 1:
                            pe.wait_ge(v2_ready, 1)
                        toks = slice(P128 * t, P128 * t + P128)
                        mm = mm3(S[t][:, :], (h_hi[:, k, toks], h_lo[:, k, toks]), w, k == 0, k == KT - 1)
                mm.then_inc(tile_done, 1)
                if n == N_V2:
                    pe.wait_ge(lg_ready, QT)
                    for t in range(QT):
                        mm = pe.transpose(Z[1][0:32, P128 * t:P128 * t + P128], lg_t[:, t, :], ident[:, :])
                    mm.then_inc(fg_t, 1)

            with pe.Fori(0, PAIRS) as i:
                n, z = N_FOX + 6 * i, 3 * i
                project(1, 0, n, Z_FOX[0] + z)
                project(0, 1, n + 1, Z_FOX[1] + z)
                project(1, 0, n + 2, Z_FOX[0] + z + 1)
                pe.wait_ge(z_free[1], Z_FOX[1] + z + 1)
                pe.wait_ge(vf_ready, QT)
                pe.wait_ge(v2_ready, 3)
                pe.wait_ge(pt_lo_done, 5 * i + 1)
                scores(k_hi, k_lo, i)
                project(0, 1, n + 3, Z_FOX[1] + z + 1)
                project(1, 0, n + 4, Z_FOX[0] + z + 2)
                transposes(i)
                project(0, 1, n + 5, Z_FOX[1] + z + 2)
                pe.wait_ge(vpad, 4 * i + 4)
                pe.wait_ge(o_lo_done, i + 1)
                product(vp_hi, vp_lo, i, True, True).then_inc(pv_done, 1)

            project(N_CMP % 2, 0, N_CMP, Z_CMP[0])
            pe.wait_ge(w1_loaded, 16 * (3 + 8 * PAIRS))
            for b in range(2):
                pe.wait_ge(cz_ready, 3 * b + 3)
                for r in range(CMP_STRIDE):
                    mm = pe.matmul(S[b][0:CZ_W, 0:P128], cz[:, b, r, :], w1[:, b, r, :, :].rearrange("p h m -> p (h m)"),
                                   start=(r == 0), stop=(r == CMP_STRIDE - 1))
                mm.then_inc(hid_done, 1)
            pe.wait_ge(sel_ready, 2)
            for b in range(2):
                pe.wait_ge(hid_ready, b + 1)
                for h in range(2):
                    mm = pe.matmul(S[2 + b][0:64, 0:2 * N_BLK], hid_f[:, b, h, :], sel[:, h, :], start=(h == 0), stop=(h == 1))
                mm.then_inc(hid_sum, 1)
            project((N_CMP + 1) % 2, 1, N_CMP + 1, Z_CMP[1])
            pe.wait_ge(gelu_done, 1)
            for g in range(2):
                mm = pe.matmul(S[4][:, N_BLK * g:N_BLK * g + N_BLK], w2k[:, g, :], hid_k[:, N_BLK * g:N_BLK * g + N_BLK],
                               start=True, stop=True)
            mm.then_inc(cmp_done, 1)
            pe.wait_ge(gelu_done, 3)
            for g in range(2):
                mm = pe.matmul(O[0:64, 64 * g:64 * g + 64], hid_v[:, g, :], w2v[:, :], start=True, stop=True)
            mm.then_inc(cmp_done, 1)

            with pe.Fori(0, PAIRS) as i:
                n, z = N_NSA + 8 * i, 5 * i
                z0, z1 = Z_NSA[0] + z, Z_NSA[1] + z
                project(1, 0, n, z0)
                project(0, 1, n + 1, z1)
                pe.wait_ge(z_free[0], z0 + 1)
                pe.wait_ge(pt_lo_done, 5 * (PAIRS + 2 * i) + 1)
                pe.wait_ge(o_lo_done, PAIRS + i + 1)

                pe.wait_ge(cmp_lo, 2)
                scores(nk_hi[:, 2, :], nk_lo[:, 2, :], PAIRS + 2 * i)
                for t in range(QT):
                    toks = slice(P128 * t, P128 * t + P128)
                    mm = mm3(O[:, 64 * t:64 * t + 64], (q_hi[:, toks], q_lo[:, toks]), (kc_hi[:, :], kc_lo[:, :]), True, True)
                mm.then_inc(c_scored, 1)
                project(1, 0, n + 2, z0 + 1)
                branch(0, 1, n + 3, z1 + 1, 0, 0)
                branch(0, 0, n + 3, z0 + 2, PAIRS, 4)
                transposes(PAIRS + 2 * i)
                pe.wait_ge(consts, N_CONST)
                pe.wait_ge(c_ready, i + 1)
                for t in range(QT):
                    mm = pe.transpose(O[:, P128 * t:P128 * t + P128],
                                      c_pad[:, t:t + 2, :, :].rearrange("p t a c -> p (t a c)"), ident[:, :])
                mm.then_inc(c_t, 1)
                project(1, 1, n + 4, z1 + 2)
                pe.wait_ge(c_t_lo, i + 1)
                mm3(O[:, :], (vc_hi[:, :], vc_lo[:, :]), (c_pt_hi[:, :], c_pt_lo[:, :]), True, False)
                product(vn_hi[:, 0, :, :, :], vn_lo[:, 0, :, :, :], PAIRS + 2 * i, False, False).then_inc(pv_s_done, 1)
                scores(nk_hi[:, 3, :], nk_lo[:, 3, :], PAIRS + 2 * i + 1)
                project(0, 0, n + 5, z0 + 3)
                branch(1, 1, n + 6, z1 + 3, 0, 0)
                branch(1, 0, n + 6, z0 + 4, PAIRS, 4)
                transposes(PAIRS + 2 * i + 1)
                project(0, 1, n + 7, z1 + 4)
                product(vn_hi[:, 1, :, :, :], vn_lo[:, 1, :, :, :], PAIRS + 2 * i + 1, False, True).then_inc(pv_done, 1)

            n, tau = N_MIX, 0
            for kind, m in MIX_ORDER:
                if kind == "gc":
                    project(n % 2, tau % 2, n, Z_MIX[tau % 2] + tau // 2)
                    tau += 1
                else:
                    pe.wait_ge(lo_split, n + 1)
                    pe.wait_ge(o_lo_done, 2 * PAIRS + 1)
                    for mt in range(2):
                        pe.wait_ge(z_free[tau % 2], Z_MIX[tau % 2] + tau // 2)
                        for k in range(PAIRS):
                            mm = mm3(Z[tau % 2][:, :], wt(n % 2, k, 4, P128 * mt), (c_hi[:, k, :], c_lo[:, k, :]),
                                     k == 0, k == PAIRS - 1)
                        mm.then_inc(tile_done, 1)
                        tau += 1
                n += 1
            pe.wait_ge(xr_loaded, 16 * QT)
            for m in range(KT):
                if m >= 4:
                    pe.wait_ge(xr_copied, m - 3)
                for t in range(QT):
                    mm = pe.transpose(S[m % 4][:, P128 * t:P128 * t + P128], x_r[:, t, P128 * m:P128 * m + P128], ident[:, :])
                mm.then_inc(xr_t, 1)
                project((N_WO + m) % 2, m % 2, N_WO + m, Z_WO[m % 2] + m // 2, (br_hi, br_lo),
                        None if m else mix_lo)
            project(1, 0, N_UP, Z_UP[0], ready=xg_lo)
            pe.wait_ge(acc_done, KT)
            pe.matmul(S[4][:, :], ones[:, :], x_acc[:, :], start=True, stop=True).then_inc(ss_done, 1)
            project(0, 1, N_UP + 1, Z_UP[1])
            with pe.Fori(1, FT) as i:
                project(1, 0, N_UP + 2 * i, Z_UP[0] + i)
                project(0, 1, N_UP + 2 * i + 1, Z_UP[1] + i)

            def down(slot, n, j, first, last):
                pe.wait_ge(lo_split, n + 1)
                pe.wait_ge(act_lo_done, j + 1 + 1)
                act = (act_hi[:, j, :], act_lo[:, j, :])
                for m in range(KT):
                    if first and m >= 6:
                        pe.wait_ge(z_free[m - 6], Z_UP[m - 6] + FT)
                    mm = mm3(banks[m][:, :], wt(slot, m), act, first, last)
                mm.then_inc(tile_done, 1)

            down(1, N_DN, 0, True, False)
            down(0, N_DN + 1, 1, False, False)
            with pe.Fori(1, FT // 2 - 1) as i:
                down(1, N_DN + 2 * i, 2 * i, False, False)
                down(0, N_DN + 2 * i + 1, 2 * i + 1, False, False)
            down(1, N_DN + FT - 2, FT - 2, False, False)

            def back(m, t):
                return pe.transpose(banks[QT * (m // 4) + t][:, P128 * (m % 4):P128 * (m % 4) + P128],
                                    x2[:, m, P128 * t:P128 * t + P128], ident[:, :])

            pe.wait_ge(lo_split, N_END)
            pe.wait_ge(act_lo_done, FT + 1)
            for m in range(KT):
                mm3(banks[m][:, :], wt((N_END - 1) % 2, m), (act_hi[:, FT - 1, :], act_lo[:, FT - 1, :]), False, True).then_inc(down_done, 1)
                if m == 5:
                    pe.wait_ge(x3_done, 4)
                    for t in range(QT):
                        for k in range(4):
                            mm = back(k, t)
                        mm.then_inc(x3_t, 1)
            pe.wait_ge(x3_done, KT - 1)
            for t in range(QT - 1):
                for m in range(4, KT - 1):
                    back(m, t)
            pe.wait_ge(x3_done, KT)
            for t in range(QT - 1):
                back(KT - 1, t).then_inc(x3_t, 1)
            for m in range(4, KT):
                mm = back(m, QT - 1)
            mm.then_inc(x3_t, 1)

        @block.scalar
        def _(act):
            def split_hi(slot, n, tiles):
                act.wait_ge(raw_loaded[slot], 32 * (n // 2) + 32)
                wide = CH
                if n < N_V2:
                    act.wait_ge(lg_loaded[n], 32)
                    wide = V2_W * (V2_K[n][1] - V2_K[n][0])
                if tiles:
                    act.wait_ge(tile_done, tiles)
                act.activation(w_hi[:, slot, 0:wide], raw[:, slot, 0:wide], ACT.Copy).then_inc(hi_split, 1)

            def split_hi_in_loop(slot, loads, tiles):
                act.wait_ge(raw_loaded[slot], 32 * loads)
                act.wait_ge(tile_done, tiles)
                act.activation(w_hi[:, slot, :], raw[:, slot, :], ACT.Copy).then_inc(hi_split, 1)

            def evac_hi(dst, src, done, bias=0.0):
                act.activation(dst, src, ACT.Identity, bias=bias).then_inc(done, 1)

            def exponentials(pair):
                act.wait_ge(neg_ready, pair + 1)
                for a in range(2):
                    for i in range(QT):
                        t = p_f[:, a, P_OFF[i]:P_OFF[i] + P_LEN[i]]
                        act.activation(t, t, ACT.Exp, bias=neg_mx[:, a, i:i + 1], accum_out=p_sum[:, a, i:i + 1]).then_inc(exp_done, 1)

            def pt_high(pair):
                for b in range(5):
                    act.wait_ge(pt_ready, 5 * pair + b + 1)
                    dst, src = pt_part(pt_hi, b)
                    act.activation(dst, src, ACT.Copy).then_inc(pt_hi_done, 1)

            act.wait_ge(eps_ready, 1)
            act.activation(act_cell[:, 0:1], eps_c[:, :], ACT.Sqrt)
            for t in range(QT):
                act.wait_ge(x_loaded[t], 16)
                act.activation(x_n[:, t, :], x_in[:, t, :], ACT.Square, accum_out=stat[:, 0, t:t + 1]).then_inc(x_ss, 1)
                act.wait_ge(x_ss, t + 1)
                act.activation(stat[:, 2, t:t + 1], stat[:, 0, t:t + 1], ACT.Sqrt, bias=eps_c[:, :], scale=1.0 / D_MODEL).then_inc(x_sqrt, 1)
            split_hi(0, 0, 0)
            act.wait_ge(cols_ready, 2)
            for k in range(KT):
                act.wait_ge(x_t, k + 1)
                act.activation(h_hi[:, k, :], x_bank[k][:, :], ACT.Copy, scale=cols1[:, C_GMIX + k:C_GMIX + k + 1]).then_inc(h_hi_done, 1)
                if k == 4:
                    split_hi(1, 1, 0)
            split_hi(0, 2, 1)
            split_hi(1, 3, 2)
            split_hi(0, 4, 3)
            act.wait_ge(v2_ready, 3)
            act.wait_ge(z_free[0], 1)
            act.wait_ge(consts, N_CONST)
            for a in range(2):
                act.activation(vn_hi[:, :, a, :, 64 * a:64 * a + 64],
                               v2_f[:, :, :, 64 * a:64 * a + 64].rearrange("p t b d -> p b t d"), ACT.Copy).then_inc(v2_hi, 1)
            act.wait_ge(fg_t, 1)
            act.activation(fg[:, :], Z[1][0:FOX_HEADS, :], ACT.Copy).then_inc(z_free[1], 1)
            act.activation(lg_t[:, :, FOX_HEADS:], lg_t[:, :, FOX_HEADS:], ACT.Tanh, scale=0.5).then_inc(ng_tanh, 1)
            split_hi(1, 5, 4)
            act.wait_ge(fe_step, 1)
            act.activation(fe[:, :], fe[:, :], ACT.Exp).then_inc(fe_step, 1)
            act.wait_ge(fe_step, 2)
            act.activation(fe[:, :], fe[:, :], ACT.Ln, bias=1.0).then_inc(fe_step, 1)
            split_hi(0, 6, 5)
            split_hi(1, 7, 6)
            split_hi(0, 8, N_FOX)
            act.activation(act_cell[:, 5:6], eps_c[:, :], ACT.Exp)
            for t in range(QT):
                act.wait_ge(vf_ready, t + 1)
                act.activation(fv_hi[:, t, :], v_f[:, t, :], ACT.Copy).then_inc(vf_hi, 1)

            with act.Fori(0, PAIRS) as i:
                T, L = T_FOX + 6 * i, 3 * i
                act.wait_ge(tile_done, T + 1)
                evac_hi(q_hi[:, :], Z[0][:, :], q_hi_done, cols1[:, ds(C_FQ + i, 1)])
                split_hi_in_loop(1, L + 5, T + 1)
                act.wait_ge(tile_done, T + 2)
                evac_hi(k_hi[:, :], Z[1][:, :], k_hi_done, cols1[:, ds(C_FK + i, 1)])
                split_hi_in_loop(0, L + 6, T + 2)
                act.wait_ge(conv_step, 3 * i + 1)
                act.wait_ge(tile_done, T + 3)
                act.activation(conv_b[:, :], Z[0][:, :], ACT.Identity, bias=cols1[:, ds(C_CB + i, 1)]).then_inc(z_free[0], 1)
                split_hi_in_loop(1, L + 6, T + 3)
                exponentials(i)
                act.wait_ge(tile_done, T + 4)
                act.wait_ge(conv_lo, i + 1)
                act.activation(conv_c[:, :], Z[1][:, :], ACT.Identity, bias=cols1[:, ds(C_CC + i, 1)]).then_inc(z_free[1], 1)
                split_hi_in_loop(0, L + 7, T + 4)
                split_hi_in_loop(1, L + 7, T + 5)
                pt_high(i)
                act.wait_ge(conv_t_done, i + 1)
                act.activation(conv_u[:, :], conv_t[:, 2:SEQ + 2], ACT.Copy, scale=cols1[:, ds(C_SC + 8 + i, 1)]).then_inc(conv_w2, 1)
                act.wait_ge(tile_done, T + 6)
                evac_hi(nk_hi[:, i, :], Z[1][:, :], nk_hi_done, cols1[:, ds(C_NK + i, 1)])
                split_hi_in_loop(0, L + 8, T + 6)
                act.wait_ge(conv_step, 3 * i + 3 + 1)
                act.activation(br_hi[:, PAIRS + i, :], conv_c[:, :], ACT.Copy).then_inc(conv_hi, 1)
                act.wait_ge(pv_done, i + 1 + 1)
                act.activation(br_hi[:, i, :], O[:, :], ACT.Copy).then_inc(o_hi_done, 1)

            def gate_c(m, z, tiles):
                act.wait_ge(tile_done, tiles)
                act.activation(g_c[:, m, :], Z[z][:, :], ACT.Tanh, bias=half_b[:, 16 + m:17 + m], scale=0.5).then_inc(z_free[z], 1)

            act.wait_ge(vpad, 4 * PAIRS)
            gate_c(4, 0, T_CMP + 1)
            split_hi(N_NSA % 2, N_NSA, T_CMP + 1)
            act.activation(act_cell[:, 1:2], eps_c[:, :], ACT.Gelu_apprx_tanh)
            for b, dst in enumerate(([(hid_k[:, :], slice(0, 2 * N_BLK))],
                                     [(hid_v[:, g, N_BLK * g:N_BLK * g + N_BLK], slice(N_BLK * g, N_BLK * g + N_BLK)) for g in range(2)])):
                act.wait_ge(hid_sum, b + 1)
                for d, cols in dst:
                    act.activation(d, S[2 + b][0:64, cols], ACT.Gelu_apprx_tanh).then_inc(gelu_done, 1)
            act.activation(act_cell[:, 2:3], eps_c[:, :], ACT.Exp)
            gate_c(5, 1, T_CMP + 2)
            act.wait_ge(cmp_done, 1)
            act.activation(kc_hi[:, :], S[4][:, 0:2 * N_BLK], ACT.Copy).then_inc(cmp_hi, 1)
            act.wait_ge(cmp_done, 2)
            act.activation(vc_hi[:, :], O[0:64, 0:P128], ACT.Copy).then_inc(cmp_hi, 1)
            with act.Fori(0, PAIRS) as i:
                T, L = T_NSA + 10 * i, 4 * i + N_NSA // 2
                z0, z1 = Z_NSA[0] + 5 * i, Z_NSA[1] + 5 * i
                split_hi_in_loop(0, L + 2, T)
                act.wait_ge(tile_done, T + 1)
                evac_hi(q_hi[:, :], Z[0][:, :], q_hi_done, cols1[:, ds(C_NQ + i, 1)])
                split_hi_in_loop(1, L + 2, T + 1)

                def tanh_gate(dst, z, col):
                    act.activation(dst, Z[z][:, :], ACT.Tanh, bias=half_b[:, col], scale=0.5).then_inc(z_free[z], 1)

                act.wait_ge(z_free[1], z1 - 1)
                act.wait_ge(tile_done, T + 2)
                tanh_gate(g_a[:, :], 1, ds(2 * i, 1))
                split_hi_in_loop(0, L + 3, T + 2)
                exponentials(PAIRS + 2 * i)
                act.wait_ge(c_step, 5 * i + 3)
                act.activation(c_p[:, :, :, :], c_p[:, :, :, :], ACT.Exp).then_inc(c_exp, 1)
                act.wait_ge(gb_used, 2 * i + 1)
                act.wait_ge(tile_done, T + 3)
                tanh_gate(g_b[:, :], 0, ds(8 + 2 * i, 1))
                split_hi_in_loop(1, L + 3, T + 3)
                split_hi_in_loop(0, L + 4, T + 5)
                pt_high(PAIRS + 2 * i)
                act.wait_ge(c_t, i + 1 + 1)
                act.activation(c_pt_hi[:, :], O[0:64, :], ACT.Copy).then_inc(c_t_hi, 1)
                act.wait_ge(z_free[1], z1 + 2)
                act.wait_ge(tile_done, T + 6)
                tanh_gate(g_a[:, :], 1, ds(2 * i + 1, 1))
                split_hi_in_loop(1, L + 4, T + 6)
                exponentials(PAIRS + 2 * i + 1)
                act.wait_ge(gb_used, 2 * i + 1 + 1)
                act.wait_ge(tile_done, T + 7)
                tanh_gate(g_b[:, :], 0, ds(8 + 2 * i + 1, 1))
                split_hi_in_loop(0, L + 5, T + 7)
                split_hi_in_loop(1, L + 5, T + 9)
                pt_high(PAIRS + 2 * i + 1)
                act.wait_ge(tile_done, T + 10)
                tanh_gate(g_c[:, i, :], 1, ds(16 + i, 1))
                act.wait_ge(pv_done, PAIRS + i + 1 + 1)
                act.activation(c_hi[:, i, :], O[:, :], ACT.Copy).then_inc(o_hi_done, 1)

            def mix_high(m):
                act.wait_ge(mix_done, m + 1)
                act.activation(br_hi[:, m, :], mix[:, m, :], ACT.Copy, scale=0.5).then_inc(mix_hi, 1)

            n, tau = N_MIX, 0
            pending = []
            for kind, m in MIX_ORDER:
                split_hi((n + 1) % 2, n + 1, T_MIX + tau)
                for mt in pending:
                    mix_high(mt)
                pending = []
                if kind == "gc":
                    gate_c(m, tau % 2, T_MIX + tau + 1)
                    tau += 1
                else:
                    tau += 2
                    pending = [m, m + 1]
                n += 1
            for mt in pending:
                mix_high(mt)
            for m in range(KT):
                split_hi((N_WO + m + 1) % 2, N_WO + m + 1, T_WO + m)
                act.wait_ge(xr_t, m + 1)
                act.activation(x2[:, m, :], S[m % 4][:, :], ACT.Copy).then_inc(xr_copied, 1)
                act.wait_ge(z_free[m % 2], Z_WO[m % 2] + m // 2 + 1)
                act.activation(h_hi[:, m, :], x2[:, m, :], ACT.Copy, scale=cols1[:, C_GFFN + m:C_GFFN + m + 1]).then_inc(xg_hi, 1)
            split_hi((N_UP + 1) % 2, N_UP + 1, T_UP)
            act.wait_ge(ss_done, 1)
            act.activation(rstd[:, :], S[4][:, :], ACT.Sqrt, bias=eps_c[:, :], scale=1.0 / D_MODEL).then_inc(rs_sqrt, 1)

            act.activation(act_cell[:, 3:4], eps_c[:, :], ACT.Silu)
            with act.Fori(0, FT) as i:
                T, L = T_UP + 2 * i, i + N_UP // 2
                split_hi_in_loop(1, L + 2, T + 1)
                act.wait_ge(u_ready, i + 1)
                act.wait_ge(act_lo_done, i + 1)
                act.activation(u_c[:, :], u_t[:, 2:SEQ + 2], ACT.Copy, scale=cols2[:, ds(C_FFN + 2 * FT + i, 1)]).then_inc(u_w2, 1)
                act.wait_ge(u_step, 2 * i + 2 + 1)
                act.activation(u_c[:, :], u_c[:, :], ACT.Silu).then_inc(u_silu, 1)
                split_hi_in_loop(0, L + 3, T + 2)
                act.wait_ge(uv_done, i + 1)
                act.activation(act_hi[:, i, :], u_c[:, :], ACT.Copy).then_inc(act_hi_done, 1)
            T, L = T_DN, N_DN // 2
            with act.Fori(0, FT // 2 - 1) as i:
                split_hi_in_loop(1, L + i + 2, T + 2 * i + 1)
                split_hi_in_loop(0, L + i + 3, T + 2 * i + 2)
            act.activation(act_cell[:, 4:5], eps_c[:, :], ACT.Sqrt)
            def square(n):
                act.wait_ge(x3_t, n + 1)
                act.activation(y_sq[:, n, :], banks[n][:, :], ACT.Square, accum_out=stat[:, n // QT, n % QT:n % QT + 1]).then_inc(y_sqd, 1)

            def root(t):
                act.wait_ge(y_ms, t + 1)
                act.activation(stat[:, 2, t:t + 1], stat[:, 2, t:t + 1], ACT.Sqrt, bias=eps_c[:, :], scale=1.0 / D_MODEL).then_inc(y_sqrt, 1)

            for n in range(QT + 1):
                square(n)
            for n in range(QT + 1, 2 * QT):
                square(n)
                root(n - QT - 1)
            root(QT - 1)
            act.wait_ge(y_gained, QT)
            act.wait_ge(y_low, 1)
            for t in range(1, QT):
                act.wait_ge(y_rs, t + 1)
                act.activation(y_out[:, t, :], y_out[:, t, :], ACT.Copy, scale=stat[:, 3, t:t + 1]).then_inc(y_low, 1)

        @block.vector
        def _(dve):
            def sub_lo(dst, src, bias, hi, done):
                dve.scalar_tensor_tensor(dst, src, bias, hi.bitcast(F), ALU.add, ALU.subtract).then_inc(done, 1)

            def pt_low(pair):
                for b in range(5):
                    dve.wait_ge(pt_hi_done, 5 * pair + b + 1)
                    if b == 0:
                        dve.wait_ge(pt_ready, 5 * pair + 5)
                    dst, src = pt_part(pt_lo, b)
                    hi, _ = pt_part(pt_hi, b)
                    dve.tensor_tensor(dst, src, hi.bitcast(F), ALU.subtract).then_inc(pt_lo_done, 1)

            score_at = {(0, 3): (0, 0, 1), (1, 3): (2, 0, 2), (0, 2): (1, 0, 3), (0, 0): (1, P_LEN[2], 3),
                        (1, 2): (3, 0, 4), (1, 0): (3, P_LEN[2], 4), (0, 1): (4, 0, 5), (1, 1): (4, P_LEN[1], 5)}

            def mask_tile(a, i, k0, k1, bias, top):
                bank, col, _ = score_at[a, i]
                return dve.tensor_tensor_reduce(p_f[:, a, P_OFF[i] + k0:P_OFF[i] + k1], S[bank][:, col + k0:col + k1],
                                                bias, SCALE, -3e38, ALU.add, ALU.max, top)

            def wait_scores(pair, a, i):
                n = score_at[a, i][2]
                if (a, i) in ((0, 3), (0, 2), (1, 3), (1, 2), (0, 1)):
                    dve.wait_ge(scored, 5 * pair + n)
                    dve.memset(wait_cell[:, n - 1:n], 0.0)

            def invert(pair):
                dve.wait_ge(exp_done, 8 * pair + 8)
                dve.reciprocal(p_inv[:, :, :], p_sum[:, :, :]).then_inc(inv_ready, 1)

            def normalise(pair):
                for a in range(2):
                    for i in range(QT):
                        t = p_f[:, a, P_OFF[i]:P_OFF[i] + P_LEN[i]]
                        op = dve.tensor_scalar(t, t, p_inv[:, a, i:i + 1], None, ALU.mult)
                op.then_inc(normed, 1)

            for done in (pt_lo_done, o_lo_done, masked, conv_step, conv_lo, gb_used, act_lo_done, u_step):
                dve.sem_inc(done, 1)
            dve.memset(eps_c[:, :], EPS).then_inc(eps_ready, 1)
            for t in range(QT):
                dve.wait_ge(x_sqrt, t + 1)
                dve.reciprocal(stat[:, 3, t:t + 1], stat[:, 2, t:t + 1]).then_inc(x_rs, 1)
                dve.wait_ge(x_rs, t + 1)
                dve.tensor_scalar(x_n[:, t, :], x_in[:, t, :], stat[:, 3, t:t + 1], None, ALU.mult).then_inc(x_normed, 1)
            dve.wait_ge(cols_t, 1)
            dve.tensor_copy(cols1[:, :], Z[1][:, 0:N_COLS1]).then_inc(cols_ready, 1)
            dve.tensor_copy(cols2[:, :], Z[1][:, P128:P128 + N_COLS2]).then_inc(cols_ready, 1)
            dve.wait_ge(cols_ready, 1)
            dve.tensor_scalar(half_b[:, :], cols1[:, C_GATE:C_GATE + 24], 0.5, None, ALU.mult)
            for k in range(KT):
                dve.wait_ge(h_hi_done, k + 1)
                dve.scalar_tensor_tensor(h_lo[:, k, :], x_bank[k][:, :], cols1[:, C_GMIX + k:C_GMIX + k + 1],
                                         h_hi[:, k, :].bitcast(F), ALU.mult, ALU.subtract).then_inc(h_lo_done, 1)
            dve.wait_ge(small_loaded, 16 * 5)
            dve.wait_ge(tile_done, N_V2)
            for t in (3, 0, 1, 2):
                dve.tensor_tensor(lg_t[:, t, :], v2_bank[t][:, V2_V:V2_W], vb[:, BR_W + V2_V:BR_W + V2_W], ALU.add).then_inc(lg_ready, 1)
                dve.tensor_tensor(v2_f[:, t, :, :].rearrange("p b d -> p (b d)"), v2_bank[t][:, 0:V2_V], vb[:, BR_W:BR_W + V2_V], ALU.add) \
                    .then_inc(z_free[0] if t == 2 else v2_ready, 1)
            dve.wait_ge(z_free[1], 1)
            dve.scalar_tensor_tensor(fe[:, :], fg[:, :], -1.0, fg[:, :], ALU.mult, ALU.min).then_inc(fe_step, 1)
            dve.wait_ge(v2_ready, 3)
            dve.wait_ge(z_free[0], 1)
            for a in range(2):
                dve.wait_ge(v2_hi, a + 1)
                dve.tensor_tensor(vn_lo[:, :, a, :, 64 * a:64 * a + 64],
                                  v2_f[:, :, :, 64 * a:64 * a + 64].rearrange("p t b d -> p b t d"),
                                  vn_hi[:, :, a, :, 64 * a:64 * a + 64].bitcast(F), ALU.subtract).then_inc(v2_lo, 1)
            dve.wait_ge(ng_tanh, 1)
            dve.tensor_scalar(gates[:, :, :, :], lg_t[:, :, FOX_HEADS:].rearrange("p t (h b) -> p b h t", b=3),
                              0.5, 0.5, ALU.mult, ALU.add).then_inc(gates_ready, 1)
            dve.wait_ge(fe_step, 3)
            dve.scalar_tensor_tensor(fe[:, :], fg[:, :], 0.0, fe[:, :], ALU.min, ALU.subtract).then_inc(fe_step, 1)
            dve.wait_ge(consts, 5)
            dve.wait_ge(fe_step, 4)
            dve.tensor_tensor_scan(fe[:, :], f_one[:, :], fe[:, :], 0.0, ALU.mult, ALU.add).then_inc(fe_step, 1)
            dve.wait_ge(fe_step, 5)
            dve.tensor_scalar(fe[:, :], fe[:, :], -1.0 / SCALE, None, ALU.mult).then_inc(fe_step, 1)
            dve.wait_ge(tile_done, N_FOX)
            for t in range(QT):
                dve.tensor_tensor(v_f[:, t, :], S[t][:, :], vb[:, 0:BR_W], ALU.add).then_inc(vf_ready, 1)
            for t in range(QT):
                dve.wait_ge(vf_hi, t + 1)
                dve.tensor_tensor(fv_lo[:, t, :], v_f[:, t, :], fv_hi[:, t, :].bitcast(F), ALU.subtract).then_inc(vf_lo, 1)

            with dve.Fori(0, PAIRS) as i:
                T = T_FOX + 6 * i
                dve.wait_ge(q_hi_done, i + 1)
                sub_lo(q_lo[:, :], Z[0][:, :], cols1[:, ds(C_FQ + i, 1)], q_hi[:, :], z_free[0])
                dve.wait_ge(k_hi_done, i + 1)
                sub_lo(k_lo[:, :], Z[1][:, :], cols1[:, ds(C_FK + i, 1)], k_hi[:, :], z_free[1])
                dve.wait_ge(diag_ready, 2 * i + 2)
                dve.wait_ge(consts, N_CONST)
                for a, t in score_at:
                    wait_scores(i, a, t)
                    k = P128 * t
                    op = mask_tile(a, t, k, k + P128, f_diag[:, a, t, :], mx2[:, a, t, 0:1])
                    if t:
                        op = mask_tile(a, t, 0, k, f_bias[:, a, 0:k], mx2[:, a, t, 1:2])
                op.then_inc(masked, 1)
                dve.wait_ge(masked, i + 1 + 1)
                dve.tensor_reduce(mx[:, :, :], mx2[:, :, :, :], AX.X, ALU.max).then_inc(neg_pre, 1)
                dve.wait_ge(neg_pre, i + 1)
                dve.tensor_scalar(neg_mx[:, :, :], mx[:, :, :], -1.0, None, ALU.mult).then_inc(neg_ready, 1)
                invert(i)
                dve.wait_ge(inv_ready, i + 1)
                normalise(i)
                dve.wait_ge(tile_done, T + 5)
                dve.wait_ge(z_free[1], Z_FOX[1] + 3 * i + 2)
                dve.scalar_tensor_tensor(conv_t[:, 2:SEQ + 2], Z[0][:, :], cols1[:, ds(C_CX + i, 1)], conv_c[:, :],
                                         ALU.add, ALU.mult).then_inc(z_free[0], 1)
                dve.wait_ge(z_free[0], Z_FOX[0] + 3 * i + 3)
                dve.memset(conv_t[:, 0:2], 0.0).then_inc(conv_t_done, 1)
                pt_low(i)
                dve.wait_ge(conv_w2, i + 1)
                for tap in (1, 0):
                    dve.scalar_tensor_tensor(conv_u[:, :], conv_t[:, tap:SEQ + tap], cols1[:, ds(C_SC + 4 * tap + i, 1)], conv_u[:, :],
                                             ALU.mult, ALU.add).then_inc(conv_step, 1)
                    dve.wait_ge(conv_step, 3 * i + 2 - tap + 1)
                dve.tensor_tensor(conv_c[:, :], conv_u[:, :], conv_b[:, :], ALU.mult).then_inc(conv_step, 1)
                dve.wait_ge(nk_hi_done, i + 1)
                sub_lo(nk_lo[:, i, :], Z[1][:, :], cols1[:, ds(C_NK + i, 1)], nk_hi[:, i, :], z_free[1])
                dve.wait_ge(conv_hi, i + 1)
                dve.tensor_tensor(br_lo[:, PAIRS + i, :], conv_c[:, :], br_hi[:, PAIRS + i, :].bitcast(F), ALU.subtract).then_inc(conv_lo, 1)
                dve.wait_ge(o_hi_done, i + 1)
                dve.tensor_tensor(br_lo[:, i, :], O[:, :], br_hi[:, i, :].bitcast(F), ALU.subtract).then_inc(o_lo_done, 1)

            dve.wait_ge(pv_done, PAIRS + 1)
            dve.wait_ge(z_free[1], Z_CMP[1])
            for b, pe_col, pe_cols in ((0, C_PEK, cols1), (1, C_PEV, cols2)):
                for g in range(2):
                    dve.memset(cz[64 * g:64 * g + 64, b, :, N_BLK * (1 - g):N_BLK * (2 - g)], 0.0)
                    rows = slice(64 * g, 64 * g + 64)
                    dve.tensor_tensor(cz[rows, b, :, N_BLK * g:N_BLK * g + N_BLK],
                                      nk_hi[rows, b, :].bitcast(F).rearrange("p (c r) -> p r c", r=CMP_STRIDE),
                                      nk_lo[rows, b, :].bitcast(F).rearrange("p (c r) -> p r c", r=CMP_STRIDE), ALU.add) \
                        .then_inc(cz_ready, 1)
                dve.tensor_copy(cz[:, b, :, 2 * N_BLK:CZ_W],
                                pe_cols[:, pe_col:pe_col + CMP_LEN].rearrange("p (h r) -> p r h", h=2)).then_inc(cz_ready, 1)
            for h in range(2):
                dve.tensor_scalar(sel[:, h, :], ident[0:CZ_W, h:h + 2 * N_BLK], ident[0:CZ_W, 2 * N_BLK + h:2 * N_BLK + h + 1],
                                  None, ALU.add).then_inc(sel_ready, 1)
            for b in range(2):
                dve.wait_ge(hid_done, b + 1)
                dve.tensor_copy(hid_f[:, b, :, :], S[b][0:CZ_W, 0:P128].rearrange("p (h m) -> p h m", h=2)).then_inc(hid_ready, 1)
            dve.wait_ge(cmp_hi, 1)
            dve.tensor_tensor(kc_lo[:, :], S[4][:, 0:2 * N_BLK], kc_hi[:, :].bitcast(F), ALU.subtract).then_inc(cmp_lo, 1)
            dve.wait_ge(cmp_hi, 2)
            dve.tensor_tensor(vc_lo[:, :], O[0:64, 0:P128], vc_hi[:, :].bitcast(F), ALU.subtract).then_inc(cmp_lo, 1)
            dve.wait_ge(alibi_ready, 3)
            for a in range(2):
                dve.tensor_scalar(alibi[:, a, :], alibi[:, a, :], 0.5 ** (1 + 4 * a) / SCALE, None, ALU.mult).then_inc(alibi_scaled, 1)
            dve.wait_ge(alibi_scaled, 2)

            with dve.Fori(0, PAIRS) as i:
                T = T_NSA + 10 * i
                z0, z1 = Z_NSA[0] + 5 * i, Z_NSA[1] + 5 * i

                def softmax_scores(pair):
                    for a, t in score_at:
                        wait_scores(pair, a, t)
                        op = mask_tile(a, t, 0, P_LEN[t], alibi[:, a, SEQ - P_LEN[t]:SEQ], mx[:, a, t:t + 1])
                    op.then_inc(masked, 1)
                    dve.wait_ge(masked, pair + 1 + 1)
                    dve.tensor_scalar(neg_mx[:, :, :], mx[:, :, :], -1.0, None, ALU.mult).then_inc(neg_ready, 1)

                def gate_inv(pair, br):
                    invert(pair)
                    dve.wait_ge(inv_ready, pair + (pair - PAIRS) + 1)
                    g = gates[:, br, :, :].rearrange("p (a h) t -> p a h t", a=2)[:, :, ds(i, 1), :] \
                        .rearrange("p a h t -> p a (h t)")
                    dve.tensor_tensor(p_inv[:, :, :], p_inv[:, :, :], g, ALU.mult).then_inc(inv_ready, 1)
                    dve.wait_ge(inv_ready, pair + (pair - PAIRS) + 2)

                dve.wait_ge(q_hi_done, PAIRS + i + 1)
                sub_lo(q_lo[:, :], Z[0][:, :], cols1[:, ds(C_NQ + i, 1)], q_hi[:, :], z_free[0])
                softmax_scores(PAIRS + 2 * i)
                flat = "p t a c -> p (t a) c"
                cp = c_p[:, :, :, :].rearrange(flat)
                dve.wait_ge(c_t, i + 1)
                dve.wait_ge(c_scored, i + 1)
                dve.scalar_tensor_tensor(c_p[:, :, :, :].rearrange("p t a c -> p (t a c)"), O[:, 0:256], SCALE,
                                         c_bias[:, :, :, :].rearrange("p t a c -> p (t a c)"), ALU.mult, ALU.add).then_inc(c_step, 1)
                dve.wait_ge(c_step, 5 * i + 1)
                dve.tensor_reduce(c_mx[:, :, :].rearrange("p t a -> p (t a)"), cp, AX.X, ALU.max).then_inc(c_step, 1)
                dve.wait_ge(c_step, 5 * i + 2)
                dve.tensor_tensor(cp, cp, c_mx[:, :, :].rearrange("p t (a o) -> p (t a) o", o=1).to_broadcast([P128, 2 * QT, CMP_LEN]),
                                  ALU.subtract).then_inc(c_step, 1)
                gate_inv(PAIRS + 2 * i, 1)
                normalise(PAIRS + 2 * i)
                dve.wait_ge(c_exp, i + 1)
                dve.tensor_reduce(c_sum[:, :, :].rearrange("p t a -> p (t a)"), cp, AX.X, ALU.add).then_inc(c_red, 1)
                dve.wait_ge(c_red, 4 * i + 1)
                dve.reciprocal(c_sum[:, :, :], c_sum[:, :, :]).then_inc(c_red, 1)
                dve.wait_ge(c_red, 4 * i + 2)
                dve.tensor_tensor(c_sum[:, :, :], c_sum[:, :, :],
                                  gates[:, 0, :, :].rearrange("p (a h) t -> p h t a", a=2)[:, ds(i, 1), :, :]
                                  .rearrange("p h t a -> p (h t) a"), ALU.mult).then_inc(c_red, 1)
                dve.tensor_tensor(cp, cp, c_mask[:, :, :, :].rearrange(flat), ALU.mult).then_inc(c_red, 1)
                dve.wait_ge(c_red, 4 * i + 4)
                dve.tensor_tensor(cp, cp, c_sum[:, :, :].rearrange("p t (a o) -> p (t a) o", o=1).to_broadcast([P128, 2 * QT, CMP_LEN]),
                                  ALU.mult).then_inc(c_ready, 1)

                def gated(m, t, z_a, z_b):
                    dve.wait_ge(z_free[1], z_a)
                    dve.wait_ge(tile_done, t + 1)
                    dve.scalar_tensor_tensor(mix[:, m, :], g_a[:, :], 1.0, Z[1][:, :], ALU.add, ALU.mult).then_inc(z_free[1], 1)
                    dve.wait_ge(z_free[0], z_b)
                    dve.wait_ge(tile_done, t + 2)
                    dve.scalar_tensor_tensor(g_b[:, :], g_b[:, :], 1.0, Z[0][:, :], ALU.add, ALU.mult).then_inc(z_free[0], 1)
                    dve.wait_ge(z_free[1], z_a + 1)
                    dve.wait_ge(z_free[0], z_b + 1)
                    dve.tensor_tensor(mix[:, m, :], mix[:, m, :], g_b[:, :], ALU.add).then_inc(gb_used, 1)

                gated(2 * i, T + 3, z1 + 1, z0 + 2)
                pt_low(PAIRS + 2 * i)
                dve.wait_ge(c_t_hi, i + 1)
                dve.tensor_tensor(c_pt_lo[:, :], O[0:64, :], c_pt_hi[:, :].bitcast(F), ALU.subtract).then_inc(c_t_lo, 1)
                dve.wait_ge(pv_s_done, i + 1)
                softmax_scores(PAIRS + 2 * i + 1)
                dve.wait_ge(masked, PAIRS + 2 * i + 2 + 1)
                dve.tensor_scalar(alibi[:, :, :], alibi[:, :, :], 0.5, None, ALU.mult).then_inc(c_step, 1)
                dve.tensor_scalar(c_bias[:, :, :, :], c_bias[:, :, :, :], 0.5, None, ALU.mult).then_inc(c_step, 1)
                dve.wait_ge(c_step, 5 * i + 5)
                gate_inv(PAIRS + 2 * i + 1, 2)
                normalise(PAIRS + 2 * i + 1)
                gated(2 * i + 1, T + 7, z1 + 3, z0 + 4)
                pt_low(PAIRS + 2 * i + 1)
                dve.wait_ge(o_hi_done, PAIRS + i + 1)
                dve.tensor_tensor(c_lo[:, i, :], O[:, :], c_hi[:, i, :].bitcast(F), ALU.subtract).then_inc(o_lo_done, 1)

            tau = 0
            for kind, m in MIX_ORDER:
                if kind == "gc":
                    tau += 1
                    continue
                for mt in (m, m + 1):
                    z = tau % 2
                    dve.wait_ge(z_free[z], Z_MIX[z] + tau // 2)
                    dve.wait_ge(tile_done, T_MIX + tau + 1)
                    g = g_c[:, mt, :]
                    dve.scalar_tensor_tensor(g, g, 1.0, Z[z][:, :], ALU.add, ALU.mult).then_inc(z_free[z], 1)
                    dve.wait_ge(z_free[z], Z_MIX[z] + tau // 2 + 1)
                    dve.tensor_tensor(mix[:, mt, :], mix[:, mt, :], g, ALU.add).then_inc(mix_done, 1)
                    tau += 1
                for mt in (m, m + 1):
                    dve.wait_ge(mix_hi, mt + 1)
                    dve.scalar_tensor_tensor(br_lo[:, mt, :], mix[:, mt, :], 0.5, br_hi[:, mt, :].bitcast(F),
                                             ALU.mult, ALU.subtract).then_inc(mix_lo, 1)
            for m in range(KT):
                z = m % 2
                dve.wait_ge(xr_copied, m + 1)
                dve.wait_ge(tile_done, T_WO + m + 1)
                dve.tensor_tensor(x2[:, m, :], Z[z][:, :], x2[:, m, :], ALU.add).then_inc(z_free[z], 1)
                dve.wait_ge(z_free[z], Z_WO[z] + m // 2 + 1)
                dve.wait_ge(xg_hi, m + 1)
                dve.scalar_tensor_tensor(h_lo[:, m, :], x2[:, m, :], cols1[:, C_GFFN + m:C_GFFN + m + 1], h_hi[:, m, :].bitcast(F),
                                         ALU.mult, ALU.subtract).then_inc(xg_lo, 1)
                if m:
                    dve.wait_ge(acc_done, m)
                sq = x_sq if m else x_acc
                dve.tensor_tensor(sq[:, :], x2[:, m, :], x2[:, m, :], ALU.mult).then_inc(sq_done if m else acc_done, 1)
                if m:
                    dve.wait_ge(sq_done, m)
                    dve.tensor_tensor(x_acc[:, :], x_acc[:, :], x_sq[:, :], ALU.add).then_inc(acc_done, 1)
            dve.memset(u_t[:, 0:2], 0.0).then_inc(rs_ready, 1)
            dve.wait_ge(rs_sqrt, 1)
            dve.reciprocal(rstd[:, :], rstd[:, :]).then_inc(rs_ready, 1)
            dve.wait_ge(rs_ready, 2)

            with dve.Fori(0, FT) as i:
                T = T_UP + 2 * i
                dve.wait_ge(u_step, 2 * i + 1)
                dve.wait_ge(tile_done, T + 1)
                dve.tensor_tensor(u_t[:, 2:SEQ + 2], Z[0][:, :], rstd[:, :], ALU.mult).then_inc(z_free[0], 1)
                dve.wait_ge(z_free[0], Z_UP[0] + i + 1)
                dve.memset(u_t[:, 0:2], 0.0).then_inc(u_ready, 1)
                dve.wait_ge(u_w2, i + 1)
                for tap in (1, 0):
                    dve.scalar_tensor_tensor(u_c[:, :], u_t[:, tap:SEQ + tap], cols2[:, ds(C_FFN + FT * tap + i, 1)], u_c[:, :],
                                             ALU.mult, ALU.add).then_inc(u_step, 1)
                    dve.wait_ge(u_step, 2 * i + 2 - tap + 1)
                dve.wait_ge(tile_done, T + 2)
                dve.tensor_tensor(v_t[:, :], Z[1][:, :], rstd[:, :], ALU.mult).then_inc(z_free[1], 1)
                dve.wait_ge(z_free[1], Z_UP[1] + i + 1)
                dve.wait_ge(u_silu, i + 1)
                dve.tensor_tensor(u_c[:, :], u_c[:, :], v_t[:, :], ALU.mult).then_inc(uv_done, 1)
                dve.wait_ge(act_hi_done, i + 1)
                dve.tensor_tensor(act_lo[:, i, :], u_c[:, :], act_hi[:, i, :].bitcast(F), ALU.subtract).then_inc(act_lo_done, 1)

            def add_residual(m):
                dve.wait_ge(down_done, m + 1)
                dve.tensor_tensor(x2[:, m, :], banks[m][:, :], x2[:, m, :], ALU.add).then_inc(x3_done, 1)

            def gain(n):
                dve.wait_ge(y_sqd, n + 1)
                dve.tensor_tensor(y_out[:, n, :], banks[n][:, :], g_out[:, 0:BR_W], ALU.mult).then_inc(y_gained, 1)

            def add_squares(t):
                dve.wait_ge(y_sqd, QT + t + 1)
                dve.tensor_tensor(stat[:, 2, t:t + 1], stat[:, 0, t:t + 1], stat[:, 1, t:t + 1], ALU.add).then_inc(y_ms, 1)

            for m in range(6):
                add_residual(m)
            dve.wait_ge(g_loaded, 16)
            gain(0)
            gain(1)
            for m in range(6, KT):
                add_residual(m)
            gain(2)
            gain(3)
            add_squares(0)
            add_squares(1)
            for t in range(QT):
                dve.wait_ge(y_sqrt, t + 1)
                dve.reciprocal(stat[:, 3, t:t + 1], stat[:, 2, t:t + 1]).then_inc(y_rs, 1)
                dve.wait_ge(y_rs, t + 1)
                dve.scalar_tensor_tensor(y_out[:, QT + t, :], banks[QT + t][:, :], stat[:, 3, t:t + 1], g_out[:, BR_W:D_MODEL],
                                         ALU.mult, ALU.mult).then_inc(y_high, 1)
                if t == 0:
                    add_squares(2)
                    dve.wait_ge(y_gained, 1)
                    dve.tensor_scalar(y_out[:, 0, :], y_out[:, 0, :], stat[:, 3, 0:1], None, ALU.mult).then_inc(y_low, 1)
                    add_squares(3)


_INS = ["x", "norm_mix_g", "w_in", "b_in", "cmp_pe_k", "cmp_w1_k", "cmp_w2_k", "cmp_pe_v", "cmp_w1_v",
        "cmp_w2_v", "sc_conv_w", "w_br_a", "w_br_b", "w_br_c", "w_o", "norm_ffn_g", "w_up", "ffn_conv_w",
        "w_down", "norm_final_g"]


def kernel(**inputs):
    import numpy as np
    import concourse.bacc as bacc
    from concourse import mybir
    from concourse.bass_utils import run_bass_kernel_spmd

    nc = bacc.Bacc("TRN2", target_bir_lowering=False, num_devices=1, dynamic_dma_scratch_size=1024)
    arrays, args = {}, []
    for name in _INS:
        a = np.ascontiguousarray(inputs[name])
        arrays[f"in_{name}"] = a
        args.append(nc.dram_tensor(f"in_{name}", a.shape, mybir.dt.from_np(a.dtype), kind="ExternalInput").ap())
    out = nc.dram_tensor("out_0", (1, SEQ, D_MODEL), mybir.dt.float32, kind="ExternalOutput").ap()
    hybrid_block(nc, *args, out)
    r = run_bass_kernel_spmd(nc, [arrays], core_ids=[0])
    return r.results[0]["out_0"]
```
